# Optimizing a Trainium2 kernel written in Bass

```python
import jax, jax.numpy as jnp
from jax import lax
import numpy as np

D_MODEL = 1024
BATCH = 1
SEQ = 1024
DEPTH = 1
DEC_BATCH = 8
DEC_SEQ = 4
PAST_LEN = 256
PAGE_SIZE = 128

A_HEADS = 4
A_DK = 128
A_DV = 128
A_WIDTH_K = A_HEADS * A_DK
A_WIDTH_V = A_HEADS * A_DV
HGRN_CHUNK = 64
SB_HEADS = 8
SB_HEAD_DIM = 64
SB_WIDTH = SB_HEADS * SB_HEAD_DIM
SB_BLOCK = 128
SB_BIAS_HI = -2.0
SB_BIAS_LO = -8.0
C_CH = 512
CONV_W = 31
D_FF = 4 * D_MODEL
N_BRANCH = 3
EPS = 1e-6
IN_SIZES = (A_WIDTH_K, A_WIDTH_K, A_WIDTH_V, A_WIDTH_V, SB_WIDTH, SB_WIDTH, SB_WIDTH, 2 * C_CH, N_BRANCH * D_MODEL)
IN_WIDTH = sum(IN_SIZES)

kernel_name = 'hgrn2_stickbreak_conformer_gated_hybrid_step'

def _split_points():
    return [int(s) for s in np.cumsum(IN_SIZES)[:-1]]

def _rmsnorm(x, g):
    xf = x.astype(jnp.float32)
    y = xf * lax.rsqrt(jnp.mean(xf * xf, axis=-1, keepdims=True) + EPS) * g.astype(jnp.float32)
    return y.astype(x.dtype)

def _layernorm(x, g, b):
    xf = x.astype(jnp.float32)
    mu = jnp.mean(xf, axis=-1, keepdims=True)
    var = jnp.mean(jnp.square(xf - mu), axis=-1, keepdims=True)
    y = (xf - mu) * lax.rsqrt(var + EPS) * g.astype(jnp.float32) + b.astype(jnp.float32)
    return y.astype(x.dtype)

def _hgrn2_chunked(q, k, v, log_f, s0):
    Bn, T, H, DK = q.shape
    C = min(HGRN_CHUNK, T)
    n = -(-T // C)
    pad = n * C - T
    q, k, v, log_f = (a.astype(jnp.float32) for a in (q, k, v, log_f))
    if pad:
        pw = ((0, 0), (0, pad), (0, 0), (0, 0))
        q, k, v, log_f = (jnp.pad(a, pw) for a in (q, k, v, log_f))
    def chunks(a):
        return a.reshape(Bn, n, C, H, a.shape[-1]).transpose(1, 0, 3, 2, 4)
    tri = jnp.tril(jnp.ones((C, C), dtype=bool))

    def step(S, inp):
        qc, kc, vc, gc = inp
        b = jnp.cumsum(gc, axis=2)
        diff = b[:, :, :, None, :] - b[:, :, None, :, :]
        decay = jnp.exp(jnp.where(tri[:, :, None], diff, -jnp.inf))
        att = jnp.einsum('bhtd,bhsd,bhtsd->bhts', qc, kc, decay)
        o = jnp.einsum('bhts,bhsv->bhtv', att, vc) + jnp.einsum('bhtd,bhdv->bhtv', qc * jnp.exp(b), S)
        b_last = b[:, :, -1:, :]
        S_new = jnp.exp(b_last[:, :, 0, :])[..., None] * S + jnp.einsum('bhsd,bhsv->bhdv', kc * jnp.exp(b_last - b), vc)
        return S_new, o

    S, o = lax.scan(step, s0.astype(jnp.float32), (chunks(q), chunks(k), chunks(v), chunks(log_f)))
    o = o.transpose(1, 0, 3, 2, 4).reshape(Bn, n * C, H, v.shape[-1])[:, :T]
    return o, S

def _sb_block(q, k, v, bias, q_pos, k_pos):
    z = jnp.einsum('bhqd,bhkd->bhqk', q, k) * (SB_HEAD_DIM ** -0.5) + bias[None, :, None, None]
    mask = k_pos[None, :] < q_pos[:, None]
    log_beta = jax.nn.log_sigmoid(z)
    log_rest = jnp.where(mask, jax.nn.log_sigmoid(-z), 0.0)
    tail = lax.cumsum(log_rest, axis=3, reverse=True) - log_rest
    A = jnp.where(mask, jnp.exp(log_beta + tail), 0.0)
    return jnp.einsum('bhqk,bhkd->bhqd', A, v)

def _sb_attention(q, k, v, bias, q_pos, k_pos):
    Bn, Tq, H, d = q.shape
    qh = q.astype(jnp.float32).transpose(0, 2, 1, 3)
    kh = k.astype(jnp.float32).transpose(0, 2, 1, 3)
    vh = v.astype(jnp.float32).transpose(0, 2, 1, 3)
    bf = bias.astype(jnp.float32)
    blk = SB_BLOCK if Tq % SB_BLOCK == 0 else Tq
    nb = Tq // blk
    qblk = qh.reshape(Bn, H, nb, blk, d).transpose(2, 0, 1, 3, 4)
    pblk = q_pos.reshape(nb, blk)
    out = lax.map(lambda a: _sb_block(a[0], kh, vh, bf, a[1], k_pos), (qblk, pblk))
    return out.transpose(1, 0, 3, 2, 4).reshape(Bn, Tq, H, d).astype(q.dtype)

def _causal_dwconv(u_full, w, b):
    y = lax.conv_general_dilated(u_full, w[:, None, :].astype(u_full.dtype), window_strides=(1,), padding='VALID',
                                 dimension_numbers=('NWC', 'WIO', 'NWC'), feature_group_count=u_full.shape[-1])
    return y + b.astype(u_full.dtype)

def _mixer(h, l, W, lb, past):
    Bn, T, _ = h.shape
    dt = h.dtype
    proj = h @ W['w_in'][l]
    qa, fa, ia, ga, qb, kb, vb, uc, gl = jnp.split(proj, _split_points(), axis=-1)

    qa = jax.nn.silu(qa).reshape(Bn, T, A_HEADS, A_DK)
    ff = fa.astype(jnp.float32)
    if l == 0:
        log_f = jax.nn.log_sigmoid(ff)
    else:
        log_f = jnp.log(lb[l] + (1.0 - lb[l]) * jax.nn.sigmoid(ff))
    ka = -jnp.expm1(log_f)
    s0 = jnp.zeros((Bn, A_HEADS, A_DK, A_DV), jnp.float32) if past is None else past['s']
    oa, s_new = _hgrn2_chunked(qa, ka.reshape(Bn, T, A_HEADS, A_DK), ia.reshape(Bn, T, A_HEADS, A_DV),
                               log_f.reshape(Bn, T, A_HEADS, A_DK), s0)
    oa = _rmsnorm(oa.astype(dt), W['a_norm'][l]) * jax.nn.silu(ga.reshape(Bn, T, A_HEADS, A_DV))
    ya = oa.reshape(Bn, T, A_WIDTH_V) @ W['w_pa'][l]

    qb = qb.reshape(Bn, T, SB_HEADS, SB_HEAD_DIM)
    kb = kb.reshape(Bn, T, SB_HEADS, SB_HEAD_DIM)
    vb = vb.reshape(Bn, T, SB_HEADS, SB_HEAD_DIM)
    if past is None:
        k_all, v_all, offset = kb, vb, 0
    else:
        k_all = jnp.concatenate([past['k'].astype(dt), kb], axis=1)
        v_all = jnp.concatenate([past['v'].astype(dt), vb], axis=1)
        offset = past['k'].shape[1]
    q_pos = offset + jnp.arange(T, dtype=jnp.int32)
    k_pos = jnp.arange(k_all.shape[1], dtype=jnp.int32)
    ob = _sb_attention(qb, k_all, v_all, W['sb_bias'][l], q_pos, k_pos)
    yb = ob.reshape(Bn, T, SB_WIDTH) @ W['w_pb'][l]

    ua, ug = jnp.split(uc, 2, axis=-1)
    u = ua * jax.nn.sigmoid(ug)
    prev = jnp.zeros((Bn, CONV_W - 1, C_CH), dt) if past is None else past['conv'].astype(dt)
    u_full = jnp.concatenate([prev, u], axis=1)
    c = _causal_dwconv(u_full, W['conv_w'][l], W['conv_b'][l])
    c = jax.nn.silu(_layernorm(c, W['ln_g'][l], W['ln_b'][l]))
    yc = c @ W['w_pc'][l]
    conv_new = u_full[:, -(CONV_W - 1):]

    gates = jax.nn.sigmoid(gl.reshape(Bn, T, N_BRANCH, D_MODEL))
    m = gates[:, :, 0] * ya + gates[:, :, 1] * yb + gates[:, :, 2] * yc
    out = m @ W['w_o'][l]
    return out, (kb, vb, s_new.astype(dt), conv_new)

def _trunk(x, W, lb, cache):
    ks, vs, ss, cs = [], [], [], []
    for l in range(DEPTH):
        past = None
        if cache is not None:
            cache_k, cache_v, page_table, state_hgrn, state_conv = cache
            n_seq, n_pages = page_table.shape
            past_len = n_pages * cache_k.shape[2]
            past = dict(k=cache_k[l][page_table].reshape(n_seq, past_len, SB_HEADS, SB_HEAD_DIM),
                        v=cache_v[l][page_table].reshape(n_seq, past_len, SB_HEADS, SB_HEAD_DIM),
                        s=state_hgrn[l], conv=state_conv[l])
        h = _rmsnorm(x, W['g_pre_mix'][l])
        mix, (k_new, v_new, s_new, c_new) = _mixer(h, l, W, lb, past)
        x = x + _rmsnorm(mix, W['g_post_mix'][l])
        h = _rmsnorm(x, W['g_pre_ffn'][l])
        ff = jnp.square(jax.nn.relu(h @ W['w_ff1'][l])) @ W['w_ff2'][l]
        x = x + _rmsnorm(ff, W['g_post_ffn'][l])
        ks.append(k_new); vs.append(v_new); ss.append(s_new); cs.append(c_new)
    return x, jnp.stack(ks), jnp.stack(vs), jnp.stack(ss), jnp.stack(cs)

def setup_inputs(seed: int = 0) -> dict:
    key = jax.random.key(seed)
    ks = jax.random.split(key, 32)
    f32 = jnp.float32
    n_pages = PAST_LEN // PAGE_SIZE
    n_used = DEC_BATCH * n_pages
    n_phys = (5 * n_used + 3) // 4
    nrm = lambda k, shape, s: (jax.random.normal(k, shape, f32) * s)
    gain = lambda k, shape: 1.0 + 0.05 * jax.random.normal(k, shape, f32)
    perm = jax.random.permutation(ks[5], n_phys)[:n_used]
    sb_bias = jnp.linspace(SB_BIAS_HI, SB_BIAS_LO, SB_HEADS, dtype=f32)[None, :] + nrm(ks[24], (DEPTH, SB_HEADS), 0.1)
    return {
        'x_prompt': nrm(ks[0], (BATCH, SEQ, D_MODEL), 1.0),
        'x_sample': nrm(ks[1], (DEC_BATCH, DEC_SEQ, D_MODEL), 1.0),
        'cache_k': nrm(ks[2], (DEPTH, n_phys, PAGE_SIZE, SB_HEADS, SB_HEAD_DIM), 1.0),
        'cache_v': nrm(ks[3], (DEPTH, n_phys, PAGE_SIZE, SB_HEADS, SB_HEAD_DIM), 1.0),
        'page_table': perm.reshape(DEC_BATCH, n_pages).astype(jnp.int32),
        'state_hgrn': nrm(ks[4], (DEPTH, DEC_BATCH, A_HEADS, A_DK, A_DV), 0.5),
        'state_conv': nrm(ks[6], (DEPTH, DEC_BATCH, CONV_W - 1, C_CH), 0.5),
        'g_pre_mix': gain(ks[7], (DEPTH, D_MODEL)),
        'g_post_mix': gain(ks[8], (DEPTH, D_MODEL)),
        'g_pre_ffn': gain(ks[9], (DEPTH, D_MODEL)),
        'g_post_ffn': gain(ks[10], (DEPTH, D_MODEL)),
        'w_in': nrm(ks[11], (DEPTH, D_MODEL, IN_WIDTH), D_MODEL ** -0.5),
        'hgrn_lb': nrm(ks[12], (DEPTH, A_WIDTH_K), 1.0),
        'a_norm': gain(ks[13], (DEPTH, A_DV)),
        'w_pa': nrm(ks[14], (DEPTH, A_WIDTH_V, D_MODEL), A_WIDTH_V ** -0.5),
        'w_pb': nrm(ks[15], (DEPTH, SB_WIDTH, D_MODEL), SB_WIDTH ** -0.5),
        'sb_bias': sb_bias,
        'conv_w': nrm(ks[16], (DEPTH, CONV_W, C_CH), CONV_W ** -0.5),
        'conv_b': nrm(ks[17], (DEPTH, C_CH), 0.02),
        'ln_g': gain(ks[18], (DEPTH, C_CH)),
        'ln_b': nrm(ks[19], (DEPTH, C_CH), 0.02),
        'w_pc': nrm(ks[20], (DEPTH, C_CH, D_MODEL), C_CH ** -0.5),
        'w_o': nrm(ks[21], (DEPTH, D_MODEL, D_MODEL), D_MODEL ** -0.5),
        'w_ff1': nrm(ks[22], (DEPTH, D_MODEL, D_FF), D_MODEL ** -0.5),
        'w_ff2': nrm(ks[23], (DEPTH, D_FF, D_MODEL), D_FF ** -0.5),
    }

def reference(x_prompt, x_sample, cache_k, cache_v, page_table, state_hgrn, state_conv,
              g_pre_mix, g_post_mix, g_pre_ffn, g_post_ffn, w_in, hgrn_lb, a_norm, w_pa, w_pb, sb_bias,
              conv_w, conv_b, ln_g, ln_b, w_pc, w_o, w_ff1, w_ff2):
    W = dict(g_pre_mix=g_pre_mix, g_post_mix=g_post_mix, g_pre_ffn=g_pre_ffn, g_post_ffn=g_post_ffn,
             w_in=w_in, a_norm=a_norm, w_pa=w_pa, w_pb=w_pb, sb_bias=sb_bias, conv_w=conv_w, conv_b=conv_b,
             ln_g=ln_g, ln_b=ln_b, w_pc=w_pc, w_o=w_o, w_ff1=w_ff1, w_ff2=w_ff2)
    lb = jnp.cumsum(jax.nn.softmax(hgrn_lb.astype(jnp.float32), axis=0), axis=0)
    lb = lb - lb[0:1]
    y_prompt, k_p, v_p, s_p, c_p = _trunk(x_prompt, W, lb, None)
    y_sample, k_s, v_s, s_s, c_s = _trunk(x_sample, W, lb, (cache_k, cache_v, page_table, state_hgrn, state_conv))
    return (y_prompt, y_sample, k_p, v_p, s_p, c_p, k_s, v_s, s_s, c_s)


_drawn_inputs = setup_inputs


def setup_inputs(seed=0):
    import zlib

    import numpy as np

    out = dict(_drawn_inputs(seed))
    spreads = {}
    factors = {'conv_b': 2.833, 'ln_b': 5.557}
    for name, (base, spread) in spreads.items():
        noise = np.random.default_rng([zlib.crc32(name.encode()), seed]).standard_normal(out[name].shape)
        drawn = base * np.exp(spread * noise) if base else spread * noise
        out[name] = __import__('jax').numpy.asarray(drawn.astype(out[name].dtype))
    for name, factor in factors.items():
        out[name] = (out[name] * factor).astype(out[name].dtype)
    return out
```

```python
from contextlib import ExitStack

import concourse.bass as bass
from concourse import mybir

F32 = mybir.dt.float32
F32R = mybir.dt.float32r
U8 = mybir.dt.uint8
I32 = mybir.dt.int32
ALU = mybir.AluOpType
ACT = mybir.ActivationFunctionType

P = 128
D = 1024
KD = D // P
TP, NSEQ, TS = 1024, 8, 4
T = TP + NSEQ * TS
G = 3
GW = T // G
NH = 4
DH = 64
PAST = 256
NPG = 2
CH = TP // P
SM = NSEQ * TS
CW = 31
PAD = CW - 1
FF = 4096
FCH = 8
EPS = 1e-6
SBK = PAST + SM
NEG_BIG = -1e30
ZMAX = 40.0

C_QA, C_FA, C_IA, C_GA, C_QB, C_KB, C_VB, C_UA, C_UG, C_GL = (
    0, 512, 1024, 1536, 2048, 2560, 3072, 3584, 4096, 4608)
PRE = 5
PER = 9
U2 = PRE + PER * (NH - 1) + 4
LEVELS = (128, 64, 32, 16, 8, 4, 2)
NL = len(LEVELS)

PK = {}
_at = 0
for _n, _w in (("g_pre_mix", 8), ("g_post_mix", 8), ("g_pre_ffn", 8), ("g_post_ffn", 8), ("a_norm", 1),
               ("conv_w", NH * CW), ("conv_b", NH), ("ln_g", NH), ("ln_b", NH), ("sb_bias", 2 * NH),
               ("sample_bias", NH), ("ident", P), ("neg", P), ("neg_new", SM), ("own_seq", NSEQ)):
    PK[_n] = (_at, _at + _w)
    _at += _w
NPK = _at

A_Z, A_L, A_AT = (0, 1024, 2048), (3072, 4096), 5120
A_KS, A_VS, A_QPAD, A_QFULL, A_VT, A_ZS, A_LS, A_ATS = 6144, 8192, 10240, 10816, 10880, 12032, 12320, 12608
A_OB, A_U, A_US, A_ACC = 12832, 13888, 14944, 15216
B_T1, B_B, B_D, B_W, B_KK, B_ATT, B_QB, B_KD = 0, 1056, 2112, (3168, 4224), 5280, 6336, 7392, 8448
B_VA, B_KDT, B_S0, B_O, B_OSQ, B_RS = 9504, 10656, 11808, 12832, 13888, 14944
ARENA = A_ACC + T


class Signal:

    def __init__(self, sem, per, before=0):
        self.sem, self.per, self.before = sem, per, before

    def wait(self, eng, p, k):
        eng.wait_ge(*self.at(p, k))

    def at(self, p, k):
        return self.sem, p * self.per + (self.before + k)


class Chain:

    def __init__(self, eng, sem, start=0):
        self.eng, self.sem, self.n, self.start = eng, sem, 0, start

    def mark(self, ins):
        ins.then_inc(self.sem, 1)
        self.n += 1

    def wait(self):
        self.eng.wait_ge(self.sem, self.start + self.n)

    def link(self, ins):
        self.mark(ins)
        self.wait()


def build(nc, dr):
    ctx = ExitStack()
    with ctx:
        def sem(name):
            return ctx.enter_context(nc.semaphore(name))

        def sb(name, shape, dt, stack=ctx):
            return stack.enter_context(nc.sbuf_tensor(name, shape, dt))

        hh = sb("h_hi", [P, KD, T], F32R)
        hl = sb("h_lo", [P, KD, T], F32R)
        raw = sb("w_raw", [P, 3, KD, P], F32)
        wh = sb("w_hi", [P, 3, KD, P], F32R)
        wl = sb("w_lo", [P, 3, KD, P], F32R)
        ones = sb("ones", [P, P], F32)
        pk = sb("params", [P, NPK], F32)
        eps = sb("eps", [P, 1], F32)
        levm = sb("level_masks", [P, NL, P], U8)
        keep = sb("scan_keep", [P, T], U8)
        cwp = sb("conv_w_now", [P, CW + 1], F32)
        sbp = sb("bias_now", [P, 3], F32)
        ebl = sb("chunk_decay", [P, CH + NSEQ], F32)
        pages = sb("pages", [1, NSEQ * NPG], I32)

        s2 = ExitStack()
        kT = sb("kT", [P, T], F32, s2)
        qT = sb("qT", [P, T], F32, s2)
        vT = sb("vT", [P, T], F32, s2)
        fT = sb("fT", [P, T], F32, s2)
        qA = sb("qA", [P, T], F32, s2)
        gA = sb("gA", [P, T], F32, s2)
        iT = sb("iT", [P, T], F32, s2)
        ua = sb("ua", [P, T], F32, s2)
        ug = sb("ug", [P, T], F32, s2)
        ar = sb("arena", [P, ARENA], F32, s2)
        s2.close()

        s3 = ExitStack()
        of = sb("o_full", [P, NH, T], F32, s3)
        oh = sb("o_hi", [P, NH, T], F32R, s3)
        ol = sb("o_lo", [P, NH, T], F32R, s3)
        mm_ = sb("mixed", [P, KD, T], F32, s3)
        gs = sb("gate", [P, T], F32, s3)
        tm = sb("gated", [P, T], F32, s3)
        s3.close()

        s4 = ExitStack()
        x4 = sb("x_again", [P, KD, T], F32, s4)
        acc4_gap = sb("gap4", [P, NH, T], F32, s4)
        mix = sb("mix", [P, KD, T], F32, s4)
        sq4 = sb("sq4", [P, T], F32, s4)
        ss4 = sb("ss4", [P, T], F32, s4)
        s4.close()

        s5 = ExitStack()
        fh = sb("hid_hi", [P, NH, T], F32R, s5)
        fl = sb("hid_lo", [P, NH, T], F32R, s5)
        hid = sb("hid", [P, 2, T], F32, s5)
        gap5 = sb("gap5", [P, 2, T], F32, s5)
        acc = sb("ff_sum", [P, KD, T], F32, s5)
        sq5 = sb("sq5", [P, T], F32, s5)
        ss5 = sb("ss5", [P, T], F32, s5)
        s5.close()

        ps = ctx.enter_context(nc.psum_tensor("psum", [P, 8, 512], F32))
        flat = ps[:, :, :].rearrange("p b n -> p (b n)")

        def bank(b, n=512, rows=slice(0, P)):
            return ps[rows, b, 0:n]

        def banks(b, n):
            return flat[:, 512 * b:512 * b + n]

        def A(off, n, rows=slice(0, P)):
            return ar[rows, off:off + n]

        def par(name, j=0, n=1):
            a = PK[name][0] + j
            return pk[:, a:a + n]

        ident = par("ident", 0, P)
        neg = par("neg", 0, P)
        xT = A(0, KD * T).rearrange("p (k t) -> p k t", k=KD)
        sq1 = A(KD * T, 2 * T).rearrange("p (k t) -> p k t", k=2)
        ss1 = A((KD + 2) * T, T)
        rs1 = A((KD + 3) * T, T)
        mask_f = A((KD + 4) * T, NL * P + T)

        S = lambda name, per=0, before=0: Signal(sem(name), per, before)
        const_in = sem("const_in")
        pages_in = sem("pages_in")
        x_in = [sem(f"x_in{f}") for f in range(KD)]
        ones_set = sem("ones_set")
        x_squared = sem("x_squared")
        x_summed = sem("x_summed")
        ss_bcast = sem("ss_bcast")
        h_rstd = sem("h_rstd")
        h_full = sem("h_full")
        h_hi_set = sem("h_hi_set")
        h_ready = sem("h_ready")

        w_landed = [sem(f"w_landed{s}") for s in range(3)]
        w_hi_set = sem("w_hi_set")
        w_split = sem("w_split")
        unit_done = sem("unit_done")
        staged = S("unit_staged", PER, PRE)

        v_turned, v_staged = S("v_turned", 1), S("v_staged", 1)
        now_set = S("params_now", 2)
        q_pad = S("q_pad", 1)
        ug_sig = S("ug_sig", 1)
        u_ready = S("u_ready", 1)
        conv_done = S("conv_done", 1)
        prev_in = S("conv_prev_in", 16)
        ks_in = S("cache_in", 32 * NSEQ * NPG)
        z_ready, z_read = S("z_ready", 16), S("z_read", 16)
        e_ready = S("z_clipped", 16)
        exp1 = S("exp_done", 16)
        ln_ready = S("softplus_log", 16)
        arg_ready = S("arg_ready", 16)
        a_ready = S("a_ready", 16)
        t_done, at_ready = S("a_turned", 16), S("at_staged", 16)
        av_done = S("av_done", 16)
        o_read = S("ob_read", 8)
        zs_ready, zs_read = S("zs_ready", 1), S("zs_read", 1)
        es_ready, lns_ready = S("zs_clipped", 1), S("s_softplus", 1)
        args_ready, as_ready = S("args_ready", 1), S("as_ready", 1)
        ts_done, ats_ready = S("as_turned", 1), S("ats_staged", 1)
        os_done, os_read = S("os_done", 1), S("os_read", 1)
        kv_stored = S("kv_stored", 32)
        conv_stored = S("conv_stored", 48)
        ob_stored = S("ob_stored", 16)

        t1_ready = S("f_log", 1)
        sig_ready = S("sigmoids", 1)
        ia_turned, va_staged = S("ia_turned", 1), S("va_staged", 1)
        b_ready, eb_ready, qb_ready = S("decay_sum", 1), S("decay_exp", 1), S("q_decayed", 1)
        qk_ready = S("q_gated", 1)
        vm_ready = S("v_masked", 1)
        dsub, wexp, w_ready = S("level_diff", NL), S("level_exp", NL), S("level_qk", NL)
        lev_done, att_read = S("level_product", NL + 1), S("level_merged", NL + 1)
        dk_ready, dk_exp, kd_ready = S("k_diff", 1), S("k_exp", 1), S("k_decayed", 1)
        kd_turned, kdt_staged = S("kd_turned", 1), S("kdt_staged", 1)
        s0_in = S("state_in", 16)
        u_done, s_ready = S("chunk_update", 1), S("states_ready", 1)
        um_done, s0_new = S("sample_update", 1), S("sample_state", 1)
        o_done, osq_ready = S("oa_product", 1), S("oa_squared", 1)
        n_done, n_read, rs_ready = S("oa_norm_sum", 1), S("oa_norm_read", 1), S("oa_rstd", 1)
        oa_ready = S("oa_ready", 1)
        h_stored = S("hgrn_stored", 48)

        v_seq, a_seq = sem("vector_chain"), sem("scalar_chain")

        of_in = sem("o_in")
        ln_seq_v, ln_seq_a, ln_pe = sem("ln_vector"), sem("ln_scalar"), sem("ln_sums")
        o_hi_set, o_ready = sem("o_hi_set"), sem("o_split")
        gate_free, y_free = sem("gate_read"), sem("y_read")
        gate_ready, m_seq = sem("gate_ready"), sem("mixed_chain")
        m_hi_set, m_ready = sem("m_hi_set"), sem("m_split")
        x4_in = sem("x_again_in")
        mix_read, mix_sq, sq_used = sem("mix_read"), sem("mix_squared"), sem("square_added")
        n4_sum, n4_rs = sem("norm_sum"), sem("norm_rstd")
        x1_seq = sem("x1_chain")
        x1_stored = sem("x1_stored")
        x1_ready = sem("x1_ready")
        h2_full, h2_hi = sem("h2_full"), sem("h2_hi")
        h2_ready = sem("h2_split")
        hid_relu, hid_sq, hid_hi, hid_ready = sem("hid_relu"), sem("hid_squared"), sem("hid_hi_set"), sem("hid_split")
        acc_added = sem("ff_added")
        y_seq, y_ready, y_stored = sem("y_chain"), sem("y_ready"), sem("y_stored")
        x5_in = sem("x1_in")
        fin_sq, fin_ss = sem("ff_squared"), sem("ff_square_added")

        block = ctx.enter_context(nc.Block())


        def wait_apart(eng, *waits):
            waits = [(s, v if isinstance(v, int) else nc.snap(v)) for s, v in waits]
            eng.wait_ge(ones_set, 1)
            for s, v in waits:
                eng.wait_ge(s, v)

        w_in = dr["w_in"].rearrange("(k p) n -> p k n", p=P)
        w_p = [dr[n].rearrange("(k p) n -> p k n", p=P) for n in ("w_pa", "w_pb", "w_pc")]
        w_o = dr["w_o"].rearrange("(k p) n -> p k n", p=P)
        w_f1 = dr["w_ff1"].rearrange("(k p) n -> p k n", p=P)
        w_f2 = dr["w_ff2"].rearrange("(c k p) n -> c p k n", k=NH, p=P)
        A_COLS = (C_FA, C_QA, C_IA, C_GA)
        B_COLS = (C_KB, C_VB, C_QB, C_UA, C_UG)

        def slot2(u):
            return u % 3, u // 3

        def load_unit2(sp, u, p, cols):
            s, n = slot2(u)
            if u >= 3:
                wait_apart(sp, (w_split, p * PER + (u - 2)))
            sp.dma_start(raw[:, s, :, :], w_in[:, :, bass.ds(cols, P)]).then_inc(w_landed[s], 16)

        def split_unit2(pool, u, p):
            s, n = slot2(u)
            over = [(unit_done, p * PER + (u - 2))] if u >= 3 else []
            wait_apart(pool, (w_landed[s], p * 48 + 16 * (n + 1)), *over)
            pool.tensor_copy(wh[:, s, :, :], raw[:, s, :, :]).then_inc(w_hi_set, 1)
            pool.wait_ge(w_hi_set, p * PER + (u + 1))
            pool.tensor_tensor(wl[:, s, :, :], raw[:, s, :, :], wh[:, s, :, :].bitcast(F32),
                               ALU.subtract).then_inc(w_split, 1)

        def load_unit3(sp, v, slot, use, src, kt):
            wait_apart(sp, (w_split, v + (U2 - 1)))
            sp.dma_start(raw[:, slot, 0:kt, :], src).then_inc(w_landed[slot], 16)

        def split_unit3(pool, v, slot, use, kt):
            wait_apart(pool, (w_landed[slot], (use + (U2 // 3 + 1)) * 16), (unit_done, v + (U2 - 1)))
            pool.tensor_copy(wh[:, slot, 0:kt, :], raw[:, slot, 0:kt, :]).then_inc(w_hi_set, 1)
            pool.wait_ge(w_hi_set, v + (U2 + 1))
            pool.tensor_tensor(wl[:, slot, 0:kt, :], raw[:, slot, 0:kt, :], wh[:, slot, 0:kt, :].bitcast(F32),
                               ALU.subtract).then_inc(w_split, 1)

        def product(pe, slot, ks, kt, xh, xl, b0):
            for k in ks:
                for w, x in ((wh, xh), (wh, xl), (wl, xh)):
                    for g in range(G):
                        mm = pe.matmul(ps[:, b0 + g, 0:GW], w[:, slot, k, :], x[:, k, g * GW:(g + 1) * GW],
                                       start=(k == 0 and w is wh and x is xh), stop=(k == kt - 1 and w is wl))
            return mm

        @block.sync
        def _(sp):
            sp.dma_start(pk[:, :], dr["params"]).then_inc(const_in, 16)
            sp.dma_start(mask_f, dr["masks"]).then_inc(const_in, 16)
            sp.dma_start(pages[:, :], dr["pages"]).then_inc(pages_in, 16)
            for f in range(KD):
                sp.dma_start(xT[:, f, :], dr["xT"][f * P:(f + 1) * P, :]).then_inc(x_in[f], 16)
            for u in range(PRE):
                load_unit2(sp, u, 0, B_COLS[u])
            for j in range(4):
                load_unit2(sp, PRE + j, 0, A_COLS[j])
            sp.wait_ge(pages_in, 16)
            page = [sp.value_load(pages[0:1, i:i + 1], min_val=0, max_val=dr["kcT"].shape[0] - 1)
                    for i in range(NSEQ * NPG)]
            staged_now = staged
            sp.wait_ge(h_ready, KD)
            ksv = A(A_KS, 2048).rearrange("p (b g n) -> p b g n", b=NSEQ, g=NPG)
            vsv = A(A_VS, 2048).rearrange("p (b g n) -> p b g n", b=NSEQ, g=NPG)

            def group(p, more):
                for i in range(NSEQ * NPG):
                    b, g = divmod(i, NPG)
                    sp.dma_start(ksv[:, b, g, :], dr["kcT"][bass.ds(page[i], 1), bass.ds(p * P, P), :]
                                 .rearrange("a d t -> (a d) t")).then_inc(ks_in.sem, 16)
                    sp.dma_start(vsv[:, b, g, :], dr["vc"][bass.ds(page[i], 1), :, bass.ds(p * P, P)]
                                 .rearrange("a t d -> (a t) d")).then_inc(ks_in.sem, 16)
                sp.dma_start(A(A_US, NSEQ * (PAD + TS)).rearrange("p (b t) -> p b t", b=NSEQ)[:, :, 0:PAD],
                             dr["conv_prev"][bass.ds(p * P, P), :, :]).then_inc(prev_in.sem, 16)
                wait_apart(sp, staged_now.at(p, -3))
                sp.dma_start(dr["k_out"][bass.ds(p * P, P), :], kT[:, :]).then_inc(kv_stored.sem, 16)
                sp.dma_start(dr["v_out"][bass.ds(p * P, P), :], vT[:, :]).then_inc(kv_stored.sem, 16)
                if more:
                    for j in range(3):
                        load_unit2(sp, PRE + 4 + j, p, (p + 1) * P + B_COLS[j])
                wait_apart(sp, conv_done.at(p, 1))
                sp.dma_start(dr["c_d"][bass.ds(p * P, P), :], A(A_ACC, T)).then_inc(conv_stored.sem, 16)
                sp.dma_start(dr["conv_p"][bass.ds(p * P, P), :],
                             A(A_U + TP, PAD)).then_inc(conv_stored.sem, 16)
                sp.dma_start(dr["conv_s"][bass.ds(p * P, P), :, :],
                             A(A_US, NSEQ * (PAD + TS)).rearrange("p (b t) -> p b t", b=NSEQ)[:, :, TS:])\
                    .then_inc(conv_stored.sem, 16)
                if more:
                    for j in range(3, 5):
                        load_unit2(sp, PRE + 4 + j, p, (p + 1) * P + B_COLS[j])
                wait_apart(sp, av_done.at(p, 16))
                wait_apart(sp, os_done.at(p, 1))
                sp.dma_start(A(B_S0, NSEQ * P).rearrange("p (b v) -> p b v", b=NSEQ),
                             dr["s_in"][:, bass.ds(p, 1), :, :].rearrange("b a d v -> d (b a) v"))\
                    .then_inc(s0_in.sem, 16)
                wait_apart(sp, o_read.at(p, 8))
                wait_apart(sp, os_read.at(p, 1))
                sp.dma_start(dr["ob_d"][bass.ds(p * P, P), :], A(A_OB, T)).then_inc(ob_stored.sem, 16)
                if more:
                    for j in range(4):
                        load_unit2(sp, PRE + PER + j, p, (p + 1) * P + A_COLS[j])
                wait_apart(sp, s_ready.at(p, 1))
                sp.dma_start(dr["hgrn_p"][bass.ds(p, 1), :, :].rearrange("a d v -> (a d) v"),
                             A(B_D + 7 * P, P)).then_inc(h_stored.sem, 16)
                wait_apart(sp, s0_new.at(p, 1))
                sp.dma_start(dr["hgrn_s"][:, bass.ds(p, 1), :, :].rearrange("b a d v -> d (b a) v"),
                             A(B_W[0], NSEQ * P).rearrange("p (b v) -> p b v", b=NSEQ)).then_inc(h_stored.sem, 16)
                wait_apart(sp, oa_ready.at(p, 1))
                sp.dma_start(dr["oa_d"][bass.ds(p * P, P), :], A(B_O, T)).then_inc(h_stored.sem, 16)

            with sp.Fori(0, NH - 1) as p:
                group(p, True)
            group(NH - 1, False)

            h_stored.wait(sp, NH - 1, 48)
            conv_stored.wait(sp, NH - 1, 48)
            ob_stored.wait(sp, NH - 1, 16)
            kv_stored.wait(sp, NH - 1, 32)
            for x, src in enumerate(("c_d", "oa_d", "ob_d")):
                if x:
                    sp.wait_ge(o_ready, 4 * x)
                sp.dma_start(of[:, :, :], dr[src].rearrange("(k p) t -> p k t", p=P)).then_inc(of_in, 16)
                xx = (2, 0, 1)[x]
                with sp.Fori(0, 8) as cb:
                    load_unit3(sp, cb * 2 + 16 * x, 0, 0, w_in[:, :, bass.ds(cb * P + (C_GL + xx * D), P)], KD)
                    load_unit3(sp, cb * 2 + (16 * x + 1), 1, 0, w_p[xx][:, :, bass.ds(cb * P, P)], NH)
            with sp.Fori(0, 4) as i:
                for j in range(2):
                    load_unit3(sp, i * 2 + (48 + j), j, 0, w_o[:, :, bass.ds(i * 2 * P + j * P, P)], KD)
            sp.wait_ge(o_ready, 12)
            sp.wait_ge(unit_done, U2 + 48)
            sp.dma_start(x4[:, :, :], dr["xT"].rearrange("(k p) t -> p k t", p=P)).then_inc(x4_in, 16)
            with sp.Fori(0, FCH) as c:
                for j in range(4):
                    load_unit3(sp, c * 12 + (56 + j), j % 2, 0, w_f1[:, :, bass.ds(c * 4 * P + j * P, P)], KD)
                for j in range(8):
                    load_unit3(sp, c * 12 + (60 + j), j % 2, 0,
                               w_f2[bass.ds(c, 1), :, :, j * P:(j + 1) * P].rearrange("c p k n -> (c p) k n"), NH)
            for f in range(KD):
                sp.wait_ge(y_ready, f + 1)
                sp.dma_start(dr["yT"][f * P:(f + 1) * P, :], acc[:, f, :]).then_inc(y_stored, 16)
            sp.wait_ge(y_stored, 16 * KD)

        @block.gpsimd
        def _(pool):
            for u in range(PRE):
                split_unit2(pool, u, 0)
            with pool.Fori(0, NH - 1) as p:
                for j in range(PER):
                    split_unit2(pool, PRE + j, p)
            for j in range(4):
                split_unit2(pool, PRE + j, NH - 1)
            with pool.Fori(0, 24) as n:
                split_unit3(pool, n * 2, 0, n, KD)
                split_unit3(pool, n * 2 + 1, 1, n, NH)
            with pool.Fori(24, 28) as n:
                split_unit3(pool, n * 2, 0, n, KD)
                split_unit3(pool, n * 2 + 1, 1, n, KD)
            with pool.Fori(0, FCH) as c:
                for j in range(12):
                    split_unit3(pool, c * 12 + (56 + j), j % 2, c * 6 + (28 + j // 2), KD if j < 4 else NH)

        @block.tensor
        def _(pe):
            def unit_part(u, p, ks):
                if 0 in ks:
                    pe.wait_ge(w_split, p * PER + (u + 1))
                    if u:
                        pe.wait_ge(staged.sem, p * PER + u)
                mm = product(pe, u % 3, ks, KD, hh, hl, 0)
                if KD - 1 in ks:
                    mm.then_inc(unit_done, 1)

            pe.wait_ge(ones_set, 2)
            pe.wait_ge(x_summed, KD)
            for g in range(G):
                mm = pe.matmul(ps[:, g + 3, 0:GW], ones[:, :], ss1[:, g * GW:(g + 1) * GW], start=True, stop=True)
            mm.then_inc(ss_bcast, 1)
            for k in range(KD):
                pe.wait_ge(h_ready, k + 1)
                unit_part(0, 0, (k,))
            for u in range(1, PRE):
                unit_part(u, 0, range(KD))

            zb = [A(o, 1024) for o in A_Z]
            atv = A(A_AT, 1024)
            vtok = A(A_VT, 9 * P).rearrange("p (n d) -> p n d", n=9)
            ksv = A(A_KS, 2048).rearrange("p (b n) -> p b n", b=NSEQ)
            vsv = A(A_VS, 2048).rearrange("p (b g n) -> p b g n", b=NSEQ, g=NPG)
            ats = A(A_ATS, 192).rearrange("p (g n) -> p g n", g=3)

            def scores(p, i):
                qb, e = divmod(i, 2)
                rows = slice(DH * e, DH * e + DH)
                if i:
                    z_read.wait(pe, p, i)
                if i == 8:
                    zs_read.wait(pe, p, 1)
                nk = P * (qb + 1)
                for a in range(0, nk, 512):
                    n = min(512, nk - a)
                    mm = pe.matmul(ps[:, 3 + a // 512, 0:n], qT[rows, qb * P:(qb + 1) * P], kT[rows, a:a + n],
                                   start=True, stop=True)
                mm.then_inc(z_ready.sem, 1)

            def turn_a(p, i):
                a_ready.wait(pe, p, i + 1)
                if i:
                    at_ready.wait(pe, p, i)
                if i == 8:
                    os_read.wait(pe, p, 1)
                for kb in range(i // 2 + 1):
                    mm = pe.transpose(banks(5, 1024)[:, kb * P:(kb + 1) * P], zb[i % 3][:, kb * P:(kb + 1) * P], ident)
                mm.then_inc(t_done.sem, 1)

            def values(p, i):
                qb, e = divmod(i, 2)
                at_ready.wait(pe, p, i + 1)
                if e == 0 and qb:
                    o_read.wait(pe, p, qb)
                for kb in range(qb + 1):
                    mm = pe.matmul(ps[DH * e:DH * e + DH, 7, (qb % 4) * P:(qb % 4 + 1) * P],
                                   vtok[:, kb, DH * e:DH * e + DH], atv[:, kb * P:(kb + 1) * P],
                                   start=(kb == 0), stop=(kb == qb))
                mm.then_inc(av_done.sem, 1)

            def sample_scores(p):
                ks_in.wait(pe, p, 32 * NSEQ * NPG)
                q_pad.wait(pe, p, 1)
                for b in range(NSEQ):
                    pe.matmul(ps[0:64, 4, 0:PAST], A(A_QPAD + 64 * b, 64), ksv[:, b, :],
                              start=(b == 0), stop=(b == NSEQ - 1))
                pe.matmul(ps[0:64, 4, PAST:SBK], A(A_QFULL, 64), kT[:, TP:T], start=True, stop=True)\
                    .then_inc(zs_ready.sem, 1)

            def sample_turn(p):
                wait_apart(pe, as_ready.at(p, 1))
                for j in range(2):
                    pe.transpose(ps[:, 6, 64 * j:64 * j + 64], A(A_ZS + P * j, P, slice(0, 64)), ident[0:64, 0:64])
                pe.transpose(ps[0:SM, 6, 128:192], A(A_ZS + PAST, SM, slice(0, 64)), ident[0:64, 0:64])\
                    .then_inc(ts_done.sem, 1)

            def sample_values(p):
                ats_ready.wait(pe, p, 1)
                pe.matmul(ps[:, 6, 256:320], vtok[0:SM, 8, :], ats[0:SM, 2, :], start=True, stop=False,
                          skip_group_check=True)
                for b in range(NSEQ):
                    for g in range(NPG):
                        mm = pe.matmul(ps[:, 6, 256 + 8 * b:264 + 8 * b], vsv[:, b, g, :], ats[:, g, 8 * b:8 * b + 8],
                                       start=False, stop=(b == NSEQ - 1 and g == NPG - 1), skip_group_check=True)
                mm.then_inc(os_done.sem, 1)

            wb = [A(o, T) for o in B_W]
            kk, att, qbt, kd = A(B_KK, T), A(B_ATT, T), A(B_QB, T), A(B_KD, T)
            va = A(B_VA, 9 * P).rearrange("p (n d) -> p n d", n=9)
            kdt = A(B_KDT, 9 * P).rearrange("p (n d) -> p n d", n=9)
            s0 = A(B_S0, NSEQ * P).rearrange("p (b v) -> p b v", b=NSEQ)

            def turn9(src, b0):
                for c in range(CH):
                    pe.transpose(banks(b0, 1024)[:, c * P:(c + 1) * P], src[:, c * P:(c + 1) * P], ident)
                return pe.transpose(ps[0:SM, 7, 0:P], src[:, TP:T], ident)

            def level_product(p, idx, left, right, b0, sample):
                for c in range(CH):
                    mm = pe.matmul(banks(b0, 1024)[:, c * P:(c + 1) * P], left[:, c * P:(c + 1) * P],
                                   right[:, c * P:(c + 1) * P], start=True, stop=True)
                if sample:
                    mm = pe.matmul(ps[0:SM, 7, 0:SM], left[:, TP:T], right[:, TP:T], start=True, stop=True)
                mm.then_inc(lev_done.sem, 1)

            def group(p, more):
                def quarter(s):
                    unit_part(PRE + s // 4, p, range(2 * (s % 4), 2 * (s % 4) + 2))

                def half(s):
                    if more:
                        unit_part(PRE + 4 + s // 2, p, range(4 * (s % 2), 4 * (s % 2) + 4))

                staged.wait(pe, p, -2)
                turn9(vT, 5).then_inc(v_turned.sem, 1)
                for s in range(19):
                    if s < 16:
                        scores(p, s)
                        quarter(s)
                    if s == 3:
                        v_staged.wait(pe, p, 1)
                    if s >= 3:
                        values(p, s - 3)
                    if s == 2:
                        v_staged.wait(pe, p, 1)
                    if 2 <= s < 18:
                        turn_a(p, s - 2)
                    if s == 3:
                        sample_scores(p)
                    if s == 7:
                        sample_turn(p)
                    if s == 9:
                        sample_values(p)
                staged.wait(pe, p, 3)
                at_ready.wait(pe, p, 16)
                o_read.wait(pe, p, 8)
                turn9(iT, 5).then_inc(ia_turned.sem, 1)
                half(0)
                qk_ready.wait(pe, p, 1)
                va_staged.wait(pe, p, 1)
                level_product(p, 0, kk, qA, 3, True)
                half(1)
                for j in range(NL):
                    w_ready.wait(pe, p, j + 1)
                    sample = LEVELS[j] <= TS
                    att_read.wait(pe, p, j + (1 if sample else 0) if j else 1)
                    level_product(p, j + 1, wb[j % 2], wb[j % 2], 5 if j % 2 == 0 else 3, sample)
                    if j < 5:
                        half(2 + j)
                half(7)
                kd_ready.wait(pe, p, 1)
                att_read.wait(pe, p, NL + 1)
                turn9(kd, 3).then_inc(kd_turned.sem, 1)
                half(8)
                kdt_staged.wait(pe, p, 1)
                for c in range(CH):
                    mm = pe.matmul(banks(5, 1024)[:, c * P:(c + 1) * P], kdt[:, c, :], va[:, c, :],
                                   start=True, stop=True)
                mm.then_inc(u_done.sem, 1)
                vm_ready.wait(pe, p, 1)
                for j in range(2):
                    mm = pe.matmul(ps[:, 3 + j, :], kdt[0:SM, 8, :], A(B_T1 + 512 * j, 512, slice(0, SM)),
                                   start=True, stop=True)
                mm.then_inc(um_done.sem, 1)
                half(9)
                s_ready.wait(pe, p, 1)
                qb_ready.wait(pe, p, 1)
                s0_in.wait(pe, p, 16)
                for c in range(CH):
                    o = banks(5, 1024)[:, c * P:(c + 1) * P]
                    pe.matmul(o, va[:, c, :], att[:, c * P:(c + 1) * P], start=True, stop=(c == 0))
                    if c:
                        pe.matmul(o, A(B_D + (c - 1) * P, P), qbt[:, c * P:(c + 1) * P], start=False, stop=True)
                pe.matmul(ps[:, 7, 0:SM], va[0:SM, 8, :], att[0:SM, TP:T], start=True, stop=False,
                          skip_group_check=True)
                for b in range(NSEQ):
                    mm = pe.matmul(ps[:, 7, TS * b:TS * b + TS], s0[:, b, :], qbt[:, TP + TS * b:TP + TS * b + TS],
                                   start=False, stop=(b == NSEQ - 1), skip_group_check=True)
                mm.then_inc(o_done.sem, 1)
                osq_ready.wait(pe, p, 1)
                s0_new.wait(pe, p, 1)
                for a, n in ((0, 512), (512, 512), (1024, 32)):
                    mm = pe.matmul(banks(3, T)[:, a:a + n], ones[:, :], A(B_OSQ + a, n), start=True, stop=True)
                mm.then_inc(n_done.sem, 1)
                n_read.wait(pe, p, 1)

            with pe.Fori(0, NH - 1) as p:
                group(p, True)
            group(NH - 1, False)

            for r in range(2):
                for g in range(G):
                    pe.wait_ge(ln_seq_v, LN_V[r])
                    if LN_A[r * G + g]:
                        pe.wait_ge(ln_seq_a, LN_A[r * G + g])
                    pe.matmul(ps[:, 6 + (r * G + g) % 2, 0:GW], ones[:, :], tm[:, g * GW:(g + 1) * GW],
                              start=True, stop=True).then_inc(ln_pe, 1)
            for x in range(3):
                with pe.Fori(0, 8) as cb:
                    pe.wait_ge(w_split, cb * 2 + (U2 + 16 * x + 1))
                    pe.wait_ge(gate_free, cb + (8 * x + 1))
                    product(pe, 0, range(KD), KD, hh, hl, 0).then_inc(unit_done, 1)
                    pe.wait_ge(w_split, cb * 2 + (U2 + 16 * x + 2))
                    pe.wait_ge(y_free, cb + (8 * x + 1))
                    pe.wait_ge(o_ready, 4 * (x + 1))
                    product(pe, 1, range(NH), NH, oh, ol, 3).then_inc(unit_done, 1)

            def wo_unit(i, j, first):
                pe.wait_ge(w_split, i * 2 + (U2 + 48 + j + 1))
                if not first:
                    pe.wait_ge(mix_read, i * 2 + (j - 1))
                if first and j == 0:
                    pe.wait_ge(gate_free, 25)
                    for k in range(KD):
                        pe.wait_ge(m_ready, k + 1)
                        mm = product(pe, j, (k,), KD, hh, hl, 0)
                else:
                    if first:
                        pe.wait_ge(y_free, 25)
                    mm = product(pe, j, range(KD), KD, hh, hl, 3 * j)
                mm.then_inc(unit_done, 1)

            wo_unit(0, 0, True)
            wo_unit(0, 1, True)
            with pe.Fori(1, 4) as i:
                wo_unit(i, 0, False)
                wo_unit(i, 1, False)

            def norm_sum(src, value, sem_in, sem_out):
                pe.wait_ge(sem_in, value)
                for g in range(G):
                    mm = pe.matmul(ps[:, g, 0:GW], ones[:, :], src[:, g * GW:(g + 1) * GW], start=True, stop=True)
                mm.then_inc(sem_out, 1)

            pe.wait_ge(mix_read, 8)
            norm_sum(ss4, KD, sq_used, n4_sum)
            norm_sum(ss4, 2 * KD, sq_used, n4_sum)
            pe.wait_ge(n4_rs, 2)
            pe.wait_ge(h2_ready, KD)
            with pe.Fori(0, FCH) as c:
                for j in range(4):
                    pe.wait_ge(w_split, c * 12 + (U2 + 56 + j + 1))
                    if j < 2:
                        pe.wait_ge(acc_added, c * 8 + (j + 1))
                    else:
                        pe.wait_ge(hid_relu, c * 4 + (j - 1))
                    product(pe, j % 2, range(KD), KD, hh, hl, 3 * (j % 2)).then_inc(unit_done, 1)
                for j in range(8):
                    pe.wait_ge(w_split, c * 12 + (U2 + 60 + j + 1))
                    if j < 2:
                        pe.wait_ge(hid_relu, c * 4 + (j + 3))
                    else:
                        pe.wait_ge(acc_added, c * 8 + (j + 1))
                    for k in range(NH):
                        if j == 0:
                            pe.wait_ge(hid_ready, c * 4 + (k + 1))
                        mm = product(pe, j % 2, (k,), NH, fh, fl, 3 * (j % 2))
                    mm.then_inc(unit_done, 1)
            pe.wait_ge(acc_added, 8 * FCH + 2)
            norm_sum(ss5, KD, fin_ss, n4_sum)

        @block.scalar
        def _(act):
            IDN = ACT.Identity

            for f in range(KD):
                act.wait_ge(x_in[f], 16)
                if f >= 2:
                    act.wait_ge(x_summed, f - 1)
                act.activation(sq1[:, f % 2, :], xT[:, f, :], ACT.Square).then_inc(x_squared, 1)
            act.wait_ge(ss_bcast, 1)
            act.wait_ge(ones_set, 2)
            psg = lambda b0: ps[:, b0:b0 + G, 0:GW]
            v3 = lambda ap: ap.rearrange("p (g t) -> p g t", g=G)
            act.activation(v3(rs1), psg(3), ACT.Ln, bias=eps[:, 0:1], scale=1.0 / D).then_inc(a_seq, 1)
            act.wait_ge(a_seq, 1)
            act.activation(rs1, rs1, ACT.Exp, scale=-0.5).then_inc(h_rstd, 1)
            for f in range(KD):
                act.wait_ge(h_full, f + 1)
                act.activation(hh[:, f, :], xT[:, f, :], ACT.Copy).then_inc(h_hi_set, 1)

            def stage(u, p, dst, scale=None):
                act.wait_ge(unit_done, p * PER + (u + 1))
                ins = (act.activation(v3(dst[:, :]), psg(0), ACT.Copy) if scale is None else
                       act.activation(v3(dst[:, :]), psg(0), ACT.Copy, scale=scale))
                ins.then_inc(staged.sem, 1)

            B_DST = ((kT, None), (vT, None), (qT, DH ** -0.5), (ua, None), (ug, None))
            A_DST = (fT, qA, iT, gA)
            for u in range(PRE):
                stage(u, 0, *B_DST[u])

            zb = [A(o, 1024) for o in A_Z]
            lb = [A(o, 1024) for o in A_L]
            vtok = A(A_VT, 9 * P)
            ob = A(A_OB, T)
            CHAIN_A = 3

            def group(p, more):
                ch = Chain(act, a_seq, p * CHAIN_A + 1)
                staged.wait(act, p, 0)
                act.activation(ug[:, :], ug[:, :], ACT.Sigmoid).then_inc(ug_sig.sem, 1)
                v_turned.wait(act, p, 1)
                act.activation(vtok[:, 0:1024], banks(5, 1024), ACT.Copy)
                act.activation(vtok[0:SM, 1024:1152], ps[0:SM, 7, 0:P], ACT.Copy).then_inc(v_staged.sem, 1)
                now_set.wait(act, p, 2)
                for s in range(20):
                    i = s - 3
                    if 4 <= s <= 16 and s % 4 == 0:
                        stage(PRE + s // 4 - 1, p, A_DST[s // 4 - 1])
                    if 0 <= i < 16:
                        t_done.wait(act, p, i + 1)
                        if i:
                            av_done.wait(act, p, i)
                        n = P * (i // 2 + 1)
                        act.activation(A(A_AT, n), banks(5, n), ACT.Copy).then_inc(at_ready.sem, 1)
                    if s >= 5 and s % 2 == 1:
                        qb = (s - 5) // 2
                        av_done.wait(act, p, 2 * qb + 2)
                        act.activation(ob[:, qb * P:(qb + 1) * P], ps[:, 7, (qb % 4) * P:(qb % 4 + 1) * P],
                                       ACT.Copy).then_inc(o_read.sem, 1)
                    if s < 16:
                        z_ready.wait(act, p, s + 1)
                        if s >= 3:
                            t_done.wait(act, p, s - 2)
                        n = P * (s // 2 + 1)
                        act.activation(zb[s % 3][:, 0:n], banks(3, n), IDN, bias=sbp[:, s % 2:s % 2 + 1])\
                            .then_inc(z_read.sem, 1)
                    if 0 <= s - 1 < 16:
                        n = P * ((s - 1) // 2 + 1)
                        l = lb[(s - 1) % 2][:, 0:n]
                        e_ready.wait(act, p, s)
                        act.activation(l, l, ACT.Exp).then_inc(exp1.sem, 1)
                        exp1.wait(act, p, s)
                        act.activation(l, l, ACT.Ln, bias=1.0).then_inc(ln_ready.sem, 1)
                    if 0 <= s - 2 < 16:
                        n = P * ((s - 2) // 2 + 1)
                        z = zb[(s - 2) % 3][:, 0:n]
                        arg_ready.wait(act, p, s - 1)
                        act.activation(z, z, ACT.Exp).then_inc(a_ready.sem, 1)
                    if s == 4:
                        zs_ready.wait(act, p, 1)
                        act.activation(A(A_ZS, SBK, slice(0, 64)), ps[0:64, 4, 0:SBK], IDN, bias=sbp[0:64, 2:3])\
                            .then_inc(zs_read.sem, 1)
                    if s == 5:
                        l = A(A_LS, SBK, slice(0, 64))
                        es_ready.wait(act, p, 1)
                        ch.link(act.activation(l, l, ACT.Exp))
                        act.activation(l, l, ACT.Ln, bias=1.0).then_inc(lns_ready.sem, 1)
                    if s == 6:
                        args_ready.wait(act, p, 1)
                        z = A(A_ZS, SBK, slice(0, 64))
                        act.activation(z, z, ACT.Exp).then_inc(as_ready.sem, 1)
                    if s == 8:
                        ts_done.wait(act, p, 1)
                        act.activation(A(A_ATS, 128), ps[:, 6, 0:128], ACT.Copy)
                        act.activation(A(A_ATS + 128, 64, slice(0, SM)), ps[0:SM, 6, 128:192], ACT.Copy)\
                            .then_inc(ats_ready.sem, 1)
                    if s == 10:
                        os_done.wait(act, p, 1)
                        for e in range(2):
                            r = slice(DH * e, DH * e + DH)
                            ins = act.activation(ar[r, A_OB + TP:A_OB + T].rearrange("p (b q) -> p b q", b=NSEQ),
                                                 ps[r, 6, 256:320].rearrange("p (b e q) -> p b e q", b=NSEQ, e=2)
                                                 [:, :, e, :], ACT.Copy)
                        ins.then_inc(os_read.sem, 1)

                av_done.wait(act, p, 16)
                t_done.wait(act, p, 16)
                staged.wait(act, p, 4)
                t1 = A(B_T1, T)
                ch.link(act.activation(t1, fT[:, :], ACT.Abs))
                ch.link(act.activation(t1, t1, ACT.Exp, scale=-1.0))
                act.activation(t1, t1, ACT.Ln, bias=1.0).then_inc(t1_ready.sem, 1)
                arg_ready.wait(act, p, 16)
                act.activation(A(B_W[0], T), qA[:, :], ACT.Sigmoid)
                act.activation(A(B_W[1], T), gA[:, :], ACT.Sigmoid)
                act.activation(A(B_KK, T), fT[:, :], ACT.Sigmoid, scale=-1.0).then_inc(sig_ready.sem, 1)
                ia_turned.wait(act, p, 1)
                os_read.wait(act, p, 1)
                act.activation(A(B_VA, 1024), banks(5, 1024), ACT.Copy)
                act.activation(A(B_VA + 1024, P, slice(0, SM)), ps[0:SM, 7, 0:P], ACT.Copy).then_inc(va_staged.sem, 1)
                b_ready.wait(act, p, 1)
                act.activation(A(B_QB, T), A(B_B, T), ACT.Exp).then_inc(eb_ready.sem, 1)
                qk_ready.wait(act, p, 1)
                if more:
                    kv_stored.wait(act, p, 32)
                    u_ready.wait(act, p, 1)
                for j in range(NL):
                    dsub.wait(act, p, j + 1)
                    if j >= 2:
                        lev_done.wait(act, p, j)
                    n = T if LEVELS[j] <= TS else TP
                    act.activation(A(B_W[j % 2], n), A(B_D, n), ACT.Exp).then_inc(wexp.sem, 1)
                    if more and j in (0, 2, 4):
                        stage(PRE + 4 + j // 2, p, *B_DST[j // 2])
                dk_ready.wait(act, p, 1)
                act.activation(A(B_KD, T), A(B_D, T), ACT.Exp).then_inc(dk_exp.sem, 1)
                if more:
                    stage(PRE + 7, p, *B_DST[3])
                kd_turned.wait(act, p, 1)
                act.activation(A(B_KDT, 1024), banks(3, 1024), ACT.Copy)
                act.activation(A(B_KDT + 1024, P, slice(0, SM)), ps[0:SM, 7, 0:P], ACT.Copy)\
                    .then_inc(kdt_staged.sem, 1)
                if more:
                    stage(PRE + 8, p, *B_DST[4])
                o_done.wait(act, p, 1)
                ob_stored.wait(act, p, 16)
                conv_stored.wait(act, p, 48)
                act.activation(A(B_O, T), banks(5, T), ACT.Copy)
                act.activation(A(B_OSQ, T), banks(5, T), ACT.Square).then_inc(osq_ready.sem, 1)
                n_done.wait(act, p, 1)
                ins = act.activation(A(B_RS, T), banks(3, T), ACT.Ln, bias=eps[:, 0:1], scale=1.0 / P)
                ins.then_inc(n_read.sem, 1)
                n_read.wait(act, p, 1)
                act.activation(A(B_RS, T), A(B_RS, T), ACT.Exp, scale=-0.5).then_inc(rs_ready.sem, 1)
                oa_ready.wait(act, p, 1)
                h_stored.wait(act, p, 48)
                assert ch.n == CHAIN_A, ch.n

            with act.Fori(0, NH - 1) as p:
                group(p, True)
            group(NH - 1, False)

            kv_stored.wait(act, NH - 1, 32)
            n = 0

            def lnk(ins):
                nonlocal n
                n += 1
                ins.then_inc(ln_seq_a, 1)

            for g in range(G):
                act.wait_ge(ln_pe, g + 1)
                lnk(act.activation(gs[:, g * GW:(g + 1) * GW], ps[:, 6 + g % 2, 0:GW], ACT.Copy, scale=1.0 / 512))
            act.wait_ge(ln_seq_v, LN_CENTER)
            for k in range(NH):
                lnk(act.activation(mm_[:, k, :], of[:, k, :], ACT.Square))
            for g in range(G):
                act.wait_ge(ln_pe, G + g + 1)
                lnk(act.activation(gs[:, g * GW:(g + 1) * GW], ps[:, 6 + (G + g) % 2, 0:GW], ACT.Ln,
                                   bias=eps[:, 0:1], scale=1.0 / 512))
            act.wait_ge(ln_seq_a, n)
            lnk(act.activation(gs[:, :], gs[:, :], ACT.Exp, scale=-0.5))
            assert n == 11
            act.wait_ge(ln_seq_v, LN_SCALED)
            for k in range(NH):
                lnk(act.activation(of[:, k, :], of[:, k, :], IDN, bias=par("ln_b", k), scale=par("ln_g", k)))
            act.wait_ge(ln_seq_a, n)
            for k in range(NH):
                lnk(act.activation(mm_[:, k, :], of[:, k, :], ACT.Sigmoid))
            act.wait_ge(ln_seq_v, LN_DONE)
            for x in range(3):
                act.wait_ge(of_in, 16 * (x + 1))
                if x:
                    act.wait_ge(unit_done, U2 + 16 * x)
                for k in range(NH):
                    ins = act.activation(oh[:, k, :], of[:, k, :], ACT.Copy)
                    ins.then_inc(o_hi_set, 1)
                if x == 0:
                    act.activation(tm[:, 0:2], eps[:, 0:1].broadcast_to([P, 2]), ACT.Copy).then_inc(gate_free, 1)
                with act.Fori(0, 8) as cb:
                    act.wait_ge(unit_done, cb * 2 + (U2 + 16 * x + 1))
                    act.wait_ge(y_free, cb + (8 * x + 1))
                    act.activation(v3(gs[:, :]), psg(0), ACT.Sigmoid).then_inc(gate_free, 1)
            act.wait_ge(unit_done, U2 + 47)
            for k in range(KD):
                act.wait_ge(m_seq, 8 + k + 1)
                act.activation(hh[:, k, :], mm_[:, k, :], ACT.Copy).then_inc(m_hi_set, 1)
            act.wait_ge(m_ready, KD)
            for cb in range(KD):
                act.wait_ge(unit_done, U2 + 48 + cb + 1)
                act.activation(v3(mix[:, cb, :]), psg(3 * (cb % 2)), ACT.Copy)
                if cb:
                    act.wait_ge(sq_used, cb)
                act.activation(v3(sq4[:, :]), psg(3 * (cb % 2)), ACT.Square).then_inc(mix_read, 1)

            def rstd(dst, k):
                act.wait_ge(n4_sum, k)
                ins = act.activation(v3(dst), psg(0), ACT.Ln, bias=eps[:, 0:1], scale=1.0 / D)
                ins.then_inc(mix_sq, 1)
                act.wait_ge(mix_sq, k)
                act.activation(dst, dst, ACT.Exp, scale=-0.5).then_inc(n4_rs, 1)

            rstd(sq4[:, :], 1)
            for f in range(KD):
                act.wait_ge(x1_ready, f + 1)
                act.activation(mix[:, f, :], x4[:, f, :], ACT.Square).then_inc(x_squared, 1)
                act.dma_start(dr["x1_d"][f * P:(f + 1) * P, :], x4[:, f, :]).then_inc(x1_stored, 16)
            rstd(sq4[:, :], 2)
            for f in range(KD):
                act.wait_ge(h2_full, f + 1)
                act.activation(hh[:, f, :], mix[:, f, :], ACT.Copy).then_inc(h2_hi, 1)
            act.wait_ge(h2_ready, KD)
            act.wait_ge(x1_stored, 16 * KD)
            with act.Fori(0, FCH) as c:
                for j in range(4):
                    act.wait_ge(unit_done, c * 12 + (U2 + 56 + j + 1))
                    if j >= 2:
                        act.wait_ge(hid_ready, c * 4 + (j - 1))
                    act.activation(v3(hid[:, j % 2, :]), psg(3 * (j % 2)), ACT.Relu).then_inc(hid_relu, 1)
                    act.wait_ge(hid_sq, c * 4 + (j + 1))
                    act.activation(fh[:, j, :], hid[:, j % 2, :], ACT.Copy).then_inc(hid_hi, 1)
            for f in range(KD):
                act.wait_ge(acc_added, 8 * FCH + 2)
                if f:
                    act.wait_ge(fin_ss, f)
                act.activation(sq5[:, :], acc[:, f, :], ACT.Square).then_inc(fin_sq, 1)
            act.wait_ge(fin_ss, KD)
            act.wait_ge(unit_done, U2 + 152)
            act.dma_start(hl[:, :, :].bitcast(F32), dr["x1_d"].rearrange("(k p) t -> p k t", p=P)).then_inc(x5_in, 16)
            rstd(sq5[:, :], 3)

        @block.vector
        def _(dve):
            v3 = lambda ap: ap.rearrange("p (g t) -> p g t", g=G)
            psg = lambda b0: ps[:, b0:b0 + G, 0:GW]
            dve.memset(ones[:, :], 1.0).then_inc(ones_set, 1)
            dve.memset(eps[:, :], EPS).then_inc(ones_set, 1)
            dve.wait_ge(const_in, 32)
            dve.tensor_copy(levm[:, :, :].rearrange("p l t -> p (l t)"), mask_f[:, 0:NL * P])
            dve.tensor_copy(keep[:, :], mask_f[:, NL * P:])
            for f in range(KD):
                dve.wait_ge(x_squared, f + 1)
                if f == 0:
                    dve.tensor_copy(ss1, sq1[:, 0, :]).then_inc(x_summed, 1)
                else:
                    dve.wait_ge(x_summed, f)
                    dve.tensor_tensor(ss1, ss1, sq1[:, f % 2, :], ALU.add).then_inc(x_summed, 1)
            dve.wait_ge(h_rstd, 1)
            for f in range(KD):
                dve.scalar_tensor_tensor(xT[:, f, :], xT[:, f, :], par("g_pre_mix", f), rs1, ALU.mult, ALU.mult)\
                    .then_inc(h_full, 1)
                if f:
                    dve.wait_ge(h_hi_set, f)
                    dve.tensor_tensor(hl[:, f - 1, :], xT[:, f - 1, :], hh[:, f - 1, :].bitcast(F32), ALU.subtract)\
                        .then_inc(h_ready, 1)
            dve.wait_ge(h_hi_set, KD)
            dve.tensor_tensor(hl[:, KD - 1, :], xT[:, KD - 1, :], hh[:, KD - 1, :].bitcast(F32), ALU.subtract)\
                .then_inc(h_ready, 1)

            zb = [A(o, 1024) for o in A_Z]
            lb = [A(o, 1024) for o in A_L]

            def group(p, more):
                ch = Chain(dve, v_seq, p * CHAIN_V)
                dve.tensor_copy(cwp[:, 0:CW], pk[:, bass.ds(p * CW + PK["conv_w"][0], CW)])
                dve.tensor_copy(cwp[:, CW:CW + 1], pk[:, bass.ds(p + PK["conv_b"][0], 1)]).then_inc(now_set.sem, 1)
                dve.tensor_copy(sbp[:, 0:2], pk[:, bass.ds(p * 2 + PK["sb_bias"][0], 2)])
                dve.tensor_copy(sbp[:, 2:3], pk[:, bass.ds(p + PK["sample_bias"][0], 1)]).then_inc(now_set.sem, 1)
                dve.memset(A(A_QPAD, 576), 0.0)
                ch.link(dve.memset(A(A_QFULL, 64), 0.0))
                staged.wait(dve, p, -2)
                for e in range(2):
                    r = slice(DH * e, DH * e + DH)
                    src = qT[r, TP:T].rearrange("p (b q) -> p b q", b=NSEQ)
                    dve.tensor_copy(ar[r, A_QPAD:A_QPAD + 576].rearrange("p (b c) -> p b c", c=72)
                                    [:, :, TS * e:TS * e + TS], src)
                    ins = dve.tensor_copy(ar[r, A_QFULL:A_QFULL + 64].rearrange("p (b c) -> p b c", c=8)
                                          [:, :, TS * e:TS * e + TS], src)
                ins.then_inc(q_pad.sem, 1)
                dve.memset(A(A_U, PAD), 0.0)
                ug_sig.wait(dve, p, 1)
                up, us = A(A_U, PAD + TP), A(A_US, NSEQ * (PAD + TS)).rearrange("p (b t) -> p b t", b=NSEQ)
                dve.tensor_tensor(up[:, PAD:], ua[:, 0:TP], ug[:, 0:TP], ALU.mult)
                prev_in.wait(dve, p, 16)
                dve.tensor_tensor(us[:, :, PAD:], ua[:, TP:T].rearrange("p (b t) -> p b t", b=NSEQ),
                                  ug[:, TP:T].rearrange("p (b t) -> p b t", b=NSEQ), ALU.mult).then_inc(u_ready.sem, 1)
                u_ready.wait(dve, p, 1)
                now_set.wait(dve, p, 2)
                ca = A(A_ACC, TP)
                cs = A(A_ACC + TP, SM).rearrange("p (b t) -> p b t", b=NSEQ)
                taps = [0]

                def tap(last=False):
                    w = taps[0]
                    if w >= CW:
                        return
                    taps[0] += 1
                    if w:
                        ch.wait()
                        ch.mark(dve.scalar_tensor_tensor(ca, up[:, w:w + TP], cwp[:, w:w + 1], ca, ALU.mult, ALU.add))
                        ins = dve.scalar_tensor_tensor(cs, us[:, :, w:w + TS], cwp[:, w:w + 1], cs, ALU.mult, ALU.add)
                    else:
                        ch.mark(dve.tensor_scalar(ca, up[:, 0:TP], cwp[:, 0:1], cwp[:, CW:CW + 1], ALU.mult, ALU.add))
                        ins = dve.tensor_scalar(cs, us[:, :, 0:TS], cwp[:, 0:1], cwp[:, CW:CW + 1], ALU.mult, ALU.add)
                    if w == CW - 1:
                        ins.then_inc(conv_done.sem, 1)
                    else:
                        ch.mark(ins)

                for s in range(17):
                    if s < 16:
                        qb = s // 2
                        n = P * (qb + 1)
                        z, l = zb[s % 3][:, 0:n], lb[s % 2][:, 0:n]
                        z_read.wait(dve, p, s + 1)
                        dg = z[:, qb * P:n]
                        ch.mark(dve.tensor_tensor(dg, dg, neg, ALU.add))
                        tap()
                        ch.wait()
                        dve.tensor_scalar(l, z, ZMAX, None, ALU.min).then_inc(e_ready.sem, 1)
                    if s == 4:
                        zs, ls = A(A_ZS, SBK, slice(0, 64)), A(A_LS, SBK, slice(0, 64))
                        zs_read.wait(dve, p, 1)
                        ch.link(dve.tensor_tensor(zs[:, PAST:], zs[:, PAST:], par("neg_new", 0, SM)[0:64, :], ALU.add))
                        dve.tensor_scalar(ls, zs, ZMAX, None, ALU.min).then_inc(es_ready.sem, 1)
                    tap()
                    if s:
                        n = P * ((s - 1) // 2 + 1)
                        z, l = zb[(s - 1) % 3][:, 0:n], lb[(s - 1) % 2][:, 0:n]
                        ln_ready.wait(dve, p, s)
                        ch.link(dve.tensor_tensor(l, z, l, ALU.max))
                        r = l[:, ::-1]
                        ch.link(dve.tensor_tensor_scan(r, r, r, 0.0, ALU.add, ALU.max))
                        dve.tensor_tensor(z, z, l, ALU.subtract).then_inc(arg_ready.sem, 1)
                    if s == 5:
                        lns_ready.wait(dve, p, 1)
                        ch.link(dve.tensor_tensor(ls, zs, ls, ALU.max))
                        r = ls[:, ::-1]
                        ch.link(dve.tensor_tensor_scan(r, r, r, 0.0, ALU.add, ALU.max))
                        dve.tensor_tensor(zs, zs, ls, ALU.subtract).then_inc(args_ready.sem, 1)
                while taps[0] < CW:
                    tap()

                a_ready.wait(dve, p, 16)
                t_done.wait(dve, p, 16)
                av_done.wait(dve, p, 16)
                os_done.wait(dve, p, 1)
                Bt, Dt, w0, w1 = A(B_B, T), A(B_D, T), A(B_W[0], T), A(B_W[1], T)
                kk, att, qbt = A(B_KK, T), A(B_ATT, T), A(B_QB, T)
                t1_ready.wait(dve, p, 1)
                ch.link(dve.scalar_tensor_tensor(Dt, fT[:, :], 0.0, A(B_T1, T), ALU.min, ALU.subtract))
                dve.tensor_tensor_scan(Bt, keep[:, :], Dt, 0.0, ALU.mult, ALU.add).then_inc(b_ready.sem, 1)
                sig_ready.wait(dve, p, 1)
                dve.tensor_tensor(gA[:, :], gA[:, :], w1, ALU.mult)
                dve.tensor_tensor(qA[:, :], qA[:, :], w0, ALU.mult).then_inc(qk_ready.sem, 1)
                b_ready.wait(dve, p, 1)

                def blocks(ap, size):
                    n = T if size <= TS else TP
                    return ap[:, 0:n].rearrange("p (n c) -> p n c", c=size)

                def diff(j):
                    size = LEVELS[j]
                    half = size // 2
                    bb, dd = blocks(Bt, size), blocks(Dt, size)
                    nb = bb.shape[1]
                    mid = bb[:, :, half - 1:half].broadcast_to([P, nb, half])
                    dve.tensor_tensor(dd[:, :, half:], bb[:, :, half:], mid, ALU.subtract)
                    dve.tensor_tensor(dd[:, :, 0:half], mid, bb[:, :, 0:half], ALU.subtract).then_inc(dsub.sem, 1)

                def merge(idx):
                    if idx:
                        wait_apart(dve, lev_done.at(p, idx + 1), att_read.at(p, idx))
                    else:
                        lev_done.wait(dve, p, idx + 1)
                    j = idx - 1
                    b0 = 3 if idx == 0 or j % 2 else 5
                    src = banks(b0, 1024).rearrange("p (c t) -> p c t", c=CH)
                    dst = att[:, 0:TP].rearrange("p (c t) -> p c t", c=CH)
                    if idx == 0:
                        ch.mark(dve.tensor_tensor(dst, src, ident.unsqueeze(1).broadcast_to([P, CH, P]), ALU.mult))
                        ins = dve.tensor_tensor(att[0:SM, TP:T], ps[0:SM, 7, 0:SM], ident[0:SM, 0:SM], ALU.mult)
                    else:
                        ins = dve.copy_predicated(dst, levm[:, j:j + 1, :].broadcast_to([P, CH, P]), src)
                        if LEVELS[j] <= TS:
                            ch.mark(ins)
                            ins = dve.copy_predicated(att[0:SM, TP:T], levm[0:SM, j, 0:SM], ps[0:SM, 7, 0:SM])
                    ins.then_inc(att_read.sem, 1)

                diff(0)
                va_staged.wait(dve, p, 1)
                dve.tensor_tensor(A(B_T1, NSEQ * P, slice(0, SM)).rearrange("p (b v) -> p b v", b=NSEQ),
                                  A(B_VA + 1024, P, slice(0, SM)).unsqueeze(1).broadcast_to([SM, NSEQ, P]),
                                  par("own_seq", 0, NSEQ)[0:SM, :].unsqueeze(2).broadcast_to([SM, NSEQ, P]),
                                  ALU.mult).then_inc(vm_ready.sem, 1)
                eb_ready.wait(dve, p, 1)
                dve.tensor_copy(ebl[:, 0:CH], qbt[:, 0:TP].rearrange("p (c t) -> p c t", t=P)[:, :, P - 1])
                ch.link(dve.tensor_copy(ebl[:, CH:], qbt[:, TP:T].rearrange("p (c t) -> p c t", t=TS)[:, :, TS - 1]))
                qk_ready.wait(dve, p, 1)
                dve.tensor_tensor(qbt, qbt, qA[:, :], ALU.mult).then_inc(qb_ready.sem, 1)
                merge(0)
                for j in range(NL):
                    size = LEVELS[j]
                    half = size // 2
                    wexp.wait(dve, p, j + 1)
                    if j + 1 < NL:
                        diff(j + 1)
                    else:
                        for (a, n, c) in ((0, TP, P), (TP, SM, TS)):
                            bb = Bt[:, a:a + n].rearrange("p (n c) -> p n c", c=c)
                            ins = dve.tensor_tensor(Dt[:, a:a + n].rearrange("p (n c) -> p n c", c=c),
                                                    bb[:, :, c - 1:c].broadcast_to([P, n // c, c]), bb, ALU.subtract)
                        ins.then_inc(dk_ready.sem, 1)
                    ww, qq, k_ = blocks(A(B_W[j % 2], T), size), blocks(qA, size), blocks(kk, size)
                    dve.tensor_tensor(ww[:, :, half:], ww[:, :, half:], qq[:, :, half:], ALU.mult)
                    dve.tensor_tensor(ww[:, :, 0:half], ww[:, :, 0:half], k_[:, :, 0:half], ALU.mult)\
                        .then_inc(w_ready.sem, 1)
                    if j:
                        merge(j)
                merge(NL)
                dk_exp.wait(dve, p, 1)
                dve.tensor_tensor(A(B_KD, T), A(B_KD, T), kk, ALU.mult).then_inc(kd_ready.sem, 1)
                u_done.wait(dve, p, 1)
                ch.link(dve.tensor_copy(A(B_D, P), banks(5, 1024)[:, 0:P]))
                for c in range(1, CH):
                    ins = dve.scalar_tensor_tensor(A(B_D + c * P, P), A(B_D + (c - 1) * P, P), ebl[:, c:c + 1],
                                                   banks(5, 1024)[:, c * P:(c + 1) * P], ALU.mult, ALU.add)
                    if c < CH - 1:
                        ch.link(ins)
                    else:
                        ins.then_inc(s_ready.sem, 1)
                s0_in.wait(dve, p, 16)
                sn = A(B_W[0], NSEQ * P).rearrange("p (b v) -> p b v", b=NSEQ)
                ch.link(dve.tensor_tensor(sn, A(B_S0, NSEQ * P).rearrange("p (b v) -> p b v", b=NSEQ),
                                          ebl[:, CH:].unsqueeze(2).broadcast_to([P, NSEQ, P]), ALU.mult))
                um_done.wait(dve, p, 1)
                dve.tensor_tensor(A(B_W[0], 1024), A(B_W[0], 1024), banks(3, 1024), ALU.add).then_inc(s0_new.sem, 1)
                rs_ready.wait(dve, p, 1)
                ch.link(dve.scalar_tensor_tensor(A(B_O, T), A(B_O, T), par("a_norm"), A(B_RS, T), ALU.mult, ALU.mult))
                dve.tensor_tensor(A(B_O, T), A(B_O, T), gA[:, :], ALU.mult).then_inc(oa_ready.sem, 1)
                h_stored.wait(dve, p, 48)
                assert ch.n == CHAIN_V, ch.n

            with dve.Fori(0, NH - 1) as p:
                group(p, True)
            group(NH - 1, False)

            n = 0

            def lnk(ins):
                nonlocal n
                n += 1
                ins.then_inc(ln_seq_v, 1)

            dve.wait_ge(of_in, 16)
            lnk(dve.tensor_tensor(tm[:, :], of[:, 0, :], of[:, 1, :], ALU.add))
            for k in (2, 3):
                dve.wait_ge(ln_seq_v, n)
                lnk(dve.tensor_tensor(tm[:, :], tm[:, :], of[:, k, :], ALU.add))
            assert n == LN_V[0]
            dve.wait_ge(ln_seq_a, 3)
            for k in range(NH):
                lnk(dve.tensor_tensor(of[:, k, :], of[:, k, :], gs[:, :], ALU.subtract))
            assert n == LN_CENTER
            dve.wait_ge(ln_seq_a, 7)
            lnk(dve.tensor_tensor(tm[:, :], mm_[:, 0, :], mm_[:, 1, :], ALU.add))
            for k in (2, 3):
                dve.wait_ge(ln_seq_v, n)
                lnk(dve.tensor_tensor(tm[:, :], tm[:, :], mm_[:, k, :], ALU.add))
            assert n == LN_V[1]
            dve.wait_ge(ln_seq_a, 11)
            for k in range(NH):
                lnk(dve.tensor_tensor(of[:, k, :], of[:, k, :], gs[:, :], ALU.mult))
            assert n == LN_SCALED
            dve.wait_ge(ln_seq_a, 19)
            for k in range(NH):
                lnk(dve.tensor_tensor(of[:, k, :], of[:, k, :], mm_[:, k, :], ALU.mult))
            assert n == LN_DONE
            ms = 0
            for x in range(3):
                for k in range(NH):
                    dve.wait_ge(o_hi_set, 4 * x + k + 1)
                    dve.tensor_tensor(ol[:, k, :], of[:, k, :], oh[:, k, :].bitcast(F32), ALU.subtract)\
                        .then_inc(o_ready, 1)
                if x == 0:
                    dve.wait_ge(gate_free, 1)
                    dve.memset(tm[:, 0:2], 0.0).then_inc(y_free, 1)
                with dve.Fori(0, 8) as cb:
                    dve.wait_ge(unit_done, cb * 2 + (U2 + 16 * x + 2))
                    dve.wait_ge(gate_free, cb + (8 * x + 2))
                    mt = mm_[:, bass.ds(cb, 1), :].rearrange("p a t -> p (a t)")
                    if x == 0:
                        dve.tensor_tensor(v3(mt), psg(3), v3(gs[:, :]), ALU.mult).then_inc(y_free, 1)
                    else:
                        dve.tensor_tensor(v3(tm[:, :]), psg(3), v3(gs[:, :]), ALU.mult).then_inc(y_free, 1)
                        dve.wait_ge(y_free, cb + (8 * x + 2))
                        dve.tensor_tensor(mt, mt, tm[:, :], ALU.add).then_inc(m_seq, 1)
                        dve.wait_ge(m_seq, cb + (8 * (x - 1) + 1))
            for k in range(KD):
                dve.wait_ge(m_hi_set, k + 1)
                dve.tensor_tensor(hl[:, k, :], mm_[:, k, :], hh[:, k, :].bitcast(F32), ALU.subtract).then_inc(m_ready, 1)
            for f in range(KD):
                dve.wait_ge(mix_read, f + 1)
                if f == 0:
                    dve.tensor_copy(ss4[:, :], sq4[:, :]).then_inc(sq_used, 1)
                else:
                    dve.wait_ge(sq_used, f)
                    dve.tensor_tensor(ss4[:, :], ss4[:, :], sq4[:, :], ALU.add).then_inc(sq_used, 1)
            dve.wait_ge(n4_rs, 1)
            dve.wait_ge(x4_in, 16)
            xs = 0
            for f in range(KD):
                dve.scalar_tensor_tensor(mix[:, f, :], mix[:, f, :], par("g_post_mix", f), sq4[:, :],
                                         ALU.mult, ALU.mult).then_inc(x1_seq, 1)
                dve.wait_ge(x1_seq, f + 1)
                dve.tensor_tensor(x4[:, f, :], x4[:, f, :], mix[:, f, :], ALU.add).then_inc(x1_ready, 1)
                if f:
                    dve.wait_ge(x_squared, KD + f)
                    if f == 1:
                        dve.tensor_copy(ss4[:, :], mix[:, 0, :]).then_inc(sq_used, 1)
                    else:
                        dve.wait_ge(sq_used, KD + f - 1)
                        dve.tensor_tensor(ss4[:, :], ss4[:, :], mix[:, f - 1, :], ALU.add).then_inc(sq_used, 1)
            dve.wait_ge(x_squared, 2 * KD)
            dve.wait_ge(sq_used, 2 * KD - 1)
            dve.tensor_tensor(ss4[:, :], ss4[:, :], mix[:, KD - 1, :], ALU.add).then_inc(sq_used, 1)
            dve.wait_ge(n4_rs, 2)
            for f in range(KD):
                dve.scalar_tensor_tensor(mix[:, f, :], x4[:, f, :], par("g_pre_ffn", f), sq4[:, :],
                                         ALU.mult, ALU.mult).then_inc(h2_full, 1)
                if f:
                    dve.wait_ge(h2_hi, f)
                    dve.tensor_tensor(hl[:, f - 1, :], mix[:, f - 1, :], hh[:, f - 1, :].bitcast(F32), ALU.subtract)\
                        .then_inc(h2_ready, 1)
            dve.wait_ge(h2_hi, KD)
            dve.tensor_tensor(hl[:, KD - 1, :], mix[:, KD - 1, :], hh[:, KD - 1, :].bitcast(F32), ALU.subtract)\
                .then_inc(h2_ready, 1)
            dve.wait_ge(h2_ready, KD)
            dve.wait_ge(x1_stored, 16 * KD)
            for j in range(2):
                dve.memset(acc[:, 4 * j:4 * j + 4, :], 0.0).then_inc(acc_added, 1)
            with dve.Fori(0, FCH) as c:
                for j in range(4):
                    h = hid[:, j % 2, :]
                    dve.wait_ge(hid_relu, c * 4 + (j + 1))
                    dve.tensor_tensor(h, h, h, ALU.mult).then_inc(hid_sq, 1)
                    dve.wait_ge(hid_hi, c * 4 + (j + 1))
                    dve.tensor_tensor(fl[:, j, :], h, fh[:, j, :].bitcast(F32), ALU.subtract).then_inc(hid_ready, 1)
                for j in range(8):
                    dve.wait_ge(unit_done, c * 12 + (U2 + 60 + j + 1))
                    dve.wait_ge(acc_added, c * 8 + (j + 1))
                    dve.tensor_tensor(v3(acc[:, j, :]), v3(acc[:, j, :]), psg(3 * (j % 2)), ALU.add)\
                        .then_inc(acc_added, 1)
            for f in range(KD):
                dve.wait_ge(fin_sq, f + 1)
                if f == 0:
                    dve.tensor_copy(ss5[:, :], sq5[:, :]).then_inc(fin_ss, 1)
                else:
                    dve.wait_ge(fin_ss, f)
                    dve.tensor_tensor(ss5[:, :], ss5[:, :], sq5[:, :], ALU.add).then_inc(fin_ss, 1)
            dve.wait_ge(n4_rs, 3)
            dve.wait_ge(x5_in, 16)
            for f in range(KD):
                dve.scalar_tensor_tensor(acc[:, f, :], acc[:, f, :], par("g_post_ffn", f), sq5[:, :],
                                         ALU.mult, ALU.mult).then_inc(y_seq, 1)
                dve.wait_ge(y_seq, f + 1)
                dve.tensor_tensor(acc[:, f, :], acc[:, f, :], hl[:, f, :].bitcast(F32), ALU.add).then_inc(y_ready, 1)


LN_V = (3, 10)
LN_CENTER, LN_SCALED, LN_DONE = 7, 14, 18
CHAIN_V = 127


LN_A = (None, None, 1, 3, 3, 8)

_PARAMS = ("g_pre_mix", "g_post_mix", "g_pre_ffn", "g_post_ffn")


def kernel(**inputs):
    import numpy as np
    import concourse.bacc as _bacc
    from concourse import mybir as _mybir
    from concourse.bass_utils import run_bass_kernel_spmd as _run

    x = {k: np.asarray(v) for k, v in inputs.items()}
    f32 = np.float32

    def cols(v):
        return v.reshape(-1, P).T

    i = np.arange(P)
    ident = np.eye(P, dtype=f32)
    neg = np.where(i[None, :] < i[:, None], 0.0, NEG_BIG).astype(f32)
    levels = [((i[:, None] // s == i[None, :] // s) & (i[:, None] % s < s // 2) & (i[None, :] % s >= s // 2))
              for s in LEVELS]
    keep = np.ones(T, f32)
    keep[0:TP:P] = 0
    keep[TP::TS] = 0
    masks = np.concatenate([np.stack(levels, 1).reshape(P, -1).astype(f32), np.broadcast_to(keep, (P, T))], 1)
    r = np.arange(P)
    key = np.arange(SM)
    neg_new = np.where((r[:, None] // 8 == key[None, :] // TS) & (key[None, :] % TS < r[:, None] % TS), 0.0,
                       NEG_BIG).astype(f32)
    own = (r[:, None] // TS == np.arange(NSEQ)[None, :]).astype(f32)
    bias = x["sb_bias"][0]
    sample_bias = bias.reshape(NH, 2)[:, (r // TS) % 2].T
    conv_w = x["conv_w"][0].T.reshape(NH, P, CW).transpose(1, 0, 2).reshape(P, -1)
    params = np.concatenate(
        [cols(x[n][0]) for n in _PARAMS] + [cols(x["a_norm"][0]), conv_w, cols(x["conv_b"][0]), cols(x["ln_g"][0]),
         cols(x["ln_b"][0]), np.broadcast_to(bias, (P, 2 * NH)), sample_bias, ident, neg, neg_new, own], 1)
    ins = {
        "params": params,
        "masks": masks,
        "pages": x["page_table"].reshape(1, -1),
        "xT": np.concatenate([x["x_prompt"][0], x["x_sample"].reshape(SM, D)], 0).T,
        "kcT": x["cache_k"][0].reshape(-1, P, 8 * DH).transpose(0, 2, 1),
        "vc": x["cache_v"][0].reshape(-1, P, 8 * DH),
        "s_in": x["state_hgrn"][0],
        "conv_prev": x["state_conv"][0].transpose(2, 0, 1),
        "w_in": x["w_in"][0], "w_pa": x["w_pa"][0], "w_pb": x["w_pb"][0], "w_pc": x["w_pc"][0],
        "w_o": x["w_o"][0], "w_ff1": x["w_ff1"][0], "w_ff2": x["w_ff2"][0],
    }
    outs = {
        "yT": (D, T), "k_out": (8 * DH, T), "v_out": (8 * DH, T), "hgrn_p": (NH, P, P), "hgrn_s": (NSEQ, NH, P, P),
        "conv_p": (NH * P, PAD), "conv_s": (NH * P, NSEQ, PAD),
    }
    nc = _bacc.Bacc("TRN2", target_bir_lowering=False, num_devices=1)
    dr, arrays = {}, {}
    for n, a in ins.items():
        a = np.ascontiguousarray(a)
        arrays[f"in_{n}"] = a
        dr[n] = nc.dram_tensor(f"in_{n}", a.shape, _mybir.dt.from_np(a.dtype), kind="ExternalInput").ap()
    for n, shape in outs.items():
        dr[n] = nc.dram_tensor(f"out_{n}", shape, _mybir.dt.float32, kind="ExternalOutput").ap()
    for n, rows in (("oa_d", NH * P), ("ob_d", NH * P), ("c_d", NH * P), ("x1_d", D)):
        dr[n] = nc.dram_tensor(n, (rows, T), _mybir.dt.float32, kind="Internal").ap()
    build(nc, dr)
    res = _run(nc, [arrays], core_ids=[0]).results[0]
    res = {n: res[f"out_{n}"] for n in outs}
    y = res["yT"].T
    k, v = res["k_out"].T, res["v_out"].T
    heads = (1, 1, TP, 8, DH)
    heads_s = (1, NSEQ, TS, 8, DH)
    return (
        np.ascontiguousarray(y[:TP].reshape(1, TP, D)), np.ascontiguousarray(y[TP:].reshape(NSEQ, TS, D)),
        np.ascontiguousarray(k[:TP]).reshape(heads), np.ascontiguousarray(v[:TP]).reshape(heads),
        res["hgrn_p"].reshape(1, 1, NH, P, P), np.ascontiguousarray(res["conv_p"].T).reshape(1, 1, PAD, NH * P),
        np.ascontiguousarray(k[TP:]).reshape(heads_s), np.ascontiguousarray(v[TP:]).reshape(heads_s),
        res["hgrn_s"].reshape(1, NSEQ, NH, P, P),
        np.ascontiguousarray(res["conv_s"].transpose(1, 2, 0)).reshape(1, NSEQ, PAD, NH * P),
    )
```

```python
from contextlib import ExitStack

import concourse.bass as bass
from concourse import mybir

F32 = mybir.dt.float32
F32R = mybir.dt.float32r
U8 = mybir.dt.uint8
I32 = mybir.dt.int32
ALU = mybir.AluOpType
ACT = mybir.ActivationFunctionType

P = 128
D = 1024
KD = D // P
TP, NSEQ, TS = 1024, 8, 4
T = TP + NSEQ * TS
G = 3
GW = T // G
NH = 4
DH = 64
PAST = 256
NPG = 2
CH = TP // P
SM = NSEQ * TS
CW = 31
PAD = CW - 1
FF = 4096
FCH = 8
EPS = 1e-6
SBK = PAST + SM
NEG_BIG = -1e30
ZMAX = 40.0

C_QA, C_FA, C_IA, C_GA, C_QB, C_KB, C_VB, C_UA, C_UG, C_GL = (
    0, 512, 1024, 1536, 2048, 2560, 3072, 3584, 4096, 4608)
PRE = 5
A_UNITS, B_UNITS = 8, 6
PER = A_UNITS + B_UNITS
GPG = 5
NGATE = 3 * KD
U2 = PRE + PER * NH - 1
LEVELS = (128, 64, 32, 16, 8, 4, 2)
NL = len(LEVELS)

PK = {}
_at = 0
for _n, _w in (("g_pre_mix", 8), ("g_post_mix", 8), ("g_pre_ffn", 8), ("g_post_ffn", 8), ("a_norm", 1),
               ("conv_w", NH * CW), ("conv_b", NH), ("ln_g", NH), ("ln_b", NH), ("sb_bias", 2 * NH),
               ("sample_bias", NH), ("ident", P), ("neg", P), ("neg_new", SM), ("own_seq", NSEQ)):
    PK[_n] = (_at, _at + _w)
    _at += _w
NPK = _at

A_Z, A_L, A_AT = (0, 1024, 2048), (3072, 4096), 5120
A_KS, A_VS, A_QPAD, A_QFULL, A_VT, A_ZS, A_LS, A_ATS = 6144, 8192, 10240, 10816, 10880, 12032, 12320, 12608
A_OB, A_U, A_US, A_ACC = 12832, 13888, 14944, 15216
B_T1, B_B, B_D, B_W, B_KK, B_ATT, B_QB, B_KD = 0, 1056, 2112, (3168, 4224), 5280, 6336, 7392, 8448
B_VA, B_KDT, B_S0, B_O, B_OSQ, B_RS = 9504, 10656, 11808, 12832, 13888, 14944
ARENA = A_ACC + T


class Signal:

    def __init__(self, sem, per, before=0):
        self.sem, self.per, self.before = sem, per, before

    def wait(self, eng, p, k):
        eng.wait_ge(*self.at(p, k))

    def at(self, p, k):
        return self.sem, p * self.per + (self.before + k)


class Chain:

    def __init__(self, eng, sem, start=0):
        self.eng, self.sem, self.n, self.start = eng, sem, 0, start

    def mark(self, ins):
        ins.then_inc(self.sem, 1)
        self.n += 1

    def wait(self):
        self.eng.wait_ge(self.sem, self.start + self.n)

    def link(self, ins):
        self.mark(ins)
        self.wait()


def build(nc, dr):
    ctx = ExitStack()
    with ctx:
        def sem(name):
            return ctx.enter_context(nc.semaphore(name))

        def sb(name, shape, dt, stack=ctx):
            return stack.enter_context(nc.sbuf_tensor(name, shape, dt))

        hh = sb("h_hi", [P, KD, T], F32R)
        hl = sb("h_lo", [P, KD, T], F32R)
        raw = sb("w_raw", [P, 2, KD, P], F32)
        wh = sb("w_hi", [P, 2, KD, P], F32R)
        wl = sb("w_lo", [P, 2, KD, P], F32R)
        ones = sb("ones", [P, P], F32)
        pk = sb("params", [P, NPK], F32)
        eps = sb("eps", [P, 1], F32)
        levm = sb("level_masks", [P, NL, P], U8)
        keep = sb("scan_keep", [P, T], U8)
        cwp = sb("conv_w_now", [P, CW + 1], F32)
        sbp = sb("bias_now", [P, 3], F32)
        ebl = sb("chunk_decay", [P, CH + NSEQ], F32)
        pages = sb("pages", [1, NSEQ * NPG], I32)

        s2 = ExitStack()
        kT = sb("kT", [P, T], F32, s2)
        qT = sb("qT", [P, T], F32, s2)
        vT = sb("vT", [P, T], F32, s2)
        fT = sb("fT", [P, T], F32, s2)
        qA = sb("qA", [P, T], F32, s2)
        gA = sb("gA", [P, T], F32, s2)
        iT = sb("iT", [P, T], F32, s2)
        ua = sb("ua", [P, T], F32, s2)
        ug = sb("ug", [P, T], F32, s2)
        ar = sb("arena", [P, ARENA], F32, s2)
        gl = sb("gate_logits", [P, 2, T], F32, s2)
        s2.close()

        s3 = ExitStack()
        of = sb("o_full", [P, NH, T], F32, s3)
        oh = sb("o_hi", [P, NH, T], F32R, s3)
        ol = sb("o_lo", [P, NH, T], F32R, s3)
        mm_ = sb("mixed", [P, KD, T], F32, s3)
        gs = sb("gates", [P, 2, T], F32, s3)
        tm = sb("gated", [P, T], F32, s3)
        s3.close()

        s4 = ExitStack()
        x4 = sb("x_again", [P, KD, T], F32, s4)
        acc4_gap = sb("gap4", [P, NH, T], F32, s4)
        mix = sb("mix", [P, KD, T], F32, s4)
        sq4 = sb("sq4", [P, T], F32, s4)
        ss4 = sb("ss4", [P, T], F32, s4)
        s4.close()

        s5 = ExitStack()
        fh = sb("hid_hi", [P, NH, T], F32R, s5)
        fl = sb("hid_lo", [P, NH, T], F32R, s5)
        hid = sb("hid", [P, 2, T], F32, s5)
        gap5 = sb("gap5", [P, 2, T], F32, s5)
        acc = sb("ff_sum", [P, KD, T], F32, s5)
        sq5 = sb("sq5", [P, T], F32, s5)
        ss5 = sb("ss5", [P, T], F32, s5)
        s5.close()

        ps = ctx.enter_context(nc.psum_tensor("psum", [P, 8, 512], F32))
        flat = ps[:, :, :].rearrange("p b n -> p (b n)")

        def bank(b, n=512, rows=slice(0, P)):
            return ps[rows, b, 0:n]

        def banks(b, n):
            return flat[:, 512 * b:512 * b + n]

        def A(off, n, rows=slice(0, P)):
            return ar[rows, off:off + n]

        def par(name, j=0, n=1):
            a = PK[name][0] + j
            return pk[:, a:a + n]

        ident = par("ident", 0, P)
        neg = par("neg", 0, P)
        xT = A(0, KD * T).rearrange("p (k t) -> p k t", k=KD)
        sq1 = A(KD * T, 2 * T).rearrange("p (k t) -> p k t", k=2)
        ss1 = A((KD + 2) * T, T)
        rs1 = A((KD + 3) * T, T)
        mask_f = A((KD + 4) * T, NL * P + T)

        S = lambda name, per=0, before=0: Signal(sem(name), per, before)
        const_in = sem("const_in")
        pages_in = sem("pages_in")
        x_in = [sem(f"x_in{f}") for f in range(KD)]
        ones_set = sem("ones_set")
        x_squared = sem("x_squared")
        x_summed = sem("x_summed")
        ss_bcast = sem("ss_bcast")
        h_rstd = sem("h_rstd")
        h_full = sem("h_full")
        h_hi_set = sem("h_hi_set")
        h_ready = sem("h_ready")

        w_landed = [sem(f"w_landed{s}") for s in range(2)]
        w_hi_set = sem("w_hi_set")
        w_split = sem("w_split")
        unit_done = sem("unit_done")
        staged = S("unit_staged", PER, PRE)

        v_turned, v_staged = S("v_turned", 1), S("v_staged", 1)
        now_set = S("params_now", 2)
        q_pad = S("q_pad", 1)
        ug_sig = S("ug_sig", 1)
        u_ready = S("u_ready", 1)
        conv_done = S("conv_done", 1)
        prev_in = S("conv_prev_in", 16)
        ks_in = S("cache_in", 32 * NSEQ * NPG)
        z_ready, z_read = S("z_ready", 16), S("z_read", 16)
        e_ready = S("z_clipped", 16)
        exp1 = S("exp_done", 16)
        ln_ready = S("softplus_log", 16)
        arg_ready = S("arg_ready", 16)
        a_ready = S("a_ready", 16)
        t_done, at_ready = S("a_turned", 16), S("at_staged", 16)
        av_done = S("av_done", 16)
        o_read = S("ob_read", 8)
        zs_ready, zs_read = S("zs_ready", 1), S("zs_read", 1)
        es_ready, lns_ready = S("zs_clipped", 1), S("s_softplus", 1)
        args_ready, as_ready = S("args_ready", 1), S("as_ready", 1)
        ts_done, ats_ready = S("as_turned", 1), S("ats_staged", 1)
        os_done, os_read = S("os_done", 1), S("os_read", 1)
        kv_stored = S("kv_stored", 32)
        conv_stored = S("conv_stored", 48)
        ob_stored = S("ob_stored", 16)

        t1_ready = S("f_log", 1)
        sig_ready = S("sigmoids", 1)
        ia_turned, va_staged = S("ia_turned", 1), S("va_staged", 1)
        b_ready, eb_ready, qb_ready = S("decay_sum", 1), S("decay_exp", 1), S("q_decayed", 1)
        qk_ready = S("q_gated", 1)
        vm_ready = S("v_masked", 1)
        dsub, wexp, w_ready = S("level_diff", NL), S("level_exp", NL), S("level_qk", NL)
        lev_done, att_read = S("level_product", NL + 1), S("level_merged", NL + 1)
        dk_ready, dk_exp, kd_ready = S("k_diff", 1), S("k_exp", 1), S("k_decayed", 1)
        kd_turned, kdt_staged = S("kd_turned", 1), S("kdt_staged", 1)
        s0_in = S("state_in", 16)
        u_done, s_ready = S("chunk_update", 1), S("states_ready", 1)
        um_done, s0_new = S("sample_update", 1), S("sample_state", 1)
        o_done, osq_ready = S("oa_product", 1), S("oa_squared", 1)
        n_done, n_read, rs_ready = S("oa_norm_sum", 1), S("oa_norm_read", 1), S("oa_rstd", 1)
        oa_ready = S("oa_ready", 1)
        h_stored = S("hgrn_stored", 48)
        gl_stored = [S("gate_stored0", 16 * ((GPG + 1) // 2)), S("gate_stored1", 16 * (GPG // 2))]

        v_seq, a_seq = sem("vector_chain"), sem("scalar_chain")

        of_in = sem("o_in")
        ln_seq_v, ln_seq_a, ln_pe = sem("ln_vector"), sem("ln_scalar"), sem("ln_sums")
        o_hi_set, o_ready = sem("o_hi_set"), sem("o_split")
        y_free, gate_in = sem("y_read"), [sem(f"gate_in{j}") for j in range(2)]
        gate_ready, m_seq = sem("gate_ready"), sem("mixed_chain")
        m_hi_set, m_ready = sem("m_hi_set"), sem("m_split")
        x4_in = sem("x_again_in")
        mix_read, mix_sq, sq_used = sem("mix_read"), sem("mix_squared"), sem("square_added")
        n4_sum, n4_rs = sem("norm_sum"), sem("norm_rstd")
        x1_seq = sem("x1_chain")
        x1_stored = sem("x1_stored")
        x1_ready = sem("x1_ready")
        h2_full, h2_hi = sem("h2_full"), sem("h2_hi")
        h2_ready = sem("h2_split")
        hid_relu, hid_sq, hid_hi, hid_ready = sem("hid_relu"), sem("hid_squared"), sem("hid_hi_set"), sem("hid_split")
        acc_added = sem("ff_added")
        y_seq, y_ready, y_stored = sem("y_chain"), sem("y_ready"), sem("y_stored")
        x5_in = sem("x1_in")
        fin_sq, fin_ss = sem("ff_squared"), sem("ff_square_added")

        block = ctx.enter_context(nc.Block())


        def wait_apart(eng, *waits):
            waits = [(s, v if isinstance(v, int) else nc.snap(v)) for s, v in waits]
            eng.wait_ge(ones_set, 1)
            for s, v in waits:
                eng.wait_ge(s, v)

        w_in = dr["w_in"].rearrange("(k p) n -> p k n", p=P)
        w_p = [dr[n].rearrange("(k p) n -> p k n", p=P) for n in ("w_pa", "w_pb", "w_pc")]
        w_o = dr["w_o"].rearrange("(k p) n -> p k n", p=P)
        w_f1 = dr["w_ff1"].rearrange("(k p) n -> p k n", p=P)
        w_f2 = dr["w_ff2"].rearrange("(c k p) n -> c p k n", k=NH, p=P)
        A_COLS = (C_FA, None, C_QA, None, C_IA, None, C_GA, None)
        B_COLS = (C_KB, C_VB, C_QB, C_UA, C_UG, None)

        def gate_of(jj, more):
            if jj < A_UNITS:
                return jj // 2 if A_COLS[jj] is None else None
            if not more:
                return 4 + jj - A_UNITS
            return 4 if B_COLS[jj - A_UNITS] is None else None

        def cols_of(jj, p, more):
            g = gate_of(jj, more)
            if g is not None:
                return p * (GPG * P) + (g * P + C_GL)
            return p * P + (A_COLS[jj] if jj < A_UNITS else B_COLS[jj - A_UNITS] + P)

        def units(more):
            return PER if more else PER - 1

        def slot2(u):
            return u % 2, u // 2

        def load_unit2(sp, u, p, cols):
            s, n = slot2(u)
            if u >= 2:
                wait_apart(sp, (w_split, p * PER + (u - 1)))
            sp.dma_start(raw[:, s, :, :], w_in[:, :, bass.ds(cols, P)]).then_inc(w_landed[s], 16)

        def split_unit2(pool, u, p):
            s, n = slot2(u)
            over = [(unit_done, p * PER + (u - 1))] if u >= 2 else []
            wait_apart(pool, (w_landed[s], p * (8 * PER) + 16 * (n + 1)), *over)
            pool.tensor_copy(wh[:, s, :, :], raw[:, s, :, :]).then_inc(w_hi_set, 1)
            pool.wait_ge(w_hi_set, p * PER + (u + 1))
            pool.tensor_tensor(wl[:, s, :, :], raw[:, s, :, :], wh[:, s, :, :].bitcast(F32),
                               ALU.subtract).then_inc(w_split, 1)

        def load_unit3(sp, v, slot, src, kt):
            wait_apart(sp, (w_split, v + (U2 - 1)))
            sp.dma_start(raw[:, slot, 0:kt, :], src).then_inc(w_landed[slot], 16)

        def split_unit3(pool, v, slot, use, kt):
            wait_apart(pool, (w_landed[slot], (use + (U2 // 2 + 1)) * 16), (unit_done, v + (U2 - 1)))
            pool.tensor_copy(wh[:, slot, 0:kt, :], raw[:, slot, 0:kt, :]).then_inc(w_hi_set, 1)
            pool.wait_ge(w_hi_set, v + (U2 + 1))
            pool.tensor_tensor(wl[:, slot, 0:kt, :], raw[:, slot, 0:kt, :], wh[:, slot, 0:kt, :].bitcast(F32),
                               ALU.subtract).then_inc(w_split, 1)

        def product(pe, slot, ks, kt, xh, xl, b0):
            for k in ks:
                for w, x in ((wh, xh), (wh, xl), (wl, xh)):
                    for g in range(G):
                        mm = pe.matmul(ps[:, b0 + g, 0:GW], w[:, slot, k, :], x[:, k, g * GW:(g + 1) * GW],
                                       start=(k == 0 and w is wh and x is xh), stop=(k == kt - 1 and w is wl))
            return mm

        @block.sync
        def _(sp):
            sp.dma_start(pk[:, :], dr["params"]).then_inc(const_in, 16)
            sp.dma_start(mask_f, dr["masks"]).then_inc(const_in, 16)
            sp.dma_start(pages[:, :], dr["pages"]).then_inc(pages_in, 16)
            for f in range(KD):
                sp.dma_start(xT[:, f, :], dr["xT"][f * P:(f + 1) * P, :]).then_inc(x_in[f], 16)
            for u in range(PRE):
                load_unit2(sp, u, 0, B_COLS[u])
            for jj in range(3):
                load_unit2(sp, PRE + jj, 0, cols_of(jj, 0, True))
            sp.wait_ge(pages_in, 16)
            page = [sp.value_load(pages[0:1, i:i + 1], min_val=0, max_val=dr["kcT"].shape[0] - 1)
                    for i in range(NSEQ * NPG)]
            sp.wait_ge(h_ready, KD)
            ksv = A(A_KS, 2048).rearrange("p (b g n) -> p b g n", b=NSEQ, g=NPG)
            vsv = A(A_VS, 2048).rearrange("p (b g n) -> p b g n", b=NSEQ, g=NPG)

            def group(p, more):
                for i in range(NSEQ * NPG):
                    b, g = divmod(i, NPG)
                    sp.dma_start(ksv[:, b, g, :], dr["kcT"][bass.ds(page[i], 1), bass.ds(p * P, P), :]
                                 .rearrange("a d t -> (a d) t")).then_inc(ks_in.sem, 16)
                    sp.dma_start(vsv[:, b, g, :], dr["vc"][bass.ds(page[i], 1), :, bass.ds(p * P, P)]
                                 .rearrange("a t d -> (a t) d")).then_inc(ks_in.sem, 16)
                sp.dma_start(A(A_US, NSEQ * (PAD + TS)).rearrange("p (b t) -> p b t", b=NSEQ)[:, :, 0:PAD],
                             dr["conv_prev"][bass.ds(p * P, P), :, :]).then_inc(prev_in.sem, 16)
                load = lambda jj: load_unit2(sp, PRE + jj, p, cols_of(jj, p, more))
                following = lambda jj: load_unit2(sp, PRE + PER + jj, p, cols_of(jj, p + 1, True)) if more else None

                def store_gate(jj):
                    g = gate_of(jj, more)
                    wait_apart(sp, staged.at(p, jj + 1))
                    sp.dma_start(dr["g_d"][bass.ds(p * (GPG * P) + g * P, P), :], gl[:, g % 2, :])\
                        .then_inc(gl_stored[g % 2].sem, 16)

                load(3)
                wait_apart(sp, staged.at(p, -3))
                sp.dma_start(dr["k_out"][bass.ds(p * P, P), :], kT[:, :]).then_inc(kv_stored.sem, 16)
                sp.dma_start(dr["v_out"][bass.ds(p * P, P), :], vT[:, :]).then_inc(kv_stored.sem, 16)
                load(4)
                store_gate(1)
                load(5)
                load(6)
                store_gate(3)
                load(7)
                load(8)
                store_gate(5)
                load(9)
                load(10)
                store_gate(7)
                wait_apart(sp, conv_done.at(p, 1))
                sp.dma_start(dr["c_d"][bass.ds(p * P, P), :], A(A_ACC, T)).then_inc(conv_stored.sem, 16)
                sp.dma_start(dr["conv_p"][bass.ds(p * P, P), :],
                             A(A_U + TP, PAD)).then_inc(conv_stored.sem, 16)
                sp.dma_start(dr["conv_s"][bass.ds(p * P, P), :, :],
                             A(A_US, NSEQ * (PAD + TS)).rearrange("p (b t) -> p b t", b=NSEQ)[:, :, TS:])\
                    .then_inc(conv_stored.sem, 16)
                wait_apart(sp, av_done.at(p, 16))
                wait_apart(sp, os_done.at(p, 1))
                sp.dma_start(A(B_S0, NSEQ * P).rearrange("p (b v) -> p b v", b=NSEQ),
                             dr["s_in"][:, bass.ds(p, 1), :, :].rearrange("b a d v -> d (b a) v"))\
                    .then_inc(s0_in.sem, 16)
                wait_apart(sp, o_read.at(p, 8))
                wait_apart(sp, os_read.at(p, 1))
                sp.dma_start(dr["ob_d"][bass.ds(p * P, P), :], A(A_OB, T)).then_inc(ob_stored.sem, 16)
                load(11)
                if not more:
                    store_gate(8)
                load(12)
                if more:
                    load(13)
                else:
                    for jj in (9, 10, 11):
                        store_gate(jj)
                following(0)
                wait_apart(sp, s_ready.at(p, 1))
                sp.dma_start(dr["hgrn_p"][bass.ds(p, 1), :, :].rearrange("a d v -> (a d) v"),
                             A(B_D + 7 * P, P)).then_inc(h_stored.sem, 16)
                following(1)
                wait_apart(sp, s0_new.at(p, 1))
                sp.dma_start(dr["hgrn_s"][:, bass.ds(p, 1), :, :].rearrange("b a d v -> d (b a) v"),
                             A(B_W[0], NSEQ * P).rearrange("p (b v) -> p b v", b=NSEQ)).then_inc(h_stored.sem, 16)
                following(2)
                wait_apart(sp, oa_ready.at(p, 1))
                sp.dma_start(dr["oa_d"][bass.ds(p * P, P), :], A(B_O, T)).then_inc(h_stored.sem, 16)
                store_gate(13 if more else 12)

            with sp.Fori(0, NH - 1) as p:
                group(p, True)
            group(NH - 1, False)

            h_stored.wait(sp, NH - 1, 48)
            conv_stored.wait(sp, NH - 1, 48)
            ob_stored.wait(sp, NH - 1, 16)
            kv_stored.wait(sp, NH - 1, 32)
            for b in range(2):
                gl_stored[b].wait(sp, NH - 1, 16 * ((NGATE - GPG * (NH - 1) - b + 1) // 2))
            for x, src in enumerate(("c_d", "oa_d", "ob_d")):
                if x:
                    sp.wait_ge(o_ready, 4 * x)
                sp.dma_start(of[:, :, :], dr[src].rearrange("(k p) t -> p k t", p=P)).then_inc(of_in, 16)
                xx = BRANCH[x]
                with sp.Fori(0, 4) as i:
                    for j in range(2):
                        load_unit3(sp, i * 2 + (8 * x + j), j, w_p[xx][:, :, bass.ds(i * (2 * P) + j * P, P)], NH)
                        wait_apart(sp, (y_free, i * 2 + (8 * x + j + 1)))
                        sp.dma_start(gs[:, j, :], dr["g_d"][bass.ds(i * (2 * P) + (xx * D + j * P), P), :])\
                            .then_inc(gate_in[j], 16)
            with sp.Fori(0, 4) as i:
                for j in range(2):
                    load_unit3(sp, i * 2 + (24 + j), j, w_o[:, :, bass.ds(i * 2 * P + j * P, P)], KD)
            sp.wait_ge(o_ready, 12)
            sp.wait_ge(unit_done, U2 + 24)
            sp.dma_start(x4[:, :, :], dr["xT"].rearrange("(k p) t -> p k t", p=P)).then_inc(x4_in, 16)
            with sp.Fori(0, FCH) as c:
                for j in range(4):
                    load_unit3(sp, c * 12 + (32 + j), j % 2, w_f1[:, :, bass.ds(c * 4 * P + j * P, P)], KD)
                for j in range(8):
                    load_unit3(sp, c * 12 + (36 + j), j % 2,
                               w_f2[bass.ds(c, 1), :, :, j * P:(j + 1) * P].rearrange("c p k n -> (c p) k n"), NH)
            for f in range(KD):
                sp.wait_ge(y_ready, f + 1)
                sp.dma_start(dr["yT"][f * P:(f + 1) * P, :], acc[:, f, :]).then_inc(y_stored, 16)
            sp.wait_ge(y_stored, 16 * KD)

        @block.gpsimd
        def _(pool):
            for u in range(PRE):
                split_unit2(pool, u, 0)
            with pool.Fori(0, NH - 1) as p:
                for jj in range(PER):
                    split_unit2(pool, PRE + jj, p)
            for jj in range(PER - 1):
                split_unit2(pool, PRE + jj, NH - 1)
            with pool.Fori(0, 12) as n:
                split_unit3(pool, n * 2, 0, n, NH)
                split_unit3(pool, n * 2 + 1, 1, n, NH)
            with pool.Fori(12, 16) as n:
                split_unit3(pool, n * 2, 0, n, KD)
                split_unit3(pool, n * 2 + 1, 1, n, KD)
            with pool.Fori(0, FCH) as c:
                for j in range(12):
                    split_unit3(pool, c * 12 + (32 + j), j % 2, c * 6 + (16 + j // 2), KD if j < 4 else NH)

        @block.tensor
        def _(pe):
            def unit_part(u, p, ks):
                if 0 in ks:
                    pe.wait_ge(w_split, p * PER + (u + 1))
                    if u:
                        pe.wait_ge(staged.sem, p * PER + u)
                mm = product(pe, u % 2, ks, KD, hh, hl, 0)
                if KD - 1 in ks:
                    mm.then_inc(unit_done, 1)

            pe.wait_ge(ones_set, 2)
            pe.wait_ge(x_summed, KD)
            for g in range(G):
                mm = pe.matmul(ps[:, g + 3, 0:GW], ones[:, :], ss1[:, g * GW:(g + 1) * GW], start=True, stop=True)
            mm.then_inc(ss_bcast, 1)
            for k in range(KD):
                pe.wait_ge(h_ready, k + 1)
                unit_part(0, 0, (k,))
            for u in range(1, PRE):
                unit_part(u, 0, range(KD))

            zb = [A(o, 1024) for o in A_Z]
            atv = A(A_AT, 1024)
            vtok = A(A_VT, 9 * P).rearrange("p (n d) -> p n d", n=9)
            ksv = A(A_KS, 2048).rearrange("p (b n) -> p b n", b=NSEQ)
            vsv = A(A_VS, 2048).rearrange("p (b g n) -> p b g n", b=NSEQ, g=NPG)
            ats = A(A_ATS, 192).rearrange("p (g n) -> p g n", g=3)

            def scores(p, i):
                qb, e = divmod(i, 2)
                rows = slice(DH * e, DH * e + DH)
                if i:
                    z_read.wait(pe, p, i)
                if i == 8:
                    zs_read.wait(pe, p, 1)
                nk = P * (qb + 1)
                for a in range(0, nk, 512):
                    n = min(512, nk - a)
                    mm = pe.matmul(ps[:, 3 + a // 512, 0:n], qT[rows, qb * P:(qb + 1) * P], kT[rows, a:a + n],
                                   start=True, stop=True)
                mm.then_inc(z_ready.sem, 1)

            def turn_a(p, i):
                a_ready.wait(pe, p, i + 1)
                if i:
                    at_ready.wait(pe, p, i)
                if i == 8:
                    os_read.wait(pe, p, 1)
                for kb in range(i // 2 + 1):
                    mm = pe.transpose(banks(5, 1024)[:, kb * P:(kb + 1) * P], zb[i % 3][:, kb * P:(kb + 1) * P], ident)
                mm.then_inc(t_done.sem, 1)

            def values(p, i):
                qb, e = divmod(i, 2)
                at_ready.wait(pe, p, i + 1)
                if e == 0 and qb:
                    o_read.wait(pe, p, qb)
                for kb in range(qb + 1):
                    mm = pe.matmul(ps[DH * e:DH * e + DH, 7, (qb % 4) * P:(qb % 4 + 1) * P],
                                   vtok[:, kb, DH * e:DH * e + DH], atv[:, kb * P:(kb + 1) * P],
                                   start=(kb == 0), stop=(kb == qb))
                mm.then_inc(av_done.sem, 1)

            def sample_scores(p):
                ks_in.wait(pe, p, 32 * NSEQ * NPG)
                q_pad.wait(pe, p, 1)
                for b in range(NSEQ):
                    pe.matmul(ps[0:64, 4, 0:PAST], A(A_QPAD + 64 * b, 64), ksv[:, b, :],
                              start=(b == 0), stop=(b == NSEQ - 1))
                pe.matmul(ps[0:64, 4, PAST:SBK], A(A_QFULL, 64), kT[:, TP:T], start=True, stop=True)\
                    .then_inc(zs_ready.sem, 1)

            def sample_turn(p):
                wait_apart(pe, as_ready.at(p, 1))
                for j in range(2):
                    pe.transpose(ps[:, 6, 64 * j:64 * j + 64], A(A_ZS + P * j, P, slice(0, 64)), ident[0:64, 0:64])
                pe.transpose(ps[0:SM, 6, 128:192], A(A_ZS + PAST, SM, slice(0, 64)), ident[0:64, 0:64])\
                    .then_inc(ts_done.sem, 1)

            def sample_values(p):
                ats_ready.wait(pe, p, 1)
                pe.matmul(ps[:, 6, 256:320], vtok[0:SM, 8, :], ats[0:SM, 2, :], start=True, stop=False,
                          skip_group_check=True)
                for b in range(NSEQ):
                    for g in range(NPG):
                        mm = pe.matmul(ps[:, 6, 256 + 8 * b:264 + 8 * b], vsv[:, b, g, :], ats[:, g, 8 * b:8 * b + 8],
                                       start=False, stop=(b == NSEQ - 1 and g == NPG - 1), skip_group_check=True)
                mm.then_inc(os_done.sem, 1)

            wb = [A(o, T) for o in B_W]
            kk, att, qbt, kd = A(B_KK, T), A(B_ATT, T), A(B_QB, T), A(B_KD, T)
            va = A(B_VA, 9 * P).rearrange("p (n d) -> p n d", n=9)
            kdt = A(B_KDT, 9 * P).rearrange("p (n d) -> p n d", n=9)
            s0 = A(B_S0, NSEQ * P).rearrange("p (b v) -> p b v", b=NSEQ)

            def turn9(src, b0):
                for c in range(CH):
                    pe.transpose(banks(b0, 1024)[:, c * P:(c + 1) * P], src[:, c * P:(c + 1) * P], ident)
                return pe.transpose(ps[0:SM, 7, 0:P], src[:, TP:T], ident)

            def level_product(p, idx, left, right, b0, sample):
                for c in range(CH):
                    mm = pe.matmul(banks(b0, 1024)[:, c * P:(c + 1) * P], left[:, c * P:(c + 1) * P],
                                   right[:, c * P:(c + 1) * P], start=True, stop=True)
                if sample:
                    mm = pe.matmul(ps[0:SM, 7, 0:SM], left[:, TP:T], right[:, TP:T], start=True, stop=True)
                mm.then_inc(lev_done.sem, 1)

            def group(p, more):
                def half(jj, h):
                    if jj < units(more):
                        unit_part(PRE + jj, p, range(4 * h, 4 * h + 4))

                def half_b(s):
                    half(A_UNITS + s // 2, s % 2)

                staged.wait(pe, p, -2)
                turn9(vT, 5).then_inc(v_turned.sem, 1)
                for s in range(19):
                    if s < 16:
                        scores(p, s)
                        half(s // 2, s % 2)
                    if s == 3:
                        v_staged.wait(pe, p, 1)
                    if s >= 3:
                        values(p, s - 3)
                    if s == 2:
                        v_staged.wait(pe, p, 1)
                    if 2 <= s < 18:
                        turn_a(p, s - 2)
                    if s == 3:
                        sample_scores(p)
                    if s == 7:
                        sample_turn(p)
                    if s == 9:
                        sample_values(p)
                staged.wait(pe, p, 3)
                at_ready.wait(pe, p, 16)
                o_read.wait(pe, p, 8)
                turn9(iT, 5).then_inc(ia_turned.sem, 1)
                half_b(0)
                qk_ready.wait(pe, p, 1)
                va_staged.wait(pe, p, 1)
                level_product(p, 0, kk, qA, 3, True)
                half_b(1)
                for j in range(NL):
                    w_ready.wait(pe, p, j + 1)
                    sample = LEVELS[j] <= TS
                    att_read.wait(pe, p, j + (1 if sample else 0) if j else 1)
                    level_product(p, j + 1, wb[j % 2], wb[j % 2], 5 if j % 2 == 0 else 3, sample)
                    if j < 5:
                        half_b(2 + j)
                half_b(7)
                kd_ready.wait(pe, p, 1)
                att_read.wait(pe, p, NL + 1)
                turn9(kd, 3).then_inc(kd_turned.sem, 1)
                half_b(8)
                kdt_staged.wait(pe, p, 1)
                for c in range(CH):
                    mm = pe.matmul(banks(5, 1024)[:, c * P:(c + 1) * P], kdt[:, c, :], va[:, c, :],
                                   start=True, stop=True)
                mm.then_inc(u_done.sem, 1)
                vm_ready.wait(pe, p, 1)
                for j in range(2):
                    mm = pe.matmul(ps[:, 3 + j, :], kdt[0:SM, 8, :], A(B_T1 + 512 * j, 512, slice(0, SM)),
                                   start=True, stop=True)
                mm.then_inc(um_done.sem, 1)
                half_b(9)
                s_ready.wait(pe, p, 1)
                qb_ready.wait(pe, p, 1)
                s0_in.wait(pe, p, 16)
                for c in range(CH):
                    o = banks(5, 1024)[:, c * P:(c + 1) * P]
                    pe.matmul(o, va[:, c, :], att[:, c * P:(c + 1) * P], start=True, stop=(c == 0))
                    if c:
                        pe.matmul(o, A(B_D + (c - 1) * P, P), qbt[:, c * P:(c + 1) * P], start=False, stop=True)
                pe.matmul(ps[:, 7, 0:SM], va[0:SM, 8, :], att[0:SM, TP:T], start=True, stop=False,
                          skip_group_check=True)
                for b in range(NSEQ):
                    mm = pe.matmul(ps[:, 7, TS * b:TS * b + TS], s0[:, b, :], qbt[:, TP + TS * b:TP + TS * b + TS],
                                   start=False, stop=(b == NSEQ - 1), skip_group_check=True)
                mm.then_inc(o_done.sem, 1)
                half_b(10)
                osq_ready.wait(pe, p, 1)
                s0_new.wait(pe, p, 1)
                for a, n in ((0, 512), (512, 512), (1024, 32)):
                    mm = pe.matmul(banks(3, T)[:, a:a + n], ones[:, :], A(B_OSQ + a, n), start=True, stop=True)
                mm.then_inc(n_done.sem, 1)
                half_b(11)
                n_read.wait(pe, p, 1)

            with pe.Fori(0, NH - 1) as p:
                group(p, True)
            group(NH - 1, False)

            for r in range(2):
                for g in range(G):
                    pe.wait_ge(ln_seq_v, LN_V[r])
                    if LN_A[r * G + g]:
                        pe.wait_ge(ln_seq_a, LN_A[r * G + g])
                    pe.matmul(ps[:, 6 + (r * G + g) % 2, 0:GW], ones[:, :], tm[:, g * GW:(g + 1) * GW],
                              start=True, stop=True).then_inc(ln_pe, 1)
            pe.wait_ge(staged.sem, U2)
            for x in range(3):
                with pe.Fori(0, 4) as i:
                    for j in range(2):
                        pe.wait_ge(w_split, i * 2 + (U2 + 8 * x + j + 1))
                        pe.wait_ge(y_free, i * 2 + (8 * x + j + 1))
                        for k in range(NH):
                            if j == 0:
                                pe.wait_ge(o_ready, 4 * x + k + 1)
                            mm = product(pe, j, (k,), NH, oh, ol, 3 * j)
                        mm.then_inc(unit_done, 1)

            def wo_unit(i, j, first):
                pe.wait_ge(w_split, i * 2 + (U2 + 24 + j + 1))
                if not first:
                    pe.wait_ge(mix_read, i * 2 + (j - 1))
                if first and j == 0:
                    pe.wait_ge(y_free, 25)
                    for k in range(KD):
                        pe.wait_ge(m_ready, k + 1)
                        mm = product(pe, j, (k,), KD, hh, hl, 0)
                else:
                    if first:
                        pe.wait_ge(y_free, 26)
                    mm = product(pe, j, range(KD), KD, hh, hl, 3 * j)
                mm.then_inc(unit_done, 1)

            wo_unit(0, 0, True)
            wo_unit(0, 1, True)
            with pe.Fori(1, 4) as i:
                wo_unit(i, 0, False)
                wo_unit(i, 1, False)

            def norm_sum(src, value, sem_in, sem_out):
                pe.wait_ge(sem_in, value)
                for g in range(G):
                    mm = pe.matmul(ps[:, g, 0:GW], ones[:, :], src[:, g * GW:(g + 1) * GW], start=True, stop=True)
                mm.then_inc(sem_out, 1)

            pe.wait_ge(mix_read, 8)
            norm_sum(ss4, KD, sq_used, n4_sum)
            norm_sum(ss4, 2 * KD, sq_used, n4_sum)
            pe.wait_ge(n4_rs, 2)
            pe.wait_ge(h2_ready, KD)
            with pe.Fori(0, FCH) as c:
                for j in range(4):
                    pe.wait_ge(w_split, c * 12 + (U2 + 32 + j + 1))
                    if j < 2:
                        pe.wait_ge(acc_added, c * 8 + (j + 1))
                    else:
                        pe.wait_ge(hid_relu, c * 4 + (j - 1))
                    product(pe, j % 2, range(KD), KD, hh, hl, 3 * (j % 2)).then_inc(unit_done, 1)
                for j in range(8):
                    pe.wait_ge(w_split, c * 12 + (U2 + 36 + j + 1))
                    if j < 2:
                        pe.wait_ge(hid_relu, c * 4 + (j + 3))
                    else:
                        pe.wait_ge(acc_added, c * 8 + (j + 1))
                    for k in range(NH):
                        if j == 0:
                            pe.wait_ge(hid_ready, c * 4 + (k + 1))
                        mm = product(pe, j % 2, (k,), NH, fh, fl, 3 * (j % 2))
                    mm.then_inc(unit_done, 1)
            pe.wait_ge(acc_added, 8 * FCH + 2)
            norm_sum(ss5, KD, fin_ss, n4_sum)

        @block.scalar
        def _(act):
            IDN = ACT.Identity

            for f in range(KD):
                act.wait_ge(x_in[f], 16)
                if f >= 2:
                    act.wait_ge(x_summed, f - 1)
                act.activation(sq1[:, f % 2, :], xT[:, f, :], ACT.Square).then_inc(x_squared, 1)
            act.wait_ge(ss_bcast, 1)
            act.wait_ge(ones_set, 2)
            psg = lambda b0: ps[:, b0:b0 + G, 0:GW]
            v3 = lambda ap: ap.rearrange("p (g t) -> p g t", g=G)
            act.activation(v3(rs1), psg(3), ACT.Ln, bias=eps[:, 0:1], scale=1.0 / D).then_inc(a_seq, 1)
            act.wait_ge(a_seq, 1)
            act.activation(rs1, rs1, ACT.Exp, scale=-0.5).then_inc(h_rstd, 1)
            for f in range(KD):
                act.wait_ge(h_full, f + 1)
                act.activation(hh[:, f, :], xT[:, f, :], ACT.Copy).then_inc(h_hi_set, 1)

            def stage(u, p, dst, scale=None):
                act.wait_ge(unit_done, p * PER + (u + 1))
                ins = (act.activation(v3(dst), psg(0), ACT.Copy) if scale is None else
                       act.activation(v3(dst), psg(0), ACT.Copy, scale=scale))
                ins.then_inc(staged.sem, 1)

            B_DST = ((kT[:, :], None), (vT[:, :], None), (qT[:, :], DH ** -0.5), (ua[:, :], None), (ug[:, :], None))
            A_DST = (fT[:, :], qA[:, :], iT[:, :], gA[:, :])
            for u in range(PRE):
                stage(u, 0, *B_DST[u])
            lnexp = lambda: act.preload_act_table_set("natural_log_exp_and_others")

            def stage_unit(jj, p, more):
                g = gate_of(jj, more)
                if jj >= units(more):
                    return
                if g is not None:
                    if g >= 2:
                        gl_stored[g % 2].wait(act, p, 16 * (g // 2))
                    stage(PRE + jj, p, gl[:, g % 2, :])
                elif jj < A_UNITS:
                    stage(PRE + jj, p, A_DST[jj // 2])
                else:
                    stage(PRE + jj, p, *B_DST[jj - A_UNITS])

            zb = [A(o, 1024) for o in A_Z]
            lb = [A(o, 1024) for o in A_L]
            vtok = A(A_VT, 9 * P)
            ob = A(A_OB, T)
            CHAIN_A = 3

            def group(p, more):
                ch = Chain(act, a_seq, p * CHAIN_A + 1)
                staged.wait(act, p, 0)
                act.activation(ug[:, :], ug[:, :], ACT.Sigmoid).then_inc(ug_sig.sem, 1)
                lnexp()
                v_turned.wait(act, p, 1)
                act.activation(vtok[:, 0:1024], banks(5, 1024), ACT.Copy)
                act.activation(vtok[0:SM, 1024:1152], ps[0:SM, 7, 0:P], ACT.Copy).then_inc(v_staged.sem, 1)
                now_set.wait(act, p, 2)
                for s in range(20):
                    i = s - 3
                    if 2 <= s <= 16 and s % 2 == 0:
                        stage_unit(s // 2 - 1, p, more)
                    if 0 <= i < 16:
                        t_done.wait(act, p, i + 1)
                        if i:
                            av_done.wait(act, p, i)
                        n = P * (i // 2 + 1)
                        act.activation(A(A_AT, n), banks(5, n), ACT.Copy).then_inc(at_ready.sem, 1)
                    if s >= 5 and s % 2 == 1:
                        qb = (s - 5) // 2
                        av_done.wait(act, p, 2 * qb + 2)
                        act.activation(ob[:, qb * P:(qb + 1) * P], ps[:, 7, (qb % 4) * P:(qb % 4 + 1) * P],
                                       ACT.Copy).then_inc(o_read.sem, 1)
                    if s < 16:
                        z_ready.wait(act, p, s + 1)
                        if s >= 3:
                            t_done.wait(act, p, s - 2)
                        n = P * (s // 2 + 1)
                        act.activation(zb[s % 3][:, 0:n], banks(3, n), IDN, bias=sbp[:, s % 2:s % 2 + 1])\
                            .then_inc(z_read.sem, 1)
                    if 0 <= s - 1 < 16:
                        n = P * ((s - 1) // 2 + 1)
                        l = lb[(s - 1) % 2][:, 0:n]
                        e_ready.wait(act, p, s)
                        act.activation(l, l, ACT.Exp).then_inc(exp1.sem, 1)
                        exp1.wait(act, p, s)
                        act.activation(l, l, ACT.Ln, bias=1.0).then_inc(ln_ready.sem, 1)
                    if 0 <= s - 2 < 16:
                        n = P * ((s - 2) // 2 + 1)
                        z = zb[(s - 2) % 3][:, 0:n]
                        arg_ready.wait(act, p, s - 1)
                        act.activation(z, z, ACT.Exp).then_inc(a_ready.sem, 1)
                    if s == 4:
                        zs_ready.wait(act, p, 1)
                        act.activation(A(A_ZS, SBK, slice(0, 64)), ps[0:64, 4, 0:SBK], IDN, bias=sbp[0:64, 2:3])\
                            .then_inc(zs_read.sem, 1)
                    if s == 5:
                        l = A(A_LS, SBK, slice(0, 64))
                        es_ready.wait(act, p, 1)
                        ch.link(act.activation(l, l, ACT.Exp))
                        act.activation(l, l, ACT.Ln, bias=1.0).then_inc(lns_ready.sem, 1)
                    if s == 6:
                        args_ready.wait(act, p, 1)
                        z = A(A_ZS, SBK, slice(0, 64))
                        act.activation(z, z, ACT.Exp).then_inc(as_ready.sem, 1)
                    if s == 8:
                        ts_done.wait(act, p, 1)
                        act.activation(A(A_ATS, 128), ps[:, 6, 0:128], ACT.Copy)
                        act.activation(A(A_ATS + 128, 64, slice(0, SM)), ps[0:SM, 6, 128:192], ACT.Copy)\
                            .then_inc(ats_ready.sem, 1)
                    if s == 10:
                        os_done.wait(act, p, 1)
                        for e in range(2):
                            r = slice(DH * e, DH * e + DH)
                            ins = act.activation(ar[r, A_OB + TP:A_OB + T].rearrange("p (b q) -> p b q", b=NSEQ),
                                                 ps[r, 6, 256:320].rearrange("p (b e q) -> p b e q", b=NSEQ, e=2)
                                                 [:, :, e, :], ACT.Copy)
                        ins.then_inc(os_read.sem, 1)

                av_done.wait(act, p, 16)
                t_done.wait(act, p, 16)
                staged.wait(act, p, A_UNITS)
                t1 = A(B_T1, T)
                ch.link(act.activation(t1, fT[:, :], ACT.Abs))
                ch.link(act.activation(t1, t1, ACT.Exp, scale=-1.0))
                act.activation(t1, t1, ACT.Ln, bias=1.0).then_inc(t1_ready.sem, 1)
                arg_ready.wait(act, p, 16)
                act.activation(A(B_W[0], T), qA[:, :], ACT.Sigmoid)
                act.activation(A(B_W[1], T), gA[:, :], ACT.Sigmoid)
                act.activation(A(B_KK, T), fT[:, :], ACT.Sigmoid, scale=-1.0).then_inc(sig_ready.sem, 1)
                lnexp()
                ia_turned.wait(act, p, 1)
                os_read.wait(act, p, 1)
                act.activation(A(B_VA, 1024), banks(5, 1024), ACT.Copy)
                act.activation(A(B_VA + 1024, P, slice(0, SM)), ps[0:SM, 7, 0:P], ACT.Copy).then_inc(va_staged.sem, 1)
                b_ready.wait(act, p, 1)
                act.activation(A(B_QB, T), A(B_B, T), ACT.Exp).then_inc(eb_ready.sem, 1)
                qk_ready.wait(act, p, 1)
                if more:
                    kv_stored.wait(act, p, 32)
                    u_ready.wait(act, p, 1)
                for j in range(NL):
                    dsub.wait(act, p, j + 1)
                    if j >= 2:
                        lev_done.wait(act, p, j)
                    n = T if LEVELS[j] <= TS else TP
                    act.activation(A(B_W[j % 2], n), A(B_D, n), ACT.Exp).then_inc(wexp.sem, 1)
                    if j in (0, 2, 4):
                        stage_unit(A_UNITS + j // 2, p, more)
                dk_ready.wait(act, p, 1)
                act.activation(A(B_KD, T), A(B_D, T), ACT.Exp).then_inc(dk_exp.sem, 1)
                stage_unit(A_UNITS + 3, p, more)
                kd_turned.wait(act, p, 1)
                act.activation(A(B_KDT, 1024), banks(3, 1024), ACT.Copy)
                act.activation(A(B_KDT + 1024, P, slice(0, SM)), ps[0:SM, 7, 0:P], ACT.Copy)\
                    .then_inc(kdt_staged.sem, 1)
                stage_unit(A_UNITS + 4, p, more)
                o_done.wait(act, p, 1)
                ob_stored.wait(act, p, 16)
                conv_stored.wait(act, p, 48)
                act.activation(A(B_O, T), banks(5, T), ACT.Copy)
                act.activation(A(B_OSQ, T), banks(5, T), ACT.Square).then_inc(osq_ready.sem, 1)
                n_done.wait(act, p, 1)
                ins = act.activation(A(B_RS, T), banks(3, T), ACT.Ln, bias=eps[:, 0:1], scale=1.0 / P)
                ins.then_inc(n_read.sem, 1)
                n_read.wait(act, p, 1)
                act.activation(A(B_RS, T), A(B_RS, T), ACT.Exp, scale=-0.5).then_inc(rs_ready.sem, 1)
                stage_unit(A_UNITS + 5, p, more)
                oa_ready.wait(act, p, 1)
                h_stored.wait(act, p, 48)
                for b in range(2):
                    g = (GPG - b + 1) // 2 if more else (NGATE - GPG * (NH - 1) - b + 1) // 2
                    gl_stored[b].wait(act, p, 16 * g)
                assert ch.n == CHAIN_A, ch.n

            with act.Fori(0, NH - 1) as p:
                group(p, True)
            group(NH - 1, False)

            kv_stored.wait(act, NH - 1, 32)
            n = 0

            def lnk(ins):
                nonlocal n
                n += 1
                ins.then_inc(ln_seq_a, 1)

            for g in range(G):
                act.wait_ge(ln_pe, g + 1)
                lnk(act.activation(gs[:, 0, g * GW:(g + 1) * GW], ps[:, 6 + g % 2, 0:GW], ACT.Copy, scale=1.0 / 512))
            act.wait_ge(ln_seq_v, LN_CENTER)
            for k in range(NH):
                lnk(act.activation(mm_[:, k, :], of[:, k, :], ACT.Square))
            for g in range(G):
                act.wait_ge(ln_pe, G + g + 1)
                lnk(act.activation(gs[:, 0, g * GW:(g + 1) * GW], ps[:, 6 + (G + g) % 2, 0:GW], ACT.Ln,
                                   bias=eps[:, 0:1], scale=1.0 / 512))
            act.wait_ge(ln_seq_a, n)
            lnk(act.activation(gs[:, 0, :], gs[:, 0, :], ACT.Exp, scale=-0.5))
            assert n == 11
            act.wait_ge(ln_seq_v, LN_SCALED)
            for k in range(NH):
                lnk(act.activation(of[:, k, :], of[:, k, :], IDN, bias=par("ln_b", k), scale=par("ln_g", k)))
            act.wait_ge(ln_seq_a, n)
            for k in range(NH):
                lnk(act.activation(mm_[:, k, :], of[:, k, :], ACT.Sigmoid))
            act.wait_ge(ln_seq_v, LN_DONE)
            for x in range(3):
                act.wait_ge(of_in, 16 * (x + 1))
                if x:
                    act.wait_ge(unit_done, U2 + 8 * x)
                for k in range(NH):
                    ins = act.activation(oh[:, k, :], of[:, k, :], ACT.Copy)
                    ins.then_inc(o_hi_set, 1)
                with act.Fori(0, 4) as i:
                    for j in range(2):
                        act.wait_ge(gate_in[j], i * 16 + (64 * x + 16))
                        act.activation(gs[:, j, :], gs[:, j, :], ACT.Sigmoid).then_inc(gate_ready, 1)
            act.wait_ge(unit_done, U2)
            for k in range(KD):
                act.wait_ge(m_seq, 8 + k + 1)
                act.activation(hh[:, k, :], mm_[:, k, :], ACT.Copy).then_inc(m_hi_set, 1)
            act.wait_ge(m_ready, KD)
            for cb in range(KD):
                act.wait_ge(unit_done, U2 + 24 + cb + 1)
                act.activation(v3(mix[:, cb, :]), psg(3 * (cb % 2)), ACT.Copy)
                if cb:
                    act.wait_ge(sq_used, cb)
                act.activation(v3(sq4[:, :]), psg(3 * (cb % 2)), ACT.Square).then_inc(mix_read, 1)

            def rstd(dst, k):
                act.wait_ge(n4_sum, k)
                ins = act.activation(v3(dst), psg(0), ACT.Ln, bias=eps[:, 0:1], scale=1.0 / D)
                ins.then_inc(mix_sq, 1)
                act.wait_ge(mix_sq, k)
                act.activation(dst, dst, ACT.Exp, scale=-0.5).then_inc(n4_rs, 1)

            rstd(sq4[:, :], 1)
            for f in range(KD):
                act.wait_ge(x1_ready, f + 1)
                act.activation(mix[:, f, :], x4[:, f, :], ACT.Square).then_inc(x_squared, 1)
                act.dma_start(dr["x1_d"][f * P:(f + 1) * P, :], x4[:, f, :]).then_inc(x1_stored, 16)
            rstd(sq4[:, :], 2)
            for f in range(KD):
                act.wait_ge(h2_full, f + 1)
                act.activation(hh[:, f, :], mix[:, f, :], ACT.Copy).then_inc(h2_hi, 1)
            act.wait_ge(h2_ready, KD)
            act.wait_ge(x1_stored, 16 * KD)
            with act.Fori(0, FCH) as c:
                for j in range(4):
                    act.wait_ge(unit_done, c * 12 + (U2 + 32 + j + 1))
                    if j >= 2:
                        act.wait_ge(hid_ready, c * 4 + (j - 1))
                    act.activation(v3(hid[:, j % 2, :]), psg(3 * (j % 2)), ACT.Relu).then_inc(hid_relu, 1)
                    act.wait_ge(hid_sq, c * 4 + (j + 1))
                    act.activation(fh[:, j, :], hid[:, j % 2, :], ACT.Copy).then_inc(hid_hi, 1)
            for f in range(KD):
                act.wait_ge(acc_added, 8 * FCH + 2)
                if f:
                    act.wait_ge(fin_ss, f)
                act.activation(sq5[:, :], acc[:, f, :], ACT.Square).then_inc(fin_sq, 1)
            act.wait_ge(fin_ss, KD)
            act.wait_ge(unit_done, U2 + 128)
            act.dma_start(hl[:, :, :].bitcast(F32), dr["x1_d"].rearrange("(k p) t -> p k t", p=P)).then_inc(x5_in, 16)
            rstd(sq5[:, :], 3)

        @block.vector
        def _(dve):
            v3 = lambda ap: ap.rearrange("p (g t) -> p g t", g=G)
            psg = lambda b0: ps[:, b0:b0 + G, 0:GW]
            dve.memset(ones[:, :], 1.0).then_inc(ones_set, 1)
            dve.memset(eps[:, :], EPS).then_inc(ones_set, 1)
            dve.wait_ge(const_in, 32)
            dve.tensor_copy(levm[:, :, :].rearrange("p l t -> p (l t)"), mask_f[:, 0:NL * P])
            dve.tensor_copy(keep[:, :], mask_f[:, NL * P:])
            for f in range(KD):
                dve.wait_ge(x_squared, f + 1)
                if f == 0:
                    dve.tensor_copy(ss1, sq1[:, 0, :]).then_inc(x_summed, 1)
                else:
                    dve.wait_ge(x_summed, f)
                    dve.tensor_tensor(ss1, ss1, sq1[:, f % 2, :], ALU.add).then_inc(x_summed, 1)
            dve.wait_ge(h_rstd, 1)
            for f in range(KD):
                dve.scalar_tensor_tensor(xT[:, f, :], xT[:, f, :], par("g_pre_mix", f), rs1, ALU.mult, ALU.mult)\
                    .then_inc(h_full, 1)
                if f:
                    dve.wait_ge(h_hi_set, f)
                    dve.tensor_tensor(hl[:, f - 1, :], xT[:, f - 1, :], hh[:, f - 1, :].bitcast(F32), ALU.subtract)\
                        .then_inc(h_ready, 1)
            dve.wait_ge(h_hi_set, KD)
            dve.tensor_tensor(hl[:, KD - 1, :], xT[:, KD - 1, :], hh[:, KD - 1, :].bitcast(F32), ALU.subtract)\
                .then_inc(h_ready, 1)

            zb = [A(o, 1024) for o in A_Z]
            lb = [A(o, 1024) for o in A_L]

            def group(p, more):
                ch = Chain(dve, v_seq, p * CHAIN_V)
                dve.tensor_copy(cwp[:, 0:CW], pk[:, bass.ds(p * CW + PK["conv_w"][0], CW)])
                dve.tensor_copy(cwp[:, CW:CW + 1], pk[:, bass.ds(p + PK["conv_b"][0], 1)]).then_inc(now_set.sem, 1)
                dve.tensor_copy(sbp[:, 0:2], pk[:, bass.ds(p * 2 + PK["sb_bias"][0], 2)])
                dve.tensor_copy(sbp[:, 2:3], pk[:, bass.ds(p + PK["sample_bias"][0], 1)]).then_inc(now_set.sem, 1)
                dve.memset(A(A_QPAD, 576), 0.0)
                ch.link(dve.memset(A(A_QFULL, 64), 0.0))
                staged.wait(dve, p, -2)
                for e in range(2):
                    r = slice(DH * e, DH * e + DH)
                    src = qT[r, TP:T].rearrange("p (b q) -> p b q", b=NSEQ)
                    dve.tensor_copy(ar[r, A_QPAD:A_QPAD + 576].rearrange("p (b c) -> p b c", c=72)
                                    [:, :, TS * e:TS * e + TS], src)
                    ins = dve.tensor_copy(ar[r, A_QFULL:A_QFULL + 64].rearrange("p (b c) -> p b c", c=8)
                                          [:, :, TS * e:TS * e + TS], src)
                ins.then_inc(q_pad.sem, 1)
                dve.memset(A(A_U, PAD), 0.0)
                ug_sig.wait(dve, p, 1)
                up, us = A(A_U, PAD + TP), A(A_US, NSEQ * (PAD + TS)).rearrange("p (b t) -> p b t", b=NSEQ)
                dve.tensor_tensor(up[:, PAD:], ua[:, 0:TP], ug[:, 0:TP], ALU.mult)
                prev_in.wait(dve, p, 16)
                dve.tensor_tensor(us[:, :, PAD:], ua[:, TP:T].rearrange("p (b t) -> p b t", b=NSEQ),
                                  ug[:, TP:T].rearrange("p (b t) -> p b t", b=NSEQ), ALU.mult).then_inc(u_ready.sem, 1)
                u_ready.wait(dve, p, 1)
                now_set.wait(dve, p, 2)
                ca = A(A_ACC, TP)
                cs = A(A_ACC + TP, SM).rearrange("p (b t) -> p b t", b=NSEQ)
                taps = [0]

                def tap(last=False):
                    w = taps[0]
                    if w >= CW:
                        return
                    taps[0] += 1
                    if w:
                        ch.wait()
                        ch.mark(dve.scalar_tensor_tensor(ca, up[:, w:w + TP], cwp[:, w:w + 1], ca, ALU.mult, ALU.add))
                        ins = dve.scalar_tensor_tensor(cs, us[:, :, w:w + TS], cwp[:, w:w + 1], cs, ALU.mult, ALU.add)
                    else:
                        ch.mark(dve.tensor_scalar(ca, up[:, 0:TP], cwp[:, 0:1], cwp[:, CW:CW + 1], ALU.mult, ALU.add))
                        ins = dve.tensor_scalar(cs, us[:, :, 0:TS], cwp[:, 0:1], cwp[:, CW:CW + 1], ALU.mult, ALU.add)
                    if w == CW - 1:
                        ins.then_inc(conv_done.sem, 1)
                    else:
                        ch.mark(ins)

                for s in range(17):
                    if s < 16:
                        qb = s // 2
                        n = P * (qb + 1)
                        z, l = zb[s % 3][:, 0:n], lb[s % 2][:, 0:n]
                        z_read.wait(dve, p, s + 1)
                        dg = z[:, qb * P:n]
                        ch.mark(dve.tensor_tensor(dg, dg, neg, ALU.add))
                        tap()
                        ch.wait()
                        dve.tensor_scalar(l, z, ZMAX, None, ALU.min).then_inc(e_ready.sem, 1)
                    if s == 4:
                        zs, ls = A(A_ZS, SBK, slice(0, 64)), A(A_LS, SBK, slice(0, 64))
                        zs_read.wait(dve, p, 1)
                        ch.link(dve.tensor_tensor(zs[:, PAST:], zs[:, PAST:], par("neg_new", 0, SM)[0:64, :], ALU.add))
                        dve.tensor_scalar(ls, zs, ZMAX, None, ALU.min).then_inc(es_ready.sem, 1)
                    tap()
                    if s:
                        n = P * ((s - 1) // 2 + 1)
                        z, l = zb[(s - 1) % 3][:, 0:n], lb[(s - 1) % 2][:, 0:n]
                        ln_ready.wait(dve, p, s)
                        ch.link(dve.tensor_tensor(l, z, l, ALU.max))
                        r = l[:, ::-1]
                        ch.link(dve.tensor_tensor_scan(r, r, r, 0.0, ALU.add, ALU.max))
                        dve.tensor_tensor(z, z, l, ALU.subtract).then_inc(arg_ready.sem, 1)
                    if s == 5:
                        lns_ready.wait(dve, p, 1)
                        ch.link(dve.tensor_tensor(ls, zs, ls, ALU.max))
                        r = ls[:, ::-1]
                        ch.link(dve.tensor_tensor_scan(r, r, r, 0.0, ALU.add, ALU.max))
                        dve.tensor_tensor(zs, zs, ls, ALU.subtract).then_inc(args_ready.sem, 1)
                while taps[0] < CW:
                    tap()

                a_ready.wait(dve, p, 16)
                t_done.wait(dve, p, 16)
                av_done.wait(dve, p, 16)
                os_done.wait(dve, p, 1)
                Bt, Dt, w0, w1 = A(B_B, T), A(B_D, T), A(B_W[0], T), A(B_W[1], T)
                kk, att, qbt = A(B_KK, T), A(B_ATT, T), A(B_QB, T)
                t1_ready.wait(dve, p, 1)
                ch.link(dve.scalar_tensor_tensor(Dt, fT[:, :], 0.0, A(B_T1, T), ALU.min, ALU.subtract))
                dve.tensor_tensor_scan(Bt, keep[:, :], Dt, 0.0, ALU.mult, ALU.add).then_inc(b_ready.sem, 1)
                sig_ready.wait(dve, p, 1)
                dve.tensor_tensor(gA[:, :], gA[:, :], w1, ALU.mult)
                dve.tensor_tensor(qA[:, :], qA[:, :], w0, ALU.mult).then_inc(qk_ready.sem, 1)
                b_ready.wait(dve, p, 1)

                def blocks(ap, size):
                    n = T if size <= TS else TP
                    return ap[:, 0:n].rearrange("p (n c) -> p n c", c=size)

                def diff(j):
                    size = LEVELS[j]
                    half = size // 2
                    bb, dd = blocks(Bt, size), blocks(Dt, size)
                    nb = bb.shape[1]
                    mid = bb[:, :, half - 1:half].broadcast_to([P, nb, half])
                    dve.tensor_tensor(dd[:, :, half:], bb[:, :, half:], mid, ALU.subtract)
                    dve.tensor_tensor(dd[:, :, 0:half], mid, bb[:, :, 0:half], ALU.subtract).then_inc(dsub.sem, 1)

                def merge(idx):
                    if idx:
                        wait_apart(dve, lev_done.at(p, idx + 1), att_read.at(p, idx))
                    else:
                        lev_done.wait(dve, p, idx + 1)
                    j = idx - 1
                    b0 = 3 if idx == 0 or j % 2 else 5
                    src = banks(b0, 1024).rearrange("p (c t) -> p c t", c=CH)
                    dst = att[:, 0:TP].rearrange("p (c t) -> p c t", c=CH)
                    if idx == 0:
                        ch.mark(dve.tensor_tensor(dst, src, ident.unsqueeze(1).broadcast_to([P, CH, P]), ALU.mult))
                        ins = dve.tensor_tensor(att[0:SM, TP:T], ps[0:SM, 7, 0:SM], ident[0:SM, 0:SM], ALU.mult)
                    else:
                        ins = dve.copy_predicated(dst, levm[:, j:j + 1, :].broadcast_to([P, CH, P]), src)
                        if LEVELS[j] <= TS:
                            ch.mark(ins)
                            ins = dve.copy_predicated(att[0:SM, TP:T], levm[0:SM, j, 0:SM], ps[0:SM, 7, 0:SM])
                    ins.then_inc(att_read.sem, 1)

                diff(0)
                va_staged.wait(dve, p, 1)
                dve.tensor_tensor(A(B_T1, NSEQ * P, slice(0, SM)).rearrange("p (b v) -> p b v", b=NSEQ),
                                  A(B_VA + 1024, P, slice(0, SM)).unsqueeze(1).broadcast_to([SM, NSEQ, P]),
                                  par("own_seq", 0, NSEQ)[0:SM, :].unsqueeze(2).broadcast_to([SM, NSEQ, P]),
                                  ALU.mult).then_inc(vm_ready.sem, 1)
                eb_ready.wait(dve, p, 1)
                dve.tensor_copy(ebl[:, 0:CH], qbt[:, 0:TP].rearrange("p (c t) -> p c t", t=P)[:, :, P - 1])
                ch.link(dve.tensor_copy(ebl[:, CH:], qbt[:, TP:T].rearrange("p (c t) -> p c t", t=TS)[:, :, TS - 1]))
                qk_ready.wait(dve, p, 1)
                dve.tensor_tensor(qbt, qbt, qA[:, :], ALU.mult).then_inc(qb_ready.sem, 1)
                merge(0)
                for j in range(NL):
                    size = LEVELS[j]
                    half = size // 2
                    wexp.wait(dve, p, j + 1)
                    if j + 1 < NL:
                        diff(j + 1)
                    else:
                        for (a, n, c) in ((0, TP, P), (TP, SM, TS)):
                            bb = Bt[:, a:a + n].rearrange("p (n c) -> p n c", c=c)
                            ins = dve.tensor_tensor(Dt[:, a:a + n].rearrange("p (n c) -> p n c", c=c),
                                                    bb[:, :, c - 1:c].broadcast_to([P, n // c, c]), bb, ALU.subtract)
                        ins.then_inc(dk_ready.sem, 1)
                    ww, qq, k_ = blocks(A(B_W[j % 2], T), size), blocks(qA, size), blocks(kk, size)
                    dve.tensor_tensor(ww[:, :, half:], ww[:, :, half:], qq[:, :, half:], ALU.mult)
                    dve.tensor_tensor(ww[:, :, 0:half], ww[:, :, 0:half], k_[:, :, 0:half], ALU.mult)\
                        .then_inc(w_ready.sem, 1)
                    if j:
                        merge(j)
                merge(NL)
                dk_exp.wait(dve, p, 1)
                dve.tensor_tensor(A(B_KD, T), A(B_KD, T), kk, ALU.mult).then_inc(kd_ready.sem, 1)
                u_done.wait(dve, p, 1)
                ch.link(dve.tensor_copy(A(B_D, P), banks(5, 1024)[:, 0:P]))
                for c in range(1, CH):
                    ins = dve.scalar_tensor_tensor(A(B_D + c * P, P), A(B_D + (c - 1) * P, P), ebl[:, c:c + 1],
                                                   banks(5, 1024)[:, c * P:(c + 1) * P], ALU.mult, ALU.add)
                    if c < CH - 1:
                        ch.link(ins)
                    else:
                        ins.then_inc(s_ready.sem, 1)
                s0_in.wait(dve, p, 16)
                sn = A(B_W[0], NSEQ * P).rearrange("p (b v) -> p b v", b=NSEQ)
                ch.link(dve.tensor_tensor(sn, A(B_S0, NSEQ * P).rearrange("p (b v) -> p b v", b=NSEQ),
                                          ebl[:, CH:].unsqueeze(2).broadcast_to([P, NSEQ, P]), ALU.mult))
                um_done.wait(dve, p, 1)
                dve.tensor_tensor(A(B_W[0], 1024), A(B_W[0], 1024), banks(3, 1024), ALU.add).then_inc(s0_new.sem, 1)
                rs_ready.wait(dve, p, 1)
                ch.link(dve.scalar_tensor_tensor(A(B_O, T), A(B_O, T), par("a_norm"), A(B_RS, T), ALU.mult, ALU.mult))
                dve.tensor_tensor(A(B_O, T), A(B_O, T), gA[:, :], ALU.mult).then_inc(oa_ready.sem, 1)
                h_stored.wait(dve, p, 48)
                assert ch.n == CHAIN_V, ch.n

            with dve.Fori(0, NH - 1) as p:
                group(p, True)
            group(NH - 1, False)

            n = 0

            def lnk(ins):
                nonlocal n
                n += 1
                ins.then_inc(ln_seq_v, 1)

            dve.wait_ge(of_in, 16)
            lnk(dve.tensor_tensor(tm[:, :], of[:, 0, :], of[:, 1, :], ALU.add))
            for k in (2, 3):
                dve.wait_ge(ln_seq_v, n)
                lnk(dve.tensor_tensor(tm[:, :], tm[:, :], of[:, k, :], ALU.add))
            assert n == LN_V[0]
            dve.wait_ge(ln_seq_a, 3)
            for k in range(NH):
                lnk(dve.tensor_tensor(of[:, k, :], of[:, k, :], gs[:, 0, :], ALU.subtract))
            assert n == LN_CENTER
            dve.wait_ge(ln_seq_a, 7)
            lnk(dve.tensor_tensor(tm[:, :], mm_[:, 0, :], mm_[:, 1, :], ALU.add))
            for k in (2, 3):
                dve.wait_ge(ln_seq_v, n)
                lnk(dve.tensor_tensor(tm[:, :], tm[:, :], mm_[:, k, :], ALU.add))
            assert n == LN_V[1]
            dve.wait_ge(ln_seq_a, 11)
            for k in range(NH):
                lnk(dve.tensor_tensor(of[:, k, :], of[:, k, :], gs[:, 0, :], ALU.mult))
            assert n == LN_SCALED
            dve.wait_ge(ln_seq_a, 19)
            for k in range(NH):
                lnk(dve.tensor_tensor(of[:, k, :], of[:, k, :], mm_[:, k, :], ALU.mult))
            assert n == LN_DONE
            ms = 0
            for x in range(3):
                for k in range(NH):
                    dve.wait_ge(o_hi_set, 4 * x + k + 1)
                    dve.tensor_tensor(ol[:, k, :], of[:, k, :], oh[:, k, :].bitcast(F32), ALU.subtract)\
                        .then_inc(o_ready, 1)
                if x == 0:
                    dve.memset(tm[:, 0:2], 0.0).then_inc(y_free, 2)
                with dve.Fori(0, 4) as i:
                    for j in range(2):
                        dve.wait_ge(unit_done, i * 2 + (U2 + 8 * x + j + 1))
                        dve.wait_ge(gate_ready, i * 2 + (8 * x + j + 1))
                        mt = mm_[:, bass.ds(i * 2 + j, 1), :].rearrange("p a t -> p (a t)")
                        if x == 0:
                            dve.tensor_tensor(v3(mt), psg(3 * j), v3(gs[:, j, :]), ALU.mult).then_inc(y_free, 1)
                        else:
                            dve.tensor_tensor(v3(tm[:, :]), psg(3 * j), v3(gs[:, j, :]), ALU.mult).then_inc(y_free, 1)
                            dve.wait_ge(y_free, i * 2 + (8 * x + j + 3))
                            dve.tensor_tensor(mt, mt, tm[:, :], ALU.add).then_inc(m_seq, 1)
                            dve.wait_ge(m_seq, i * 2 + (8 * (x - 1) + j + 1))
            for k in range(KD):
                dve.wait_ge(m_hi_set, k + 1)
                dve.tensor_tensor(hl[:, k, :], mm_[:, k, :], hh[:, k, :].bitcast(F32), ALU.subtract).then_inc(m_ready, 1)
            for f in range(KD):
                dve.wait_ge(mix_read, f + 1)
                if f == 0:
                    dve.tensor_copy(ss4[:, :], sq4[:, :]).then_inc(sq_used, 1)
                else:
                    dve.wait_ge(sq_used, f)
                    dve.tensor_tensor(ss4[:, :], ss4[:, :], sq4[:, :], ALU.add).then_inc(sq_used, 1)
            dve.wait_ge(n4_rs, 1)
            dve.wait_ge(x4_in, 16)
            xs = 0
            for f in range(KD):
                dve.scalar_tensor_tensor(mix[:, f, :], mix[:, f, :], par("g_post_mix", f), sq4[:, :],
                                         ALU.mult, ALU.mult).then_inc(x1_seq, 1)
                dve.wait_ge(x1_seq, f + 1)
                dve.tensor_tensor(x4[:, f, :], x4[:, f, :], mix[:, f, :], ALU.add).then_inc(x1_ready, 1)
                if f:
                    dve.wait_ge(x_squared, KD + f)
                    if f == 1:
                        dve.tensor_copy(ss4[:, :], mix[:, 0, :]).then_inc(sq_used, 1)
                    else:
                        dve.wait_ge(sq_used, KD + f - 1)
                        dve.tensor_tensor(ss4[:, :], ss4[:, :], mix[:, f - 1, :], ALU.add).then_inc(sq_used, 1)
            dve.wait_ge(x_squared, 2 * KD)
            dve.wait_ge(sq_used, 2 * KD - 1)
            dve.tensor_tensor(ss4[:, :], ss4[:, :], mix[:, KD - 1, :], ALU.add).then_inc(sq_used, 1)
            dve.wait_ge(n4_rs, 2)
            for f in range(KD):
                dve.scalar_tensor_tensor(mix[:, f, :], x4[:, f, :], par("g_pre_ffn", f), sq4[:, :],
                                         ALU.mult, ALU.mult).then_inc(h2_full, 1)
                if f:
                    dve.wait_ge(h2_hi, f)
                    dve.tensor_tensor(hl[:, f - 1, :], mix[:, f - 1, :], hh[:, f - 1, :].bitcast(F32), ALU.subtract)\
                        .then_inc(h2_ready, 1)
            dve.wait_ge(h2_hi, KD)
            dve.tensor_tensor(hl[:, KD - 1, :], mix[:, KD - 1, :], hh[:, KD - 1, :].bitcast(F32), ALU.subtract)\
                .then_inc(h2_ready, 1)
            dve.wait_ge(h2_ready, KD)
            dve.wait_ge(x1_stored, 16 * KD)
            for j in range(2):
                dve.memset(acc[:, 4 * j:4 * j + 4, :], 0.0).then_inc(acc_added, 1)
            with dve.Fori(0, FCH) as c:
                for j in range(4):
                    h = hid[:, j % 2, :]
                    dve.wait_ge(hid_relu, c * 4 + (j + 1))
                    dve.tensor_tensor(h, h, h, ALU.mult).then_inc(hid_sq, 1)
                    dve.wait_ge(hid_hi, c * 4 + (j + 1))
                    dve.tensor_tensor(fl[:, j, :], h, fh[:, j, :].bitcast(F32), ALU.subtract).then_inc(hid_ready, 1)
                for j in range(8):
                    dve.wait_ge(unit_done, c * 12 + (U2 + 36 + j + 1))
                    dve.wait_ge(acc_added, c * 8 + (j + 1))
                    dve.tensor_tensor(v3(acc[:, j, :]), v3(acc[:, j, :]), psg(3 * (j % 2)), ALU.add)\
                        .then_inc(acc_added, 1)
            for f in range(KD):
                dve.wait_ge(fin_sq, f + 1)
                if f == 0:
                    dve.tensor_copy(ss5[:, :], sq5[:, :]).then_inc(fin_ss, 1)
                else:
                    dve.wait_ge(fin_ss, f)
                    dve.tensor_tensor(ss5[:, :], ss5[:, :], sq5[:, :], ALU.add).then_inc(fin_ss, 1)
            dve.wait_ge(n4_rs, 3)
            dve.wait_ge(x5_in, 16)
            for f in range(KD):
                dve.scalar_tensor_tensor(acc[:, f, :], acc[:, f, :], par("g_post_ffn", f), sq5[:, :],
                                         ALU.mult, ALU.mult).then_inc(y_seq, 1)
                dve.wait_ge(y_seq, f + 1)
                dve.tensor_tensor(acc[:, f, :], acc[:, f, :], hl[:, f, :].bitcast(F32), ALU.add).then_inc(y_ready, 1)


BRANCH = (2, 0, 1)
LN_V = (3, 10)
LN_CENTER, LN_SCALED, LN_DONE = 7, 14, 18
CHAIN_V = 127


LN_A = (None, None, 1, 3, 3, 8)

_PARAMS = ("g_pre_mix", "g_post_mix", "g_pre_ffn", "g_post_ffn")


def kernel(**inputs):
    import numpy as np
    import concourse.bacc as _bacc
    from concourse import mybir as _mybir
    from concourse.bass_utils import run_bass_kernel_spmd as _run

    x = {k: np.asarray(v) for k, v in inputs.items()}
    f32 = np.float32

    def cols(v):
        return v.reshape(-1, P).T

    i = np.arange(P)
    ident = np.eye(P, dtype=f32)
    neg = np.where(i[None, :] < i[:, None], 0.0, NEG_BIG).astype(f32)
    levels = [((i[:, None] // s == i[None, :] // s) & (i[:, None] % s < s // 2) & (i[None, :] % s >= s // 2))
              for s in LEVELS]
    keep = np.ones(T, f32)
    keep[0:TP:P] = 0
    keep[TP::TS] = 0
    masks = np.concatenate([np.stack(levels, 1).reshape(P, -1).astype(f32), np.broadcast_to(keep, (P, T))], 1)
    r = np.arange(P)
    key = np.arange(SM)
    neg_new = np.where((r[:, None] // 8 == key[None, :] // TS) & (key[None, :] % TS < r[:, None] % TS), 0.0,
                       NEG_BIG).astype(f32)
    own = (r[:, None] // TS == np.arange(NSEQ)[None, :]).astype(f32)
    bias = x["sb_bias"][0]
    sample_bias = bias.reshape(NH, 2)[:, (r // TS) % 2].T
    conv_w = x["conv_w"][0].T.reshape(NH, P, CW).transpose(1, 0, 2).reshape(P, -1)
    params = np.concatenate(
        [cols(x[n][0]) for n in _PARAMS] + [cols(x["a_norm"][0]), conv_w, cols(x["conv_b"][0]), cols(x["ln_g"][0]),
         cols(x["ln_b"][0]), np.broadcast_to(bias, (P, 2 * NH)), sample_bias, ident, neg, neg_new, own], 1)
    ins = {
        "params": params,
        "masks": masks,
        "pages": x["page_table"].reshape(1, -1),
        "xT": np.concatenate([x["x_prompt"][0], x["x_sample"].reshape(SM, D)], 0).T,
        "kcT": x["cache_k"][0].reshape(-1, P, 8 * DH).transpose(0, 2, 1),
        "vc": x["cache_v"][0].reshape(-1, P, 8 * DH),
        "s_in": x["state_hgrn"][0],
        "conv_prev": x["state_conv"][0].transpose(2, 0, 1),
        "w_in": x["w_in"][0], "w_pa": x["w_pa"][0], "w_pb": x["w_pb"][0], "w_pc": x["w_pc"][0],
        "w_o": x["w_o"][0], "w_ff1": x["w_ff1"][0], "w_ff2": x["w_ff2"][0],
    }
    outs = {
        "yT": (D, T), "k_out": (8 * DH, T), "v_out": (8 * DH, T), "hgrn_p": (NH, P, P), "hgrn_s": (NSEQ, NH, P, P),
        "conv_p": (NH * P, PAD), "conv_s": (NH * P, NSEQ, PAD),
    }
    nc = _bacc.Bacc("TRN2", target_bir_lowering=False, num_devices=1)
    dr, arrays = {}, {}
    for n, a in ins.items():
        a = np.ascontiguousarray(a)
        arrays[f"in_{n}"] = a
        dr[n] = nc.dram_tensor(f"in_{n}", a.shape, _mybir.dt.from_np(a.dtype), kind="ExternalInput").ap()
    for n, shape in outs.items():
        dr[n] = nc.dram_tensor(f"out_{n}", shape, _mybir.dt.float32, kind="ExternalOutput").ap()
    for n, rows in (("oa_d", NH * P), ("ob_d", NH * P), ("c_d", NH * P), ("x1_d", D), ("g_d", NGATE * P)):
        dr[n] = nc.dram_tensor(n, (rows, T), _mybir.dt.float32, kind="Internal").ap()
    build(nc, dr)
    res = _run(nc, [arrays], core_ids=[0]).results[0]
    res = {n: res[f"out_{n}"] for n in outs}
    y = res["yT"].T
    k, v = res["k_out"].T, res["v_out"].T
    heads = (1, 1, TP, 8, DH)
    heads_s = (1, NSEQ, TS, 8, DH)
    return (
        np.ascontiguousarray(y[:TP].reshape(1, TP, D)), np.ascontiguousarray(y[TP:].reshape(NSEQ, TS, D)),
        np.ascontiguousarray(k[:TP]).reshape(heads), np.ascontiguousarray(v[:TP]).reshape(heads),
        res["hgrn_p"].reshape(1, 1, NH, P, P), np.ascontiguousarray(res["conv_p"].T).reshape(1, 1, PAD, NH * P),
        np.ascontiguousarray(k[TP:]).reshape(heads_s), np.ascontiguousarray(v[TP:]).reshape(heads_s),
        res["hgrn_s"].reshape(1, NSEQ, NH, P, P),
        np.ascontiguousarray(res["conv_s"].transpose(1, 2, 0)).reshape(1, NSEQ, PAD, NH * P),
    )
```

```python
from contextlib import ExitStack

import concourse.bass as bass
from concourse import mybir

F32 = mybir.dt.float32
F32R = mybir.dt.float32r
U8 = mybir.dt.uint8
I32 = mybir.dt.int32
ALU = mybir.AluOpType
ACT = mybir.ActivationFunctionType

P = 128
D = 1024
KD = D // P
TP, NSEQ, TS = 1024, 8, 4
T = TP + NSEQ * TS
G = 3
GW = T // G
NH = 4
DH = 64
PAST = 256
NPG = 2
CH = TP // P
SM = NSEQ * TS
CW = 31
PAD = CW - 1
FF = 4096
FCH = FF // (NH * P)
EPS = 1e-6
SBK = PAST + SM
NEG_BIG = -1e30
ZMAX = 40.0

C_QA, C_FA, C_IA, C_GA, C_QB, C_KB, C_VB, C_UA, C_UG, C_GL = (
    0, 512, 1024, 1536, 2048, 2560, 3072, 3584, 4096, 4608)
PRE = 5
A_UNITS, B_UNITS = 8, 6
A_STEPS = (0, 1, 2, 3, 4, 5, 6, 7, 8, 9, 11, 12, 14, 15, 16, 17)
PER = A_UNITS + B_UNITS
GPG = 5
NGATE = 3 * KD
U2 = PRE + PER * NH - 1
V_WO = 3 * KD
V_FF = V_WO + KD
FF1, FF2 = 4, KD
FFU = FF1 + FF2
LEVELS = (128, 64, 32, 16, 8, 4, 2)
NL = len(LEVELS)

PK = {}
_at = 0
for _n, _w in (("g_pre_mix", 8), ("g_post_mix", 8), ("g_pre_ffn", 8), ("g_post_ffn", 8), ("a_norm", 1),
               ("conv_w", NH * CW), ("conv_b", NH), ("ln_g", NH), ("ln_b", NH), ("sb_bias", 2 * NH),
               ("sample_bias", NH), ("ident", P), ("neg", P), ("neg_new", SM), ("own_seq", NSEQ)):
    PK[_n] = (_at, _at + _w)
    _at += _w
NPK = _at

A_Z, A_L, A_AT = (0, 1024, 2048), (3072, 4096), 5120
A_KS, A_VS, A_QPAD, A_QFULL, A_VT, A_ZS, A_LS, A_ATS = 6144, 8192, 10240, 10816, 10880, 12032, 12320, 12608
A_OB, A_U, A_US, A_ACC = 12832, 13888, 14944, 15216
B_T1, B_B, B_D, B_W, B_KK, B_ATT, B_QB, B_KD = 0, 1056, 2112, (3168, 4224), 5280, 6336, 7392, 8448
B_VA, B_KDT, B_S0, B_O, B_OSQ, B_RS = 9504, 10656, 11808, 12832, 13888, 14944
ARENA = A_ACC + T


class Signal:

    def __init__(self, sem, per, before=0):
        self.sem, self.per, self.before = sem, per, before

    def wait(self, eng, p, k):
        eng.wait_ge(*self.at(p, k))

    def at(self, p, k):
        return self.sem, p * self.per + (self.before + k)


class Chain:

    def __init__(self, eng, sem, start=0):
        self.eng, self.sem, self.n, self.start = eng, sem, 0, start

    def mark(self, ins):
        ins.then_inc(self.sem, 1)
        self.n += 1

    def wait(self):
        self.eng.wait_ge(self.sem, self.start + self.n)

    def link(self, ins):
        self.mark(ins)
        self.wait()


def build(nc, dr):
    ctx = ExitStack()
    with ctx:
        def sem(name):
            return ctx.enter_context(nc.semaphore(name))

        def sb(name, shape, dt, stack=ctx):
            return stack.enter_context(nc.sbuf_tensor(name, shape, dt))

        s_h = ExitStack()
        hh = sb("h_hi", [P, KD, T], F32R, s_h)
        hl = sb("h_lo", [P, KD, T], F32R, s_h)
        s_h.close()
        bf = sb("ob_full", [P, NH, T], F32)
        oh = sb("o_hi", [P, NH, T], F32R)
        ol = sb("o_lo", [P, NH, T], F32R)
        ln_sum = sb("ln_sum", [P, T], F32)[:, :]
        ln_stat = sb("ln_stat", [P, T], F32)[:, :]
        sb("h_rest", [P, 2, T], F32)
        raw = sb("w_raw", [P, 2, KD, P], F32)
        wh = sb("w_hi", [P, 2, KD, P], F32R)
        wl = sb("w_lo", [P, 2, KD, P], F32R)
        ones = sb("ones", [P, P], F32)
        pk = sb("params", [P, NPK], F32)
        eps = sb("eps", [P, 1], F32)
        levm = sb("level_masks", [P, NL, P], U8)
        keep = sb("scan_keep", [P, T], U8)
        cwp = sb("conv_w_now", [P, CW + 1], F32)
        sbp = sb("bias_now", [P, 3], F32)
        ebl = sb("chunk_decay", [P, CH + NSEQ], F32)
        pages = sb("pages", [1, NSEQ * NPG], I32)

        s2 = ExitStack()
        kT = sb("kT", [P, T], F32, s2)
        qT = sb("qT", [P, T], F32, s2)
        vT = sb("vT", [P, T], F32, s2)
        fT = sb("fT", [P, T], F32, s2)
        qA = sb("qA", [P, T], F32, s2)
        gA = sb("gA", [P, T], F32, s2)
        iT = sb("iT", [P, T], F32, s2)
        ua = sb("ua", [P, T], F32, s2)
        ug = sb("ug", [P, T], F32, s2)
        ar = sb("arena", [P, ARENA], F32, s2)
        gl = sb("gate_logits", [P, 2, T], F32, s2)
        tw = sb("tapped", [P, TS, NSEQ, CW], F32, s2)
        s2.close()

        s3 = ExitStack()
        of = sb("oa_full", [P, NH, T], F32, s3)
        cf = sb("conv_full", [P, NH, T], F32, s3)
        csq = sb("conv_squares", [P, NH, T], F32, s3)
        mm_ = sb("mixed", [P, KD, T], F32, s3)
        gs = sb("gates", [P, 2, T], F32, s3)
        tm = sb("gated", [P, T], F32, s3)
        s3.close()

        s4 = ExitStack()
        x4 = sb("x_again", [P, KD, T], F32, s4)
        sb("gap4", [P, NH, T], F32, s4)
        mix = sb("mix", [P, KD, T], F32, s4)
        sq4 = sb("sq4", [P, T], F32, s4)
        ss4 = sb("ss4", [P, T], F32, s4)
        s4.close()

        s5 = ExitStack()
        fh = sb("hid_hi", [P, NH, T], F32R, s5)
        fl = sb("hid_lo", [P, NH, T], F32R, s5)
        hid = sb("hid", [P, 2, T], F32, s5)
        sb("gap5", [P, 2, T], F32, s5)
        acc = sb("ff_sum", [P, KD, T], F32, s5)
        sq5 = sb("sq5", [P, T], F32, s5)
        ss5 = sb("ss5", [P, T], F32, s5)
        s5.close()

        ps = ctx.enter_context(nc.psum_tensor("psum", [P, 8, 512], F32))
        flat = ps[:, :, :].rearrange("p b n -> p (b n)")

        def banks(b, n):
            return flat[:, 512 * b:512 * b + n]

        def A(off, n, rows=slice(0, P)):
            return ar[rows, off:off + n]

        def par(name, j=0, n=1):
            a = PK[name][0] + j
            return pk[:, a:a + n]

        ident = par("ident", 0, P)
        neg = par("neg", 0, P)
        xT = A(0, KD * T).rearrange("p (k t) -> p k t", k=KD)
        sq1 = A(KD * T, 2 * T).rearrange("p (k t) -> p k t", k=2)
        rs1 = A((KD + 3) * T, T)
        mask_f = A((KD + 4) * T, NL * P + T)

        S = lambda name, per=0, before=0: Signal(sem(name), per, before)
        const_in = sem("const_in")
        pages_in = sem("pages_in")
        x_in = [sem(f"x_in{f}") for f in range(KD)]
        ones_set = sem("ones_set")
        x_squared = sem("x_squared")
        x_summed = sem("x_summed")
        h_rstd = sem("h_rstd")
        h_full = sem("h_full")
        h_hi_set = sem("h_hi_set")
        h_ready = sem("h_ready")

        w_landed = [sem(f"w_landed{s}") for s in range(2)]
        w_hi_set = sem("w_hi_set")
        w_split = sem("w_split")
        unit_done = sem("unit_done")
        staged = S("unit_staged", PER, PRE)

        v_turned, v_staged = S("v_turned", 1), S("v_staged", 1)
        now_set = S("params_now", 2)
        q_pad = S("q_pad", 1)
        ug_sig = S("ug_sig", 1)
        u_ready = S("u_ready", 1)
        conv_done, taps_s = S("conv_done", 1), S("sample_taps", 1)
        prev_in = S("conv_prev_in", 16)
        ks_in = S("cache_in", 32 * NSEQ * NPG)
        z_ready, z_read = S("z_ready", 16), S("z_read", 16)
        e_ready = S("z_clipped", 16)
        exp1 = S("exp_done", 16)
        ln_ready = S("softplus_log", 16)
        arg_ready = S("arg_ready", 16)
        a_ready = S("a_ready", 16)
        t_done, at_ready = S("a_turned", 16), S("at_staged", 16)
        av_done = S("av_done", 16)
        o_read = S("ob_read", 8)
        zs_ready, zs_read = S("zs_ready", 1), S("zs_read", 1)
        es_ready, lns_ready = S("zs_clipped", 1), S("s_softplus", 1)
        args_ready, as_ready = S("args_ready", 1), S("as_ready", 1)
        ts_done, ats_ready = S("as_turned", 1), S("ats_staged", 1)
        os_done, os_read = S("os_done", 1), S("os_read", 1)
        kv_stored = S("kv_stored", 32)
        conv_stored = S("conv_stored", 48)
        ob_stored = S("ob_stored", 16)

        t1_ready = S("f_log", 1)
        sig_ready = S("sigmoids", 1)
        ia_turned, va_staged = S("ia_turned", 1), S("va_staged", 1)
        b_ready, eb_ready, qb_ready = S("decay_sum", 1), S("decay_exp", 1), S("q_decayed", 1)
        qk_ready = S("q_gated", 1)
        vm_ready = S("v_masked", 1)
        dsub, wexp, w_ready = S("level_diff", NL), S("level_exp", NL), S("level_qk", NL)
        lev_done, att_read = S("level_product", NL + 1), S("level_merged", NL + 1)
        dk_ready, dk_exp, kd_ready = S("k_diff", 1), S("k_exp", 1), S("k_decayed", 1)
        kd_turned, kdt_staged = S("kd_turned", 1), S("kdt_staged", 1)
        s0_in = S("state_in", 16)
        u_done, s_ready = S("chunk_update", 1), S("states_ready", 1)
        um_done, s0_new = S("sample_update", 1), S("sample_state", 1)
        o_done, osq_ready = S("oa_product", 1), S("oa_squared", 1)
        n_done, n_read, rs_ready = S("oa_norm_sum", 1), S("oa_norm_read", 1), S("oa_rstd", 1)
        oa_ready = S("oa_ready", 1)
        h_stored = S("hgrn_stored", 32)
        oa_stored = S("oa_stored", 16, 1)
        gl_stored = [S("gate_stored0", 16 * ((GPG + 1) // 2)), S("gate_stored1", 16 * (GPG // 2))]

        v_seq, a_seq = sem("vector_chain"), sem("scalar_chain")

        of_in = [sem(n) for n in ("ob_in", "oa_in", "conv_in")]
        ln_seq_v, ln_seq_a, ln_pe = sem("ln_vector"), sem("ln_scalar"), sem("ln_sums")
        o_hi_set, o_ready = sem("o_hi_set"), sem("o_split")
        y_free, gate_in = sem("y_read"), [sem(f"gate_in{j}") for j in range(2)]
        gate_ready, m_seq = sem("gate_ready"), sem("mixed_chain")
        m_hi_set, m_ready = sem("m_hi_set"), sem("m_split")
        x4_in = sem("x_again_in")
        mix_read, mix_sq, sq_used = sem("mix_read"), sem("mix_squared"), sem("square_added")
        n4_sum, n4_rs = sem("norm_sum"), sem("norm_rstd")
        x1_seq = sem("x1_chain")
        x1_stored = sem("x1_stored")
        x1_ready = [sem("x1_ready_even"), sem("x1_ready_odd")]
        h2_full, h2_hi = sem("h2_full"), sem("h2_hi")
        h2_ready = [sem("h2_split_even"), sem("h2_split_odd")]
        hid_relu, hid_sq, hid_hi, hid_ready = sem("hid_relu"), sem("hid_squared"), sem("hid_hi_set"), sem("hid_split")
        acc_added = sem("ff_added")
        y_seq, y_ready, y_stored = sem("y_chain"), [sem("y_ready_even"), sem("y_ready_odd")], sem("y_stored")
        x5_in = sem("x1_in")
        fin_sq, fin_ss = sem("ff_squared"), sem("ff_square_added")

        block = ctx.enter_context(nc.Block())


        def wait_apart(eng, *waits):
            waits = [(s, v if isinstance(v, int) else nc.snap(v)) for s, v in waits]
            eng.wait_ge(ones_set, 1)
            for s, v in waits:
                eng.wait_ge(s, v)

        w_in = dr["w_in"].rearrange("(k p) n -> p k n", p=P)
        w_p = [dr[n].rearrange("(k p) n -> p k n", p=P) for n in ("w_pa", "w_pb", "w_pc")]
        w_o = dr["w_o"].rearrange("(k p) n -> p k n", p=P)
        w_f1 = dr["w_ff1"].rearrange("(k p) n -> p k n", p=P)
        w_f2 = dr["w_ff2"].rearrange("(c k p) n -> c p k n", k=NH, p=P)
        A_COLS = (C_FA, None, C_QA, None, C_IA, None, C_GA, None)
        B_COLS = (C_KB, C_VB, C_QB, C_UA, C_UG, None)

        def gate_of(jj, more):
            if jj < A_UNITS:
                return jj // 2 if A_COLS[jj] is None else None
            if not more:
                return 4 + jj - A_UNITS
            return 4 if B_COLS[jj - A_UNITS] is None else None

        def cols_of(jj, p, more):
            g = gate_of(jj, more)
            if g is not None:
                return p * (GPG * P) + (g * P + C_GL)
            return p * P + (A_COLS[jj] if jj < A_UNITS else B_COLS[jj - A_UNITS] + P)

        def units(more):
            return PER if more else PER - 1

        def load_unit2(sp, u, p, cols):
            s, n = u % 2, u // 2
            if u >= 2:
                wait_apart(sp, (w_split, p * PER + (u - 1)))
            sp.dma_start(raw[:, s, :, :], w_in[:, :, bass.ds(cols, P)]).then_inc(w_landed[s], 16)

        def split_unit2(pool, u, p):
            s, n = u % 2, u // 2
            over = [(unit_done, p * PER + (u - 1))] if u >= 2 else []
            wait_apart(pool, (w_landed[s], p * (8 * PER) + 16 * (n + 1)), *over)
            pool.tensor_copy(wh[:, s, :, :], raw[:, s, :, :]).then_inc(w_hi_set, 1)
            pool.wait_ge(w_hi_set, p * PER + (u + 1))
            pool.tensor_tensor(wl[:, s, :, :], raw[:, s, :, :], wh[:, s, :, :].bitcast(F32),
                               ALU.subtract).then_inc(w_split, 1)

        def load_unit3(sp, v, slot, src, kt):
            wait_apart(sp, (w_split, v + (U2 - 1)))
            sp.dma_start(raw[:, slot, 0:kt, :], src).then_inc(w_landed[slot], 16)

        def split_unit3(pool, v, slot, use, kt):
            wait_apart(pool, (w_landed[slot], (use + (U2 // 2 + 1)) * 16), (unit_done, v + (U2 - 1)))
            pool.tensor_copy(wh[:, slot, 0:kt, :], raw[:, slot, 0:kt, :]).then_inc(w_hi_set, 1)
            pool.wait_ge(w_hi_set, v + (U2 + 1))
            pool.tensor_tensor(wl[:, slot, 0:kt, :], raw[:, slot, 0:kt, :], wh[:, slot, 0:kt, :].bitcast(F32),
                               ALU.subtract).then_inc(w_split, 1)

        def product(pe, slot, ks, kt, xh, xl, b0):
            for k in ks:
                for w, x in ((wh, xh), (wh, xl), (wl, xh)):
                    for g in range(G):
                        mm = pe.matmul(ps[:, b0 + g, 0:GW], w[:, slot, k, :], x[:, k, g * GW:(g + 1) * GW],
                                       start=(k == 0 and w is wh and x is xh), stop=(k == kt - 1 and w is wl))
            return mm

        @block.sync
        def _(sp):
            for f in range(KD):
                sp.dma_start(xT[:, f, :], dr["xT"][f * P:(f + 1) * P, :]).then_inc(x_in[f], 16)
            sp.dma_start(pk[:, :], dr["params"]).then_inc(const_in, 16)
            sp.dma_start(mask_f, dr["masks"]).then_inc(const_in, 16)
            sp.dma_start(pages[:, :], dr["pages"]).then_inc(pages_in, 16)
            for u in range(PRE):
                load_unit2(sp, u, 0, B_COLS[u])
            for jj in range(3):
                load_unit2(sp, PRE + jj, 0, cols_of(jj, 0, True))
            sp.wait_ge(pages_in, 16)
            page = [sp.value_load(pages[0:1, i:i + 1], min_val=0, max_val=dr["kcT"].shape[0] - 1)
                    for i in range(NSEQ * NPG)]
            sp.wait_ge(h_ready, KD)
            ksv = A(A_KS, 2048).rearrange("p (b g n) -> p b g n", b=NSEQ, g=NPG)
            vsv = A(A_VS, 2048).rearrange("p (b g n) -> p b g n", b=NSEQ, g=NPG)

            def branch_weights(x, i, j):
                load_unit3(sp, i * 2 + (8 * x + j), j, w_p[BRANCH[x]][:, :, bass.ds(i * (2 * P) + j * P, P)], NH)

            def branch_gate(x, i, j):
                wait_apart(sp, (y_free, i * 2 + (8 * x + j + 1)))
                sp.dma_start(gs[:, j, :], dr["g_d"][bass.ds(i * (2 * P) + (BRANCH[x] * D + j * P), P), :])\
                    .then_inc(gate_in[j], 16)

            def group(p, more):
                sp.dma_start(A(A_US, NSEQ * (PAD + TS)).rearrange("p (b t) -> p b t", b=NSEQ)[:, :, 0:PAD],
                             dr["conv_prev"][bass.ds(p * P, P), :, :]).then_inc(prev_in.sem, 16)
                for i in range(NSEQ * NPG):
                    b, g = divmod(i, NPG)
                    sp.dma_start(ksv[:, b, g, :], dr["kcT"][bass.ds(page[i], 1), bass.ds(p * P, P), :]
                                 .rearrange("a d t -> (a d) t")).then_inc(ks_in.sem, 16)
                    sp.dma_start(vsv[:, b, g, :], dr["vc"][bass.ds(page[i], 1), :, bass.ds(p * P, P)]
                                 .rearrange("a t d -> (a t) d")).then_inc(ks_in.sem, 16)
                load = lambda jj: load_unit2(sp, PRE + jj, p, cols_of(jj, p, more))
                following = lambda jj: load_unit2(sp, PRE + PER + jj, p, cols_of(jj, p + 1, True)) if more else None

                def store_gate(jj):
                    g = gate_of(jj, more)
                    wait_apart(sp, staged.at(p, jj + 1))
                    sp.dma_start(dr["g_d"][bass.ds(p * (GPG * P) + g * P, P), :], gl[:, g % 2, :])\
                        .then_inc(gl_stored[g % 2].sem, 16)

                load(3)
                wait_apart(sp, staged.at(p, -3))
                sp.dma_start(dr["k_out"][bass.ds(p * P, P), :], kT[:, :]).then_inc(kv_stored.sem, 16)
                sp.dma_start(dr["v_out"][bass.ds(p * P, P), :], vT[:, :]).then_inc(kv_stored.sem, 16)
                load(4)
                store_gate(1)
                load(5)
                load(6)
                store_gate(3)
                load(7)
                load(8)
                store_gate(5)
                load(9)
                load(10)
                store_gate(7)
                wait_apart(sp, conv_done.at(p, 1))
                sp.dma_start(dr["c_d"][bass.ds(p * P, P), :], A(A_ACC, T)).then_inc(conv_stored.sem, 16)
                sp.dma_start(dr["conv_p"][bass.ds(p * P, P), :],
                             A(A_U + TP, PAD)).then_inc(conv_stored.sem, 16)
                sp.dma_start(dr["conv_s"][bass.ds(p * P, P), :, :],
                             A(A_US, NSEQ * (PAD + TS)).rearrange("p (b t) -> p b t", b=NSEQ)[:, :, TS:])\
                    .then_inc(conv_stored.sem, 16)
                wait_apart(sp, av_done.at(p, 16))
                wait_apart(sp, os_done.at(p, 1))
                sp.dma_start(A(B_S0, NSEQ * P).rearrange("p (b v) -> p b v", b=NSEQ),
                             dr["s_in"][:, bass.ds(p, 1), :, :].rearrange("b a d v -> d (b a) v"))\
                    .then_inc(s0_in.sem, 16)
                wait_apart(sp, o_read.at(p, 8))
                wait_apart(sp, os_read.at(p, 1))
                sp.dma_start(dr["ob_d"][bass.ds(p * P, P), :], A(A_OB, T)).then_inc(ob_stored.sem, 16)
                load(11)
                if not more:
                    store_gate(8)
                load(12)
                if more:
                    load(13)
                else:
                    for jj in (9, 10, 11):
                        store_gate(jj)
                following(0)
                if not more:
                    branch_weights(0, 0, 0)
                    branch_weights(0, 0, 1)
                wait_apart(sp, s_ready.at(p, 1))
                sp.dma_start(dr["hgrn_p"][bass.ds(p, 1), :, :].rearrange("a d v -> (a d) v"),
                             A(B_D + 7 * P, P)).then_inc(h_stored.sem, 16)
                following(1)
                wait_apart(sp, s0_new.at(p, 1))
                sp.dma_start(dr["hgrn_s"][:, bass.ds(p, 1), :, :].rearrange("b a d v -> d (b a) v"),
                             A(B_W[0], NSEQ * P).rearrange("p (b v) -> p b v", b=NSEQ)).then_inc(h_stored.sem, 16)
                following(2)
                if not more:
                    store_gate(12)
                    ob_stored.wait(sp, NH - 1, 16)
                    sp.wait_ge(unit_done, U2)
                    sp.dma_start(bf[:, :, :], dr["ob_d"].rearrange("(k p) t -> p k t", p=P)).then_inc(of_in[0], 16)
                wait_apart(sp, oa_ready.at(p, 1))
                sp.dma_start(dr["oa_d"][bass.ds(p * P, P), :], A(B_O, T)).then_inc(oa_stored.sem, 16)
                if more:
                    store_gate(13)

            with sp.Fori(0, NH - 1) as p:
                group(p, True)
            group(NH - 1, False)

            h_stored.wait(sp, NH - 1, 32)
            oa_stored.wait(sp, NH - 1, 16)
            conv_stored.wait(sp, NH - 1, 48)
            kv_stored.wait(sp, NH - 1, 32)
            for b in range(2):
                gl_stored[b].wait(sp, NH - 1, 16 * ((NGATE - GPG * (NH - 1) - b + 1) // 2))
            branch_gate(0, 0, 0)
            branch_gate(0, 0, 1)
            branch_weights(0, 1, 0)
            sp.dma_start(cf[:, :, :], dr["c_d"].rearrange("(k p) t -> p k t", p=P)).then_inc(of_in[2], 16)
            branch_weights(0, 1, 1)
            branch_gate(0, 1, 0)
            branch_gate(0, 1, 1)
            sp.dma_start(of[:, :, :], dr["oa_d"].rearrange("(k p) t -> p k t", p=P)).then_inc(of_in[1], 16)
            for x in range(3):
                with sp.Fori(0 if x else 2, 4) as i:
                    for j in range(2):
                        branch_weights(x, i, j)
                        branch_gate(x, i, j)
            with sp.Fori(0, 4) as i:
                for j in range(2):
                    load_unit3(sp, i * 2 + (V_WO + j), j, w_o[:, :, bass.ds(i * 2 * P + j * P, P)], KD)
            sp.wait_ge(o_ready, 12)
            sp.wait_ge(unit_done, U2 + V_WO)
            sp.dma_start(x4[:, :, :], dr["xT"].rearrange("(k p) t -> p k t", p=P)).then_inc(x4_in, 16)
            with sp.Fori(0, FCH) as c:
                for j in range(4):
                    load_unit3(sp, c * FFU + (V_FF + j), j % 2, w_f1[:, :, bass.ds(c * 4 * P + j * P, P)], KD)
                for j in range(8):
                    load_unit3(sp, c * FFU + (V_FF + FF1 + j), j % 2,
                               w_f2[bass.ds(c, 1), :, :, j * P:(j + 1) * P].rearrange("c p k n -> (c p) k n"), NH)
            for f in range(KD):
                sp.wait_ge(y_ready[f % 2], f // 2 + 1)
                sp.dma_start(dr["yT"][f * P:(f + 1) * P, :], acc[:, f, :]).then_inc(y_stored, 16)
            sp.wait_ge(y_stored, 16 * KD)

        @block.gpsimd
        def _(pool):
            us = A(A_US, NSEQ * (PAD + TS)).rearrange("p (b t) -> p b t", b=NSEQ)

            def group(p, more):
                for jj in range(units(more)):
                    split_unit2(pool, PRE + jj, p)
                    if jj == 3:
                        wait_apart(pool, u_ready.at(p, 1))
                        for t in range(TS):
                            ins = pool.tensor_tensor(tw[:, t, :, :], us[:, :, t:t + CW],
                                                     cwp[:, 0:CW].unsqueeze(1).broadcast_to([P, NSEQ, CW]), ALU.mult)
                        ins.then_inc(taps_s.sem, 1)

            for u in range(PRE):
                split_unit2(pool, u, 0)
            with pool.Fori(0, NH - 1) as p:
                group(p, True)
            group(NH - 1, False)
            with pool.Fori(0, V_WO // 2) as n:
                split_unit3(pool, n * 2, 0, n, NH)
                split_unit3(pool, n * 2 + 1, 1, n, NH)
            with pool.Fori(V_WO // 2, V_FF // 2) as n:
                split_unit3(pool, n * 2, 0, n, KD)
                split_unit3(pool, n * 2 + 1, 1, n, KD)
            def split_ff(c, js):
                for j in js:
                    split_unit3(pool, c * FFU + (V_FF + j), j % 2, c * (FFU // 2) + (V_FF // 2 + j // 2), KD if j < 4 else NH)

            split_ff(0, (0, 1))
            for f in range(1, KD, 2):
                pool.wait_ge(x1_seq, f + 1)
                pool.tensor_tensor(x4[:, f, :], x4[:, f, :], mix[:, f, :], ALU.add).then_inc(x1_ready[1], 1)
            for f in range(1, KD, 2):
                pool.wait_ge(h2_hi, f + 1)
                pool.tensor_tensor(hl[:, f, :], mix[:, f, :], hh[:, f, :].bitcast(F32), ALU.subtract)\
                    .then_inc(h2_ready[1], 1)
            split_ff(0, range(2, FFU))
            with pool.Fori(1, FCH) as c:
                split_ff(c, range(FFU))
            pool.wait_ge(x5_in, 16)
            for f in range(1, KD, 2):
                pool.wait_ge(y_seq, f + 1)
                pool.tensor_tensor(acc[:, f, :], acc[:, f, :], hl[:, f, :].bitcast(F32), ALU.add)\
                    .then_inc(y_ready[1], 1)

        @block.tensor
        def _(pe):
            def unit_part(u, p, ks):
                if 0 in ks:
                    pe.wait_ge(w_split, p * PER + (u + 1))
                    if u:
                        pe.wait_ge(staged.sem, p * PER + u)
                mm = product(pe, u % 2, ks, KD, hh, hl, 0)
                if KD - 1 in ks:
                    mm.then_inc(unit_done, 1)

            def square_sum(sq, b0, f):
                for g in range(G):
                    mm = pe.matmul(ps[:, b0 + g, 0:GW], ones[:, :], sq[:, g * GW:(g + 1) * GW],
                                   start=(f == 0), stop=(f == KD - 1))
                return mm

            pe.wait_ge(ones_set, 2)
            for f in range(KD):
                pe.wait_ge(x_squared, f + 1)
                square_sum(sq1[:, f % 2, :], 3, f).then_inc(x_summed, 1)
            for k in range(KD):
                pe.wait_ge(h_ready, k + 1)
                unit_part(0, 0, (k,))
            for u in range(1, PRE):
                unit_part(u, 0, range(KD))

            zb = [A(o, 1024) for o in A_Z]
            atv = A(A_AT, 1024)
            vtok = A(A_VT, 9 * P).rearrange("p (n d) -> p n d", n=9)
            ksv = A(A_KS, 2048).rearrange("p (b n) -> p b n", b=NSEQ)
            vsv = A(A_VS, 2048).rearrange("p (b g n) -> p b g n", b=NSEQ, g=NPG)
            ats = A(A_ATS, 192).rearrange("p (g n) -> p g n", g=3)

            def scores(p, i):
                qb, e = divmod(i, 2)
                rows = slice(DH * e, DH * e + DH)
                if i:
                    z_read.wait(pe, p, i)
                if i == 8:
                    zs_read.wait(pe, p, 1)
                nk = P * (qb + 1)
                for a in range(0, nk, 512):
                    n = min(512, nk - a)
                    mm = pe.matmul(ps[:, 3 + a // 512, 0:n], qT[rows, qb * P:(qb + 1) * P], kT[rows, a:a + n],
                                   start=True, stop=True)
                mm.then_inc(z_ready.sem, 1)

            def turn_a(p, i):
                a_ready.wait(pe, p, i + 1)
                if i:
                    at_ready.wait(pe, p, i)
                if i == 8:
                    os_read.wait(pe, p, 1)
                for kb in range(i // 2 + 1):
                    mm = pe.transpose(banks(5, 1024)[:, kb * P:(kb + 1) * P], zb[i % 3][:, kb * P:(kb + 1) * P], ident)
                mm.then_inc(t_done.sem, 1)

            def values(p, i):
                qb, e = divmod(i, 2)
                at_ready.wait(pe, p, i + 1)
                if e == 0 and qb:
                    o_read.wait(pe, p, qb)
                for kb in range(qb + 1):
                    mm = pe.matmul(ps[DH * e:DH * e + DH, 7, (qb % 4) * P:(qb % 4 + 1) * P],
                                   vtok[:, kb, DH * e:DH * e + DH], atv[:, kb * P:(kb + 1) * P],
                                   start=(kb == 0), stop=(kb == qb))
                mm.then_inc(av_done.sem, 1)

            def sample_scores(p):
                ks_in.wait(pe, p, 32 * NSEQ * NPG)
                q_pad.wait(pe, p, 1)
                for b in range(NSEQ):
                    pe.matmul(ps[0:64, 4, 0:PAST], A(A_QPAD + 64 * b, 64), ksv[:, b, :],
                              start=(b == 0), stop=(b == NSEQ - 1))
                pe.matmul(ps[0:64, 4, PAST:SBK], A(A_QFULL, 64), kT[:, TP:T], start=True, stop=True)\
                    .then_inc(zs_ready.sem, 1)

            def sample_turn(p):
                wait_apart(pe, as_ready.at(p, 1))
                for j in range(2):
                    pe.transpose(ps[:, 6, 64 * j:64 * j + 64], A(A_ZS + P * j, P, slice(0, 64)), ident[0:64, 0:64])
                pe.transpose(ps[0:SM, 6, 128:192], A(A_ZS + PAST, SM, slice(0, 64)), ident[0:64, 0:64])\
                    .then_inc(ts_done.sem, 1)

            def sample_values(p):
                ats_ready.wait(pe, p, 1)
                pe.matmul(ps[:, 6, 256:320], vtok[0:SM, 8, :], ats[0:SM, 2, :], start=True, stop=False,
                          skip_group_check=True)
                for b in range(NSEQ):
                    for g in range(NPG):
                        mm = pe.matmul(ps[:, 6, 256 + 8 * b:264 + 8 * b], vsv[:, b, g, :], ats[:, g, 8 * b:8 * b + 8],
                                       start=False, stop=(b == NSEQ - 1 and g == NPG - 1), skip_group_check=True)
                mm.then_inc(os_done.sem, 1)

            wb = [A(o, T) for o in B_W]
            kk, att, qbt, kd = A(B_KK, T), A(B_ATT, T), A(B_QB, T), A(B_KD, T)
            va = A(B_VA, 9 * P).rearrange("p (n d) -> p n d", n=9)
            kdt = A(B_KDT, 9 * P).rearrange("p (n d) -> p n d", n=9)
            s0 = A(B_S0, NSEQ * P).rearrange("p (b v) -> p b v", b=NSEQ)

            def turn9(src, b0):
                for c in range(CH):
                    pe.transpose(banks(b0, 1024)[:, c * P:(c + 1) * P], src[:, c * P:(c + 1) * P], ident)
                return pe.transpose(ps[0:SM, 7, 0:P], src[:, TP:T], ident)

            def level_product(p, idx, left, right, b0, sample):
                for c in range(CH):
                    mm = pe.matmul(banks(b0, 1024)[:, c * P:(c + 1) * P], left[:, c * P:(c + 1) * P],
                                   right[:, c * P:(c + 1) * P], start=True, stop=True)
                if sample:
                    mm = pe.matmul(ps[0:SM, 7, 0:SM], left[:, TP:T], right[:, TP:T], start=True, stop=True)
                mm.then_inc(lev_done.sem, 1)

            def group(p, more):
                def half(jj, h):
                    if jj < units(more):
                        unit_part(PRE + jj, p, range(4 * h, 4 * h + 4))

                def half_b(s):
                    half(A_UNITS + s // 2, s % 2)

                staged.wait(pe, p, -2)
                turn9(vT, 5).then_inc(v_turned.sem, 1)
                for s in range(19):
                    if s < 16:
                        scores(p, s)
                    if s in A_STEPS:
                        half(A_STEPS.index(s) // 2, A_STEPS.index(s) % 2)
                    if s == 3:
                        v_staged.wait(pe, p, 1)
                    if s >= 3:
                        values(p, s - 3)
                    if s == 2:
                        v_staged.wait(pe, p, 1)
                    if 2 <= s < 18:
                        turn_a(p, s - 2)
                    if s == 3:
                        sample_scores(p)
                    if s == 7:
                        sample_turn(p)
                    if s == 9:
                        sample_values(p)
                staged.wait(pe, p, 3)
                at_ready.wait(pe, p, 16)
                o_read.wait(pe, p, 8)
                turn9(iT, 5).then_inc(ia_turned.sem, 1)
                half_b(0)
                qk_ready.wait(pe, p, 1)
                va_staged.wait(pe, p, 1)
                level_product(p, 0, kk, qA, 3, True)
                half_b(1)
                for j in range(NL):
                    w_ready.wait(pe, p, j + 1)
                    sample = LEVELS[j] <= TS
                    att_read.wait(pe, p, j + (1 if sample else 0) if j else 1)
                    level_product(p, j + 1, wb[j % 2], wb[j % 2], 5 if j % 2 == 0 else 3, sample)
                    if j < 5:
                        half_b(2 + j)
                half_b(7)
                kd_ready.wait(pe, p, 1)
                att_read.wait(pe, p, NL + 1)
                turn9(kd, 3).then_inc(kd_turned.sem, 1)
                half_b(8)
                kdt_staged.wait(pe, p, 1)
                for c in range(CH):
                    mm = pe.matmul(banks(5, 1024)[:, c * P:(c + 1) * P], kdt[:, c, :], va[:, c, :],
                                   start=True, stop=True)
                mm.then_inc(u_done.sem, 1)
                vm_ready.wait(pe, p, 1)
                for j in range(2):
                    mm = pe.matmul(ps[:, 3 + j, :], kdt[0:SM, 8, :], A(B_T1 + 512 * j, 512, slice(0, SM)),
                                   start=True, stop=True)
                mm.then_inc(um_done.sem, 1)
                half_b(9)
                s_ready.wait(pe, p, 1)
                qb_ready.wait(pe, p, 1)
                s0_in.wait(pe, p, 16)
                for c in range(CH):
                    o = banks(5, 1024)[:, c * P:(c + 1) * P]
                    pe.matmul(o, va[:, c, :], att[:, c * P:(c + 1) * P], start=True, stop=(c == 0))
                    if c:
                        pe.matmul(o, A(B_D + (c - 1) * P, P), qbt[:, c * P:(c + 1) * P], start=False, stop=True)
                pe.matmul(ps[:, 7, 0:SM], va[0:SM, 8, :], att[0:SM, TP:T], start=True, stop=False,
                          skip_group_check=True)
                for b in range(NSEQ):
                    mm = pe.matmul(ps[:, 7, TS * b:TS * b + TS], s0[:, b, :], qbt[:, TP + TS * b:TP + TS * b + TS],
                                   start=False, stop=(b == NSEQ - 1), skip_group_check=True)
                mm.then_inc(o_done.sem, 1)
                half_b(10)
                osq_ready.wait(pe, p, 1)
                s0_new.wait(pe, p, 1)
                for a, n in ((0, 512), (512, 512), (1024, 32)):
                    mm = pe.matmul(banks(3, T)[:, a:a + n], ones[:, :], A(B_OSQ + a, n), start=True, stop=True)
                mm.then_inc(n_done.sem, 1)
                half_b(11)
                n_read.wait(pe, p, 1)

            with pe.Fori(0, NH - 1) as p:
                group(p, True)
            group(NH - 1, False)

            def ln_sums(r):
                pe.wait_ge(ln_seq_v, LN_V[r])
                for g in range(G):
                    if LN_A[r][g]:
                        pe.wait_ge(ln_seq_a, LN_A[r][g])
                    pe.matmul(ps[:, 6 + (r * G + g) % 2, 0:GW], ones[:, :], ln_sum[:, g * GW:(g + 1) * GW],
                              start=True, stop=True).then_inc(ln_pe, 1)

            def branch_units(x, i):
                for j in range(2):
                    pe.wait_ge(w_split, i * 2 + (U2 + 8 * x + j + 1))
                    pe.wait_ge(y_free, i * 2 + (8 * x + j + 1))
                    for k in range(NH):
                        if j == 0:
                            pe.wait_ge(o_ready, 4 * x + k + 1)
                        mm = product(pe, j, (k,), NH, oh, ol, 3 * j)
                    mm.then_inc(unit_done, 1)

            pe.wait_ge(staged.sem, U2)
            with pe.Fori(0, 2) as i:
                branch_units(0, i)
            ln_sums(0)
            with pe.Fori(2, 4) as i:
                branch_units(0, i)
            branch_units(1, 0)
            ln_sums(1)
            with pe.Fori(1, 4) as i:
                branch_units(1, i)
            with pe.Fori(0, 4) as i:
                branch_units(2, i)

            def wo_unit(i, j, first):
                pe.wait_ge(w_split, i * 2 + (U2 + V_WO + j + 1))
                if not first:
                    pe.wait_ge(mix_read, i * 2 + (j - 1))
                if first and j == 0:
                    pe.wait_ge(y_free, 25)
                    for k in range(KD):
                        pe.wait_ge(m_ready, k + 1)
                        mm = product(pe, j, (k,), KD, hh, hl, 0)
                else:
                    if first:
                        pe.wait_ge(y_free, 26)
                    mm = product(pe, j, range(KD), KD, hh, hl, 3 * j)
                mm.then_inc(unit_done, 1)

            wo_unit(0, 0, True)
            wo_unit(0, 1, True)
            with pe.Fori(1, 4) as i:
                wo_unit(i, 0, False)
                wo_unit(i, 1, False)

            def norm_sum(src, value, sem_in, sem_out):
                pe.wait_ge(sem_in, value)
                for g in range(G):
                    mm = pe.matmul(ps[:, g, 0:GW], ones[:, :], src[:, g * GW:(g + 1) * GW], start=True, stop=True)
                mm.then_inc(sem_out, 1)

            pe.wait_ge(mix_read, 8)
            norm_sum(ss4, KD, sq_used, n4_sum)
            pe.wait_ge(n4_rs, 1)
            for f in range(KD):
                pe.wait_ge(x_squared, KD + f + 1)
                mm = square_sum(mix[:, f, :], 0, f)
            mm.then_inc(n4_sum, 1)
            with pe.Fori(0, FCH) as c:
                for j in range(4):
                    pe.wait_ge(w_split, c * FFU + (U2 + V_FF + j + 1))
                    if j < 2:
                        pe.wait_ge(acc_added, c * 8 + (j + 1))
                    else:
                        pe.wait_ge(hid_relu, c * 4 + (j - 1))
                    for k in range(KD):
                        if j == 0:
                            pe.wait_ge(h2_ready[k % 2], k // 2 + 1)
                        mm = product(pe, j % 2, (k,), KD, hh, hl, 3 * (j % 2))
                    mm.then_inc(unit_done, 1)
                for j in range(8):
                    pe.wait_ge(w_split, c * FFU + (U2 + V_FF + FF1 + j + 1))
                    if j < 2:
                        pe.wait_ge(hid_relu, c * 4 + (j + 3))
                    else:
                        pe.wait_ge(acc_added, c * 8 + (j + 1))
                    for k in range(NH):
                        if j == 0:
                            pe.wait_ge(hid_ready, c * 4 + (k + 1))
                        mm = product(pe, j % 2, (k,), NH, fh, fl, 3 * (j % 2))
                    mm.then_inc(unit_done, 1)
            pe.wait_ge(acc_added, 8 * FCH + 2)
            norm_sum(ss5, KD, fin_ss, n4_sum)

        @block.scalar
        def _(act):
            IDN = ACT.Identity

            lnexp = lambda: act.preload_act_table_set("natural_log_exp_and_others")
            lnexp()
            for f in range(KD):
                act.wait_ge(x_in[f], 16)
                if f >= 2:
                    act.wait_ge(x_summed, f - 1)
                act.activation(sq1[:, f % 2, :], xT[:, f, :], ACT.Square).then_inc(x_squared, 1)
            act.wait_ge(x_summed, KD)
            act.wait_ge(ones_set, 2)
            psg = lambda b0: ps[:, b0:b0 + G, 0:GW]
            v3 = lambda ap: ap.rearrange("p (g t) -> p g t", g=G)
            act.activation(v3(rs1), psg(3), ACT.Ln, bias=eps[:, 0:1], scale=1.0 / D).then_inc(a_seq, 1)
            act.wait_ge(a_seq, 1)
            act.activation(rs1, rs1, ACT.Exp, scale=-0.5).then_inc(h_rstd, 1)
            for f in range(KD):
                act.wait_ge(h_full, f + 1)
                act.activation(hh[:, f, :], xT[:, f, :], ACT.Copy).then_inc(h_hi_set, 1)

            def stage(u, p, dst, scale=None):
                act.wait_ge(unit_done, p * PER + (u + 1))
                ins = (act.activation(v3(dst), psg(0), ACT.Copy) if scale is None else
                       act.activation(v3(dst), psg(0), ACT.Copy, scale=scale))
                ins.then_inc(staged.sem, 1)

            B_DST = ((kT[:, :], None), (vT[:, :], None), (qT[:, :], DH ** -0.5), (ua[:, :], None), (ug[:, :], None))
            A_DST = (fT[:, :], qA[:, :], iT[:, :], gA[:, :])
            def gate_conv():
                act.activation(ug[:, :], ug[:, :], ACT.Sigmoid).then_inc(ug_sig.sem, 1)
                lnexp()

            for u in range(PRE):
                stage(u, 0, *B_DST[u])
            act.wait_ge(staged.sem, PRE)
            gate_conv()

            def stage_unit(jj, p, more):
                g = gate_of(jj, more)
                if jj >= units(more):
                    return
                if g is not None:
                    if g >= 2:
                        gl_stored[g % 2].wait(act, p, 16 * (g // 2))
                    stage(PRE + jj, p, gl[:, g % 2, :])
                elif jj < A_UNITS:
                    stage(PRE + jj, p, A_DST[jj // 2])
                else:
                    stage(PRE + jj, p, *B_DST[jj - A_UNITS])

            zb = [A(o, 1024) for o in A_Z]
            lb = [A(o, 1024) for o in A_L]
            vtok = A(A_VT, 9 * P)
            ob = A(A_OB, T)
            CHAIN_A = 3

            def group(p, more):
                ch = Chain(act, a_seq, p * CHAIN_A + 1)
                v_turned.wait(act, p, 1)
                act.activation(vtok[:, 0:1024], banks(5, 1024), ACT.Copy)
                act.activation(vtok[0:SM, 1024:1152], ps[0:SM, 7, 0:P], ACT.Copy).then_inc(v_staged.sem, 1)
                now_set.wait(act, p, 2)
                for s in range(20):
                    i = s - 3
                    if s - 1 in A_STEPS[1::2]:
                        stage_unit(A_STEPS.index(s - 1) // 2, p, more)
                    if 0 <= i < 16:
                        t_done.wait(act, p, i + 1)
                        if i:
                            av_done.wait(act, p, i)
                        n = P * (i // 2 + 1)
                        act.activation(A(A_AT, n), banks(5, n), ACT.Copy).then_inc(at_ready.sem, 1)
                    if s >= 5 and s % 2 == 1:
                        qb = (s - 5) // 2
                        av_done.wait(act, p, 2 * qb + 2)
                        if qb == 0:
                            oa_stored.wait(act, p, 0)
                        act.activation(ob[:, qb * P:(qb + 1) * P], ps[:, 7, (qb % 4) * P:(qb % 4 + 1) * P],
                                       ACT.Copy).then_inc(o_read.sem, 1)
                    if s < 16:
                        z_ready.wait(act, p, s + 1)
                        if s >= 3:
                            t_done.wait(act, p, s - 2)
                        n = P * (s // 2 + 1)
                        act.activation(zb[s % 3][:, 0:n], banks(3, n), IDN, bias=sbp[:, s % 2:s % 2 + 1])\
                            .then_inc(z_read.sem, 1)
                    if 0 <= s - 1 < 16:
                        n = P * ((s - 1) // 2 + 1)
                        l = lb[(s - 1) % 2][:, 0:n]
                        e_ready.wait(act, p, s)
                        act.activation(l, l, ACT.Exp).then_inc(exp1.sem, 1)
                        exp1.wait(act, p, s)
                        act.activation(l, l, ACT.Ln, bias=1.0).then_inc(ln_ready.sem, 1)
                    if 0 <= s - 2 < 16:
                        n = P * ((s - 2) // 2 + 1)
                        z = zb[(s - 2) % 3][:, 0:n]
                        arg_ready.wait(act, p, s - 1)
                        act.activation(z, z, ACT.Exp).then_inc(a_ready.sem, 1)
                    if s == 4:
                        zs_ready.wait(act, p, 1)
                        act.activation(A(A_ZS, SBK, slice(0, 64)), ps[0:64, 4, 0:SBK], IDN, bias=sbp[0:64, 2:3])\
                            .then_inc(zs_read.sem, 1)
                    if s == 5:
                        l = A(A_LS, SBK, slice(0, 64))
                        es_ready.wait(act, p, 1)
                        ch.link(act.activation(l, l, ACT.Exp))
                        act.activation(l, l, ACT.Ln, bias=1.0).then_inc(lns_ready.sem, 1)
                    if s == 6:
                        args_ready.wait(act, p, 1)
                        z = A(A_ZS, SBK, slice(0, 64))
                        act.activation(z, z, ACT.Exp).then_inc(as_ready.sem, 1)
                    if s == 8:
                        ts_done.wait(act, p, 1)
                        act.activation(A(A_ATS, 128), ps[:, 6, 0:128], ACT.Copy)
                        act.activation(A(A_ATS + 128, 64, slice(0, SM)), ps[0:SM, 6, 128:192], ACT.Copy)\
                            .then_inc(ats_ready.sem, 1)
                    if s == 10:
                        os_done.wait(act, p, 1)
                        for e in range(2):
                            r = slice(DH * e, DH * e + DH)
                            ins = act.activation(ar[r, A_OB + TP:A_OB + T].rearrange("p (b q) -> p b q", b=NSEQ),
                                                 ps[r, 6, 256:320].rearrange("p (b e q) -> p b e q", b=NSEQ, e=2)
                                                 [:, :, e, :], ACT.Copy)
                        ins.then_inc(os_read.sem, 1)

                av_done.wait(act, p, 16)
                t_done.wait(act, p, 16)
                staged.wait(act, p, A_UNITS)
                t1 = A(B_T1, T)
                ch.link(act.activation(t1, fT[:, :], ACT.Abs))
                ch.link(act.activation(t1, t1, ACT.Exp, scale=-1.0))
                act.activation(t1, t1, ACT.Ln, bias=1.0).then_inc(t1_ready.sem, 1)
                arg_ready.wait(act, p, 16)
                act.activation(A(B_W[0], T), qA[:, :], ACT.Sigmoid)
                act.activation(A(B_W[1], T), gA[:, :], ACT.Sigmoid)
                act.activation(A(B_KK, T), fT[:, :], ACT.Sigmoid, scale=-1.0).then_inc(sig_ready.sem, 1)
                lnexp()
                ia_turned.wait(act, p, 1)
                os_read.wait(act, p, 1)
                act.activation(A(B_VA, 1024), banks(5, 1024), ACT.Copy)
                act.activation(A(B_VA + 1024, P, slice(0, SM)), ps[0:SM, 7, 0:P], ACT.Copy).then_inc(va_staged.sem, 1)
                b_ready.wait(act, p, 1)
                act.activation(A(B_QB, T), A(B_B, T), ACT.Exp).then_inc(eb_ready.sem, 1)
                qk_ready.wait(act, p, 1)
                if more:
                    kv_stored.wait(act, p, 32)
                    u_ready.wait(act, p, 1)
                for j in range(NL):
                    dsub.wait(act, p, j + 1)
                    if j >= 2:
                        lev_done.wait(act, p, j)
                    n = T if LEVELS[j] <= TS else TP
                    act.activation(A(B_W[j % 2], n), A(B_D, n), ACT.Exp).then_inc(wexp.sem, 1)
                    if j in (0, 2, 4):
                        stage_unit(A_UNITS + j // 2, p, more)
                dk_ready.wait(act, p, 1)
                act.activation(A(B_KD, T), A(B_D, T), ACT.Exp).then_inc(dk_exp.sem, 1)
                stage_unit(A_UNITS + 3, p, more)
                kd_turned.wait(act, p, 1)
                act.activation(A(B_KDT, 1024), banks(3, 1024), ACT.Copy)
                act.activation(A(B_KDT + 1024, P, slice(0, SM)), ps[0:SM, 7, 0:P], ACT.Copy)\
                    .then_inc(kdt_staged.sem, 1)
                stage_unit(A_UNITS + 4, p, more)
                if more:
                    staged.wait(act, p, A_UNITS + 5)
                    gate_conv()
                o_done.wait(act, p, 1)
                ob_stored.wait(act, p, 16)
                conv_stored.wait(act, p, 48)
                act.activation(A(B_O, T), banks(5, T), ACT.Copy)
                act.activation(A(B_OSQ, T), banks(5, T), ACT.Square).then_inc(osq_ready.sem, 1)
                n_done.wait(act, p, 1)
                ins = act.activation(A(B_RS, T), banks(3, T), ACT.Ln, bias=eps[:, 0:1], scale=1.0 / P)
                ins.then_inc(n_read.sem, 1)
                n_read.wait(act, p, 1)
                act.activation(A(B_RS, T), A(B_RS, T), ACT.Exp, scale=-0.5).then_inc(rs_ready.sem, 1)
                stage_unit(A_UNITS + 5, p, more)
                if more:
                    oa_ready.wait(act, p, 1)
                    h_stored.wait(act, p, 32)
                    for b in range(2):
                        gl_stored[b].wait(act, p, 16 * ((GPG - b + 1) // 2))
                assert ch.n == CHAIN_A, ch.n

            with act.Fori(0, NH - 1) as p:
                group(p, True)
            group(NH - 1, False)

            def ln_step(v):
                if v == 4:
                    for g in range(G):
                        act.wait_ge(ln_pe, g + 1)
                        act.activation(ln_stat[:, g * GW:(g + 1) * GW], ps[:, 6 + g % 2, 0:GW], ACT.Copy,
                                       scale=1.0 / 512).then_inc(ln_seq_a, 1)
                if v in (6, 7):
                    act.wait_ge(ln_seq_v, 5 if v == 6 else 7)
                    for k in ((0, 1) if v == 6 else (2, 3)):
                        act.activation(csq[:, k, :], cf[:, k, :], ACT.Square).then_inc(ln_seq_a, 1)
                if v == 10:
                    lnexp()
                    for g in range(G):
                        act.wait_ge(ln_pe, G + g + 1)
                        act.activation(ln_stat[:, g * GW:(g + 1) * GW], ps[:, 6 + (G + g) % 2, 0:GW], ACT.Ln,
                                       bias=eps[:, 0:1], scale=1.0 / 512).then_inc(ln_seq_a, 1)
                    act.wait_ge(ln_seq_a, 10)
                    act.activation(ln_stat, ln_stat, ACT.Exp, scale=-0.5).then_inc(ln_seq_a, 1)
                if v == 12:
                    act.wait_ge(ln_seq_v, LN_SCALED)
                    for k in range(NH):
                        act.activation(cf[:, k, :], cf[:, k, :], IDN, bias=par("ln_b", k), scale=par("ln_g", k))\
                            .then_inc(ln_seq_a, 1)
                if v == 13:
                    for k in range(NH):
                        act.wait_ge(ln_seq_a, 12 + k)
                        act.activation(csq[:, k, :], cf[:, k, :], ACT.Sigmoid).then_inc(ln_seq_a, 1)

            for x, src in enumerate((bf, of, cf)):
                act.wait_ge(of_in[x], 16)
                if x:
                    act.wait_ge(unit_done, U2 + 8 * x)
                if x == 2:
                    act.wait_ge(ln_seq_v, LN_DONE)
                for k in range(NH):
                    act.activation(oh[:, k, :], src[:, k, :], ACT.Copy).then_inc(o_hi_set, 1)
                if x < 2:
                    for v in range(8 * x, 8 * x + 8):
                        act.wait_ge(gate_in[v % 2], 16 * (v // 2 + 1))
                        act.activation(gs[:, v % 2, :], gs[:, v % 2, :], ACT.Sigmoid).then_inc(gate_ready, 1)
                        ln_step(v)
                else:
                    with act.Fori(0, 4) as i:
                        for j in range(2):
                            act.wait_ge(gate_in[j], i * 16 + (64 * x + 16))
                            act.activation(gs[:, j, :], gs[:, j, :], ACT.Sigmoid).then_inc(gate_ready, 1)
            lnexp()
            act.wait_ge(unit_done, U2 + V_WO)
            for k in range(KD):
                act.wait_ge(m_seq, 8 + k + 1)
                act.activation(hh[:, k, :], mm_[:, k, :], ACT.Copy).then_inc(m_hi_set, 1)
            act.wait_ge(m_ready, KD)
            for cb in range(KD):
                act.wait_ge(unit_done, U2 + V_WO + cb + 1)
                act.activation(v3(mix[:, cb, :]), psg(3 * (cb % 2)), ACT.Copy)
                if cb:
                    act.wait_ge(sq_used, cb)
                act.activation(v3(sq4[:, :]), psg(3 * (cb % 2)), ACT.Square).then_inc(mix_read, 1)

            def rstd(dst, k):
                act.wait_ge(n4_sum, k)
                ins = act.activation(v3(dst), psg(0), ACT.Ln, bias=eps[:, 0:1], scale=1.0 / D)
                ins.then_inc(mix_sq, 1)
                act.wait_ge(mix_sq, k)
                act.activation(dst, dst, ACT.Exp, scale=-0.5).then_inc(n4_rs, 1)

            rstd(sq4[:, :], 1)
            for f in range(KD):
                act.wait_ge(x1_ready[f % 2], f // 2 + 1)
                act.activation(mix[:, f, :], x4[:, f, :], ACT.Square).then_inc(x_squared, 1)
                act.dma_start(dr["x1_d"][f * P:(f + 1) * P, :], x4[:, f, :]).then_inc(x1_stored, 16)
            rstd(sq4[:, :], 2)
            for f in range(KD):
                act.wait_ge(h2_full, f + 1)
                act.activation(hh[:, f, :], mix[:, f, :], ACT.Copy).then_inc(h2_hi, 1)
            for b in range(2):
                act.wait_ge(h2_ready[b], KD // 2)
            act.wait_ge(x1_stored, 16 * KD)

            def ff_chunk(c):
                for j in range(4):
                    act.wait_ge(unit_done, c * FFU + (U2 + V_FF + j + 1))
                    if j >= 2:
                        act.wait_ge(hid_ready, c * 4 + (j - 1))
                    act.activation(v3(hid[:, j % 2, :]), psg(3 * (j % 2)), ACT.Relu).then_inc(hid_relu, 1)
                    act.wait_ge(hid_sq, c * 4 + (j + 1))
                    act.activation(fh[:, j, :], hid[:, j % 2, :], ACT.Copy).then_inc(hid_hi, 1)

            with act.Fori(0, FCH - 1) as c:
                ff_chunk(c)
            ff_chunk(FCH - 1)
            act.wait_ge(unit_done, U2 + V_FF + FFU * (FCH - 1) + FF1)
            act.dma_start(hl[:, :, :].bitcast(F32), dr["x1_d"].rearrange("(k p) t -> p k t", p=P)).then_inc(x5_in, 16)
            for f in range(KD):
                act.wait_ge(acc_added, 8 * (FCH - 1) + 2 + f + 1)
                if f:
                    act.wait_ge(fin_ss, f)
                act.activation(sq5[:, :], acc[:, f, :], ACT.Square).then_inc(fin_sq, 1)
            rstd(sq5[:, :], 3)

        @block.vector
        def _(dve):
            v3 = lambda ap: ap.rearrange("p (g t) -> p g t", g=G)
            psg = lambda b0: ps[:, b0:b0 + G, 0:GW]
            dve.memset(ones[:, :], 1.0).then_inc(ones_set, 1)
            dve.memset(eps[:, :], EPS).then_inc(ones_set, 1)
            dve.memset(cwp[:, 0:1], 0.0).then_inc(oa_stored.sem, 1)
            dve.wait_ge(const_in, 32)
            dve.tensor_copy(levm[:, :, :].rearrange("p l t -> p (l t)"), mask_f[:, 0:NL * P])
            dve.tensor_copy(keep[:, :], mask_f[:, NL * P:])
            dve.wait_ge(h_rstd, 1)
            for f in range(KD):
                dve.scalar_tensor_tensor(xT[:, f, :], xT[:, f, :], par("g_pre_mix", f), rs1, ALU.mult, ALU.mult)\
                    .then_inc(h_full, 1)
                if f:
                    dve.wait_ge(h_hi_set, f)
                    dve.tensor_tensor(hl[:, f - 1, :], xT[:, f - 1, :], hh[:, f - 1, :].bitcast(F32), ALU.subtract)\
                        .then_inc(h_ready, 1)
            dve.wait_ge(h_hi_set, KD)
            dve.tensor_tensor(hl[:, KD - 1, :], xT[:, KD - 1, :], hh[:, KD - 1, :].bitcast(F32), ALU.subtract)\
                .then_inc(h_ready, 1)

            zb = [A(o, 1024) for o in A_Z]
            lb = [A(o, 1024) for o in A_L]

            def group(p, more):
                ch = Chain(dve, v_seq, p * CHAIN_V)
                dve.tensor_copy(cwp[:, 0:CW], pk[:, bass.ds(p * CW + PK["conv_w"][0], CW)])
                dve.tensor_copy(cwp[:, CW:CW + 1], pk[:, bass.ds(p + PK["conv_b"][0], 1)]).then_inc(now_set.sem, 1)
                dve.tensor_copy(sbp[:, 0:2], pk[:, bass.ds(p * 2 + PK["sb_bias"][0], 2)])
                dve.tensor_copy(sbp[:, 2:3], pk[:, bass.ds(p + PK["sample_bias"][0], 1)]).then_inc(now_set.sem, 1)
                dve.memset(A(A_QPAD, 576), 0.0)
                ch.link(dve.memset(A(A_QFULL, 64), 0.0))
                staged.wait(dve, p, -2)
                for e in range(2):
                    r = slice(DH * e, DH * e + DH)
                    src = qT[r, TP:T].rearrange("p (b q) -> p b q", b=NSEQ)
                    dve.tensor_copy(ar[r, A_QPAD:A_QPAD + 576].rearrange("p (b c) -> p b c", c=72)
                                    [:, :, TS * e:TS * e + TS], src)
                    ins = dve.tensor_copy(ar[r, A_QFULL:A_QFULL + 64].rearrange("p (b c) -> p b c", c=8)
                                          [:, :, TS * e:TS * e + TS], src)
                ins.then_inc(q_pad.sem, 1)
                dve.memset(A(A_U, PAD), 0.0)
                ug_sig.wait(dve, p, 1)
                up, us = A(A_U, PAD + TP), A(A_US, NSEQ * (PAD + TS)).rearrange("p (b t) -> p b t", b=NSEQ)
                dve.tensor_tensor(up[:, PAD:], ua[:, 0:TP], ug[:, 0:TP], ALU.mult)
                prev_in.wait(dve, p, 16)
                dve.tensor_tensor(us[:, :, PAD:], ua[:, TP:T].rearrange("p (b t) -> p b t", b=NSEQ),
                                  ug[:, TP:T].rearrange("p (b t) -> p b t", b=NSEQ), ALU.mult).then_inc(u_ready.sem, 1)
                u_ready.wait(dve, p, 1)
                now_set.wait(dve, p, 2)
                ca = A(A_ACC, TP)
                cs = A(A_ACC + TP, SM).rearrange("p (b t) -> p b t", b=NSEQ)
                taps = [0]

                def tap(last=False):
                    w = taps[0]
                    if w >= CW:
                        return
                    taps[0] += 1
                    if w:
                        ch.wait()
                        ch.mark(dve.scalar_tensor_tensor(ca, up[:, w:w + TP], cwp[:, w:w + 1], ca, ALU.mult, ALU.add))
                    else:
                        ch.mark(dve.tensor_scalar(ca, up[:, 0:TP], cwp[:, 0:1], cwp[:, CW:CW + 1], ALU.mult, ALU.add))
                    if w == CW - 1:
                        taps_s.wait(dve, p, 1)
                        ch.link(dve.tensor_reduce(cs, tw[:, :, :, :].rearrange("p t b w -> p b t w"),
                                                  axis=mybir.AxisListType.X, op=ALU.add))
                        dve.tensor_scalar(cs, cs, cwp[:, CW:CW + 1], None, ALU.add).then_inc(conv_done.sem, 1)

                for s in range(17):
                    if s < 16:
                        qb = s // 2
                        n = P * (qb + 1)
                        z, l = zb[s % 3][:, 0:n], lb[s % 2][:, 0:n]
                        z_read.wait(dve, p, s + 1)
                        dg = z[:, qb * P:n]
                        ch.mark(dve.tensor_tensor(dg, dg, neg, ALU.add))
                        tap()
                        ch.wait()
                        dve.tensor_scalar(l, z, ZMAX, None, ALU.min).then_inc(e_ready.sem, 1)
                    if s == 4:
                        zs, ls = A(A_ZS, SBK, slice(0, 64)), A(A_LS, SBK, slice(0, 64))
                        zs_read.wait(dve, p, 1)
                        ch.link(dve.tensor_tensor(zs[:, PAST:], zs[:, PAST:], par("neg_new", 0, SM)[0:64, :], ALU.add))
                        dve.tensor_scalar(ls, zs, ZMAX, None, ALU.min).then_inc(es_ready.sem, 1)
                    tap()
                    if s:
                        n = P * ((s - 1) // 2 + 1)
                        z, l = zb[(s - 1) % 3][:, 0:n], lb[(s - 1) % 2][:, 0:n]
                        ln_ready.wait(dve, p, s)
                        ch.link(dve.tensor_tensor(l, z, l, ALU.max))
                        r = l[:, ::-1]
                        ch.link(dve.tensor_tensor_scan(r, r, r, 0.0, ALU.add, ALU.max))
                        dve.tensor_tensor(z, z, l, ALU.subtract).then_inc(arg_ready.sem, 1)
                    if s == 5:
                        lns_ready.wait(dve, p, 1)
                        ch.link(dve.tensor_tensor(ls, zs, ls, ALU.max))
                        r = ls[:, ::-1]
                        ch.link(dve.tensor_tensor_scan(r, r, r, 0.0, ALU.add, ALU.max))
                        dve.tensor_tensor(zs, zs, ls, ALU.subtract).then_inc(args_ready.sem, 1)
                while taps[0] < CW:
                    tap()

                a_ready.wait(dve, p, 16)
                t_done.wait(dve, p, 16)
                av_done.wait(dve, p, 16)
                os_done.wait(dve, p, 1)
                Bt, Dt, w0, w1 = A(B_B, T), A(B_D, T), A(B_W[0], T), A(B_W[1], T)
                kk, att, qbt = A(B_KK, T), A(B_ATT, T), A(B_QB, T)
                t1_ready.wait(dve, p, 1)
                ch.link(dve.scalar_tensor_tensor(Dt, fT[:, :], 0.0, A(B_T1, T), ALU.min, ALU.subtract))
                dve.tensor_tensor_scan(Bt, keep[:, :], Dt, 0.0, ALU.mult, ALU.add).then_inc(b_ready.sem, 1)
                sig_ready.wait(dve, p, 1)
                dve.tensor_tensor(gA[:, :], gA[:, :], w1, ALU.mult)
                dve.tensor_tensor(qA[:, :], qA[:, :], w0, ALU.mult).then_inc(qk_ready.sem, 1)
                b_ready.wait(dve, p, 1)

                def blocks(ap, size):
                    n = T if size <= TS else TP
                    return ap[:, 0:n].rearrange("p (n c) -> p n c", c=size)

                def diff(j):
                    size = LEVELS[j]
                    half = size // 2
                    bb, dd = blocks(Bt, size), blocks(Dt, size)
                    nb = bb.shape[1]
                    mid = bb[:, :, half - 1:half].broadcast_to([P, nb, half])
                    dve.tensor_tensor(dd[:, :, half:], bb[:, :, half:], mid, ALU.subtract)
                    dve.tensor_tensor(dd[:, :, 0:half], mid, bb[:, :, 0:half], ALU.subtract).then_inc(dsub.sem, 1)

                def merge(idx):
                    if idx:
                        wait_apart(dve, lev_done.at(p, idx + 1), att_read.at(p, idx))
                    else:
                        lev_done.wait(dve, p, idx + 1)
                    j = idx - 1
                    b0 = 3 if idx == 0 or j % 2 else 5
                    src = banks(b0, 1024).rearrange("p (c t) -> p c t", c=CH)
                    dst = att[:, 0:TP].rearrange("p (c t) -> p c t", c=CH)
                    if idx == 0:
                        ch.mark(dve.tensor_tensor(dst, src, ident.unsqueeze(1).broadcast_to([P, CH, P]), ALU.mult))
                        ins = dve.tensor_tensor(att[0:SM, TP:T], ps[0:SM, 7, 0:SM], ident[0:SM, 0:SM], ALU.mult)
                    else:
                        ins = dve.copy_predicated(dst, levm[:, j:j + 1, :].broadcast_to([P, CH, P]), src)
                        if LEVELS[j] <= TS:
                            ch.mark(ins)
                            ins = dve.copy_predicated(att[0:SM, TP:T], levm[0:SM, j, 0:SM], ps[0:SM, 7, 0:SM])
                    ins.then_inc(att_read.sem, 1)

                diff(0)
                va_staged.wait(dve, p, 1)
                dve.tensor_tensor(A(B_T1, NSEQ * P, slice(0, SM)).rearrange("p (b v) -> p b v", b=NSEQ),
                                  A(B_VA + 1024, P, slice(0, SM)).unsqueeze(1).broadcast_to([SM, NSEQ, P]),
                                  par("own_seq", 0, NSEQ)[0:SM, :].unsqueeze(2).broadcast_to([SM, NSEQ, P]),
                                  ALU.mult).then_inc(vm_ready.sem, 1)
                eb_ready.wait(dve, p, 1)
                dve.tensor_copy(ebl[:, 0:CH], qbt[:, 0:TP].rearrange("p (c t) -> p c t", t=P)[:, :, P - 1])
                ch.link(dve.tensor_copy(ebl[:, CH:], qbt[:, TP:T].rearrange("p (c t) -> p c t", t=TS)[:, :, TS - 1]))
                qk_ready.wait(dve, p, 1)
                dve.tensor_tensor(qbt, qbt, qA[:, :], ALU.mult).then_inc(qb_ready.sem, 1)
                merge(0)
                for j in range(NL):
                    size = LEVELS[j]
                    half = size // 2
                    wexp.wait(dve, p, j + 1)
                    if j + 1 < NL:
                        diff(j + 1)
                    else:
                        for (a, n, c) in ((0, TP, P), (TP, SM, TS)):
                            bb = Bt[:, a:a + n].rearrange("p (n c) -> p n c", c=c)
                            ins = dve.tensor_tensor(Dt[:, a:a + n].rearrange("p (n c) -> p n c", c=c),
                                                    bb[:, :, c - 1:c].broadcast_to([P, n // c, c]), bb, ALU.subtract)
                        ins.then_inc(dk_ready.sem, 1)
                    ww, qq, k_ = blocks(A(B_W[j % 2], T), size), blocks(qA, size), blocks(kk, size)
                    dve.tensor_tensor(ww[:, :, half:], ww[:, :, half:], qq[:, :, half:], ALU.mult)
                    dve.tensor_tensor(ww[:, :, 0:half], ww[:, :, 0:half], k_[:, :, 0:half], ALU.mult)\
                        .then_inc(w_ready.sem, 1)
                    if j:
                        merge(j)
                merge(NL)
                dk_exp.wait(dve, p, 1)
                dve.tensor_tensor(A(B_KD, T), A(B_KD, T), kk, ALU.mult).then_inc(kd_ready.sem, 1)
                u_done.wait(dve, p, 1)
                ch.link(dve.tensor_copy(A(B_D, P), banks(5, 1024)[:, 0:P]))
                for c in range(1, CH):
                    ins = dve.scalar_tensor_tensor(A(B_D + c * P, P), A(B_D + (c - 1) * P, P), ebl[:, c:c + 1],
                                                   banks(5, 1024)[:, c * P:(c + 1) * P], ALU.mult, ALU.add)
                    if c < CH - 1:
                        ch.link(ins)
                    else:
                        ins.then_inc(s_ready.sem, 1)
                s0_in.wait(dve, p, 16)
                sn = A(B_W[0], NSEQ * P).rearrange("p (b v) -> p b v", b=NSEQ)
                ch.link(dve.tensor_tensor(sn, A(B_S0, NSEQ * P).rearrange("p (b v) -> p b v", b=NSEQ),
                                          ebl[:, CH:].unsqueeze(2).broadcast_to([P, NSEQ, P]), ALU.mult))
                um_done.wait(dve, p, 1)
                dve.tensor_tensor(A(B_W[0], 1024), A(B_W[0], 1024), banks(3, 1024), ALU.add).then_inc(s0_new.sem, 1)
                rs_ready.wait(dve, p, 1)
                ch.link(dve.scalar_tensor_tensor(A(B_O, T), A(B_O, T), par("a_norm"), A(B_RS, T), ALU.mult, ALU.mult))
                dve.tensor_tensor(A(B_O, T), A(B_O, T), gA[:, :], ALU.mult).then_inc(oa_ready.sem, 1)
                if more:
                    h_stored.wait(dve, p, 32)
                assert ch.n == CHAIN_V, ch.n

            with dve.Fori(0, NH - 1) as p:
                group(p, True)
            group(NH - 1, False)

            def add_up(src, k):
                if k == 1:
                    dve.tensor_tensor(ln_sum, src[:, 0, :], src[:, 1, :], ALU.add).then_inc(ln_seq_v, 1)
                else:
                    dve.tensor_tensor(ln_sum, ln_sum, src[:, k, :], ALU.add).then_inc(ln_seq_v, 1)

            def ln_step(v):
                if v in (5, 6):
                    dve.wait_ge(ln_seq_a, 3)
                    for k in ((0, 1) if v == 5 else (2, 3)):
                        dve.tensor_tensor(cf[:, k, :], cf[:, k, :], ln_stat, ALU.subtract).then_inc(ln_seq_v, 1)
                if v == 7:
                    dve.wait_ge(ln_seq_a, 5)
                    add_up(csq, 1)
                if v == 8:
                    dve.wait_ge(ln_seq_a, 7)
                    for k in (2, 3):
                        dve.wait_ge(ln_seq_v, LN_CENTER + k - 1)
                        add_up(csq, k)
                if v == 11:
                    dve.wait_ge(ln_seq_a, 11)
                    for k in range(NH):
                        dve.tensor_tensor(cf[:, k, :], cf[:, k, :], ln_stat, ALU.mult).then_inc(ln_seq_v, 1)
                if v in (13, 14):
                    dve.wait_ge(ln_seq_a, 17 if v == 13 else 19)
                    for k in ((0, 1) if v == 13 else (2, 3)):
                        dve.tensor_tensor(cf[:, k, :], cf[:, k, :], csq[:, k, :], ALU.mult).then_inc(ln_seq_v, 1)

            def gated(v, j, mt, first, m):
                dve.wait_ge(unit_done, v + (U2 + 1))
                dve.wait_ge(gate_ready, v + 1)
                if first:
                    dve.tensor_tensor(v3(mt), psg(3 * j), v3(gs[:, j, :]), ALU.mult).then_inc(y_free, 1)
                else:
                    dve.tensor_tensor(v3(tm[:, :]), psg(3 * j), v3(gs[:, j, :]), ALU.mult).then_inc(y_free, 1)
                    dve.wait_ge(y_free, v + 3)
                    dve.tensor_tensor(mt, mt, tm[:, :], ALU.add).then_inc(m_seq, 1)
                    dve.wait_ge(m_seq, m + 1)

            for x, src in enumerate((bf, of, cf)):
                for k in range(NH):
                    dve.wait_ge(o_hi_set, 4 * x + k + 1)
                    dve.tensor_tensor(ol[:, k, :], src[:, k, :], oh[:, k, :].bitcast(F32), ALU.subtract)\
                        .then_inc(o_ready, 1)
                if x == 0:
                    oa_stored.wait(dve, NH - 1, 16)
                    dve.memset(tm[:, 0:2], 0.0).then_inc(y_free, 2)
                    dve.wait_ge(of_in[2], 16)
                    for k in (1, 2, 3):
                        if k > 1:
                            dve.wait_ge(ln_seq_v, k - 1)
                        add_up(cf, k)
                if x < 2:
                    for v in range(8 * x, 8 * x + 8):
                        gated(v, v % 2, mm_[:, v % 8, :], x == 0, v - 8)
                        ln_step(v)
                else:
                    with dve.Fori(0, 4) as i:
                        for j in range(2):
                            mt = mm_[:, bass.ds(i * 2 + j, 1), :].rearrange("p a t -> p (a t)")
                            gated(i * 2 + (8 * x + j), j, mt, False, i * 2 + (8 * (x - 1) + j))
            for k in range(KD):
                dve.wait_ge(m_hi_set, k + 1)
                dve.tensor_tensor(hl[:, k, :], mm_[:, k, :], hh[:, k, :].bitcast(F32), ALU.subtract).then_inc(m_ready, 1)
            for f in range(KD):
                dve.wait_ge(mix_read, f + 1)
                if f == 0:
                    dve.tensor_copy(ss4[:, :], sq4[:, :]).then_inc(sq_used, 1)
                else:
                    dve.wait_ge(sq_used, f)
                    dve.tensor_tensor(ss4[:, :], ss4[:, :], sq4[:, :], ALU.add).then_inc(sq_used, 1)
            dve.wait_ge(n4_rs, 1)
            dve.wait_ge(x4_in, 16)
            for f in range(KD):
                dve.scalar_tensor_tensor(mix[:, f, :], mix[:, f, :], par("g_post_mix", f), sq4[:, :],
                                         ALU.mult, ALU.mult).then_inc(x1_seq, 1)
                if f % 2 == 0:
                    dve.wait_ge(x1_seq, f + 1)
                    dve.tensor_tensor(x4[:, f, :], x4[:, f, :], mix[:, f, :], ALU.add).then_inc(x1_ready[0], 1)
            dve.wait_ge(n4_rs, 2)
            dve.memset(ss4[:, 0:2], 0.0).then_inc(acc_added, 2)
            dve.wait_ge(x1_ready[1], KD // 2)
            for f in range(KD):
                dve.scalar_tensor_tensor(mix[:, f, :], x4[:, f, :], par("g_pre_ffn", f), sq4[:, :],
                                         ALU.mult, ALU.mult).then_inc(h2_full, 1)
                if f % 2:
                    dve.wait_ge(h2_hi, f)
                    dve.tensor_tensor(hl[:, f - 1, :], mix[:, f - 1, :], hh[:, f - 1, :].bitcast(F32), ALU.subtract)\
                        .then_inc(h2_ready[0], 1)
            for b in range(2):
                dve.wait_ge(h2_ready[b], KD // 2)
            dve.wait_ge(x1_stored, 16 * KD)

            def ff_chunk(c, first=False, last=False):
                for j in range(4):
                    h = hid[:, j % 2, :]
                    dve.wait_ge(hid_relu, c * 4 + (j + 1))
                    dve.tensor_tensor(h, h, h, ALU.mult).then_inc(hid_sq, 1)
                    dve.wait_ge(hid_hi, c * 4 + (j + 1))
                    dve.tensor_tensor(fl[:, j, :], h, fh[:, j, :].bitcast(F32), ALU.subtract).then_inc(hid_ready, 1)
                for j in range(8):
                    dve.wait_ge(unit_done, c * FFU + (U2 + V_FF + FF1 + j + 1))
                    if first:
                        dve.tensor_copy(v3(acc[:, j, :]), psg(3 * (j % 2))).then_inc(acc_added, 1)
                    else:
                        dve.wait_ge(acc_added, c * 8 + (j - 8 + 3))
                        dve.tensor_tensor(v3(acc[:, j, :]), v3(acc[:, j, :]), psg(3 * (j % 2)), ALU.add)\
                            .then_inc(acc_added, 1)
                    if last and j:
                        ff_square(j - 1)

            def ff_square(f):
                dve.wait_ge(fin_sq, f + 1)
                if f == 0:
                    dve.tensor_copy(ss5[:, :], sq5[:, :]).then_inc(fin_ss, 1)
                else:
                    dve.wait_ge(fin_ss, f)
                    dve.tensor_tensor(ss5[:, :], ss5[:, :], sq5[:, :], ALU.add).then_inc(fin_ss, 1)

            ff_chunk(0, first=True)
            with dve.Fori(1, FCH - 1) as c:
                ff_chunk(c)
            ff_chunk(FCH - 1, last=True)
            ff_square(KD - 1)
            dve.wait_ge(n4_rs, 3)
            dve.wait_ge(x5_in, 16)
            for f in range(KD):
                dve.scalar_tensor_tensor(acc[:, f, :], acc[:, f, :], par("g_post_ffn", f), sq5[:, :],
                                         ALU.mult, ALU.mult).then_inc(y_seq, 1)
                if f % 2 == 0:
                    dve.wait_ge(y_seq, f + 1)
                    dve.tensor_tensor(acc[:, f, :], acc[:, f, :], hl[:, f, :].bitcast(F32), ALU.add)\
                        .then_inc(y_ready[0], 1)


BRANCH = (1, 0, 2)
LN_V = (3, 10)
LN_CENTER, LN_SCALED, LN_DONE = 7, 14, 18
CHAIN_V = 98


LN_A = ((0, 0, 1), (2, 3, 8))

_PARAMS = ("g_pre_mix", "g_post_mix", "g_pre_ffn", "g_post_ffn")


def kernel(**inputs):
    import numpy as np
    import concourse.bacc as _bacc
    from concourse import mybir as _mybir
    from concourse.bass_utils import run_bass_kernel_spmd as _run

    x = {k: np.asarray(v) for k, v in inputs.items()}
    f32 = np.float32

    def cols(v):
        return v.reshape(-1, P).T

    i = np.arange(P)
    ident = np.eye(P, dtype=f32)
    neg = np.where(i[None, :] < i[:, None], 0.0, NEG_BIG).astype(f32)
    levels = [((i[:, None] // s == i[None, :] // s) & (i[:, None] % s < s // 2) & (i[None, :] % s >= s // 2))
              for s in LEVELS]
    keep = np.ones(T, f32)
    keep[0:TP:P] = 0
    keep[TP::TS] = 0
    masks = np.concatenate([np.stack(levels, 1).reshape(P, -1).astype(f32), np.broadcast_to(keep, (P, T))], 1)
    r = np.arange(P)
    key = np.arange(SM)
    neg_new = np.where((r[:, None] // 8 == key[None, :] // TS) & (key[None, :] % TS < r[:, None] % TS), 0.0,
                       NEG_BIG).astype(f32)
    own = (r[:, None] // TS == np.arange(NSEQ)[None, :]).astype(f32)
    bias = x["sb_bias"][0]
    sample_bias = bias.reshape(NH, 2)[:, (r // TS) % 2].T
    conv_w = x["conv_w"][0].T.reshape(NH, P, CW).transpose(1, 0, 2).reshape(P, -1)
    params = np.concatenate(
        [cols(x[n][0]) for n in _PARAMS] + [cols(x["a_norm"][0]), conv_w, cols(x["conv_b"][0]), cols(x["ln_g"][0]),
         cols(x["ln_b"][0]), np.broadcast_to(bias, (P, 2 * NH)), sample_bias, ident, neg, neg_new, own], 1)
    ins = {
        "params": params,
        "masks": masks,
        "pages": x["page_table"].reshape(1, -1),
        "xT": np.concatenate([x["x_prompt"][0], x["x_sample"].reshape(SM, D)], 0).T,
        "kcT": x["cache_k"][0].reshape(-1, P, 8 * DH).transpose(0, 2, 1),
        "vc": x["cache_v"][0].reshape(-1, P, 8 * DH),
        "s_in": x["state_hgrn"][0],
        "conv_prev": x["state_conv"][0].transpose(2, 0, 1),
        "w_in": x["w_in"][0], "w_pa": x["w_pa"][0], "w_pb": x["w_pb"][0], "w_pc": x["w_pc"][0],
        "w_o": x["w_o"][0], "w_ff1": x["w_ff1"][0], "w_ff2": x["w_ff2"][0],
    }
    outs = {
        "yT": (D, T), "k_out": (8 * DH, T), "v_out": (8 * DH, T), "hgrn_p": (NH, P, P), "hgrn_s": (NSEQ, NH, P, P),
        "conv_p": (NH * P, PAD), "conv_s": (NH * P, NSEQ, PAD),
    }
    nc = _bacc.Bacc("TRN2", target_bir_lowering=False, num_devices=1)
    dr, arrays = {}, {}
    for n, a in ins.items():
        a = np.ascontiguousarray(a)
        arrays[f"in_{n}"] = a
        dr[n] = nc.dram_tensor(f"in_{n}", a.shape, _mybir.dt.from_np(a.dtype), kind="ExternalInput").ap()
    for n, shape in outs.items():
        dr[n] = nc.dram_tensor(f"out_{n}", shape, _mybir.dt.float32, kind="ExternalOutput").ap()
    for n, rows in (("oa_d", NH * P), ("ob_d", NH * P), ("c_d", NH * P), ("x1_d", D), ("g_d", NGATE * P)):
        dr[n] = nc.dram_tensor(n, (rows, T), _mybir.dt.float32, kind="Internal").ap()
    build(nc, dr)
    res = _run(nc, [arrays], core_ids=[0]).results[0]
    res = {n: res[f"out_{n}"] for n in outs}
    y = res["yT"].T
    k, v = res["k_out"].T, res["v_out"].T
    heads = (1, 1, TP, 8, DH)
    heads_s = (1, NSEQ, TS, 8, DH)
    return (
        np.ascontiguousarray(y[:TP].reshape(1, TP, D)), np.ascontiguousarray(y[TP:].reshape(NSEQ, TS, D)),
        np.ascontiguousarray(k[:TP]).reshape(heads), np.ascontiguousarray(v[:TP]).reshape(heads),
        res["hgrn_p"].reshape(1, 1, NH, P, P), np.ascontiguousarray(res["conv_p"].T).reshape(1, 1, PAD, NH * P),
        np.ascontiguousarray(k[TP:]).reshape(heads_s), np.ascontiguousarray(v[TP:]).reshape(heads_s),
        res["hgrn_s"].reshape(1, NSEQ, NH, P, P),
        np.ascontiguousarray(res["conv_s"].transpose(1, 2, 0)).reshape(1, NSEQ, PAD, NH * P),
    )
```
